# Optimizing a Trainium2 kernel written in Bass

```python
import math
import jax, jax.numpy as jnp
from jax import lax
import numpy as np

D_MODEL = 1024
BATCH = 1
SEQ = 256
DEPTH = 1

CHUNK = 64
CONV_W = D_MODEL // 2
CONV_K = 3
N_HEADS = 8
HEAD_DIM = 64
ATT_W = N_HEADS * HEAD_DIM
IDX_HEADS = 4
IDX_DIM = 64
IDX_TOPK = 256
IDX_SCALE = (IDX_HEADS * IDX_DIM) ** -0.5
SPLIT_SIZES = (CONV_W, CONV_W, CONV_W,
               ATT_W, ATT_W, ATT_W,
               IDX_HEADS * IDX_DIM, IDX_DIM, IDX_HEADS,
               D_MODEL, D_MODEL)
IN_W = sum(SPLIT_SIZES)
N_EXPERTS = 32
TOP_K = 4
D_FF = D_MODEL
SWIGLU_LIMIT = 7.0
SWIGLU_ALPHA = 1.702
EXPERT_BLOCK = 256
EPS = 1e-6

kernel_name = 'hybrid_conv_dsa_moe_adaln_block'

def rms_norm(x, g):
    xf = x.astype(jnp.float32)
    y = xf * lax.rsqrt(jnp.mean(xf * xf, axis=-1, keepdims=True) + EPS)
    return (y * g.astype(jnp.float32)).astype(x.dtype)

def causal_depthwise_conv(u, w):
    return lax.conv_general_dilated(
        u, w[:, None, :].astype(u.dtype), window_strides=(1,),
        padding=[(CONV_K - 1, 0)], dimension_numbers=('NWC', 'WIO', 'NWC'),
        feature_group_count=u.shape[-1])

def dsa_sparse_attention(q, k, v, qi, ki, wi):
    bsz, seq = q.shape[0], q.shape[1]
    topk = min(IDX_TOPK, seq // 4)
    nblk = seq // CHUNK
    key_pos = jnp.arange(seq)
    kif = ki.astype(jnp.float32)
    gather = jax.vmap(lambda a, i: a[i])

    def to_blocks(a):
        return jnp.moveaxis(a.reshape(bsz, nblk, CHUNK, *a.shape[2:]), 1, 0)

    def block(args):
        qb, qib, wib, j = args
        limit = (j + 1) * CHUNK
        dots = jnp.einsum('bqhd,bsd->bqhs', qib.astype(jnp.float32), kif)
        score = jnp.einsum('bqh,bqhs->bqs', wib.astype(jnp.float32) * IDX_SCALE, jax.nn.relu(dots))
        score = jnp.where(key_pos[None, None, :] < limit, score, -jnp.inf)
        _, sel = lax.top_k(score, topk)
        valid = sel < limit
        k_sel = gather(k, sel)
        v_sel = gather(v, sel)
        logits = jnp.einsum('bqhd,bqkhd->bqhk', qb, k_sel).astype(jnp.float32) * HEAD_DIM ** -0.5
        logits = jnp.where(valid[:, :, None, :], logits, -jnp.inf)
        p = jax.nn.softmax(logits, axis=-1).astype(v.dtype)
        return jnp.einsum('bqhk,bqkhd->bqhd', p, v_sel)

    out = lax.map(block, (to_blocks(q), to_blocks(qi), to_blocks(wi), jnp.arange(nblk)))
    return jnp.moveaxis(out, 0, 1).reshape(bsz, seq, ATT_W)

def hybrid_mixer(h, w_in, conv_w, q_norm_g, k_norm_g, w_conv_out, w_attn_out, w_o):
    bsz, seq, _ = h.shape
    z = jnp.einsum('bsd,de->bse', h, w_in)
    cuts = list(np.cumsum(SPLIT_SIZES)[:-1])
    xin, gb, gc, q, k, v, qi, ki, wi, g_a, g_b = jnp.split(z, cuts, axis=-1)
    y_a = gb * causal_depthwise_conv(gc * xin, conv_w)
    q = rms_norm(q.reshape(bsz, seq, N_HEADS, HEAD_DIM), q_norm_g)
    k = rms_norm(k.reshape(bsz, seq, N_HEADS, HEAD_DIM), k_norm_g)
    v = v.reshape(bsz, seq, N_HEADS, HEAD_DIM)
    qi = qi.reshape(bsz, seq, IDX_HEADS, IDX_DIM)
    y_b = dsa_sparse_attention(q, k, v, qi, ki, wi)
    merged = (jax.nn.sigmoid(g_a) * jnp.einsum('bsc,cd->bsd', y_a, w_conv_out)
              + jax.nn.sigmoid(g_b) * jnp.einsum('bsc,cd->bsd', y_b, w_attn_out))
    return jnp.einsum('bsd,de->bse', merged, w_o)

def routed_moe(h, w_router, b_router, w_gate_up, b_gate_up, w_down, b_down):
    bsz, seq, d = h.shape
    xt = h.reshape(-1, d)
    n_tok = xt.shape[0]
    logits = (xt @ w_router + b_router).astype(jnp.float32)
    top_val, top_idx = lax.top_k(logits, TOP_K)
    gates = jax.nn.softmax(top_val, axis=-1)
    nk = n_tok * TOP_K
    flat_e = top_idx.reshape(-1)
    flat_tok = jnp.arange(nk) // TOP_K
    flat_g = gates.reshape(-1)
    order = jnp.argsort(flat_e)
    sorted_e = flat_e[order]
    counts = jnp.bincount(flat_e, length=N_EXPERTS)
    padded = (counts + EXPERT_BLOCK - 1) // EXPERT_BLOCK * EXPERT_BLOCK
    pad_end = jnp.cumsum(padded)
    pad_start = pad_end - padded
    start = jnp.cumsum(counts) - counts
    dest = pad_start[sorted_e] + jnp.arange(nk) - start[sorted_e]
    cap = (-(-nk // EXPERT_BLOCK)) * EXPERT_BLOCK + N_EXPERTS * EXPERT_BLOCK
    n_blocks = cap // EXPERT_BLOCK
    buf_tok = jnp.zeros((cap,), jnp.int32).at[dest].set(flat_tok[order].astype(jnp.int32))
    buf_g = jnp.zeros((cap,), jnp.float32).at[dest].set(flat_g[order])
    block_e = jnp.minimum(
        jnp.searchsorted(pad_end, jnp.arange(n_blocks) * EXPERT_BLOCK, side='right'),
        N_EXPERTS - 1)

    def expert_block(args):
        e, tok, g = args
        xb = xt[tok]
        gu = xb @ w_gate_up[e] + b_gate_up[e]
        x_glu = jnp.minimum(gu[:, :D_FF], SWIGLU_LIMIT)
        x_lin = jnp.clip(gu[:, D_FF:], -SWIGLU_LIMIT, SWIGLU_LIMIT)
        act = x_glu * jax.nn.sigmoid(SWIGLU_ALPHA * x_glu) * (x_lin + 1)
        y = act @ w_down[e] + b_down[e]
        return y * g[:, None].astype(y.dtype)

    ys = lax.map(expert_block, (block_e, buf_tok.reshape(n_blocks, EXPERT_BLOCK),
                                buf_g.reshape(n_blocks, EXPERT_BLOCK)))
    out = jnp.zeros_like(xt).at[buf_tok].add(ys.reshape(cap, d).astype(xt.dtype))
    return out.reshape(bsz, seq, d)

def setup_inputs(seed: int = 0) -> dict:
    key = jax.random.key(seed)
    ks = jax.random.split(key, 20)
    f32 = jnp.float32

    def dense(k, shape, fan_in):
        return jax.random.normal(k, shape, f32) * fan_in ** -0.5

    def gain(k, shape):
        return 1.0 + 0.1 * jax.random.normal(k, shape, f32)

    def bias(k, shape, s):
        return s * jax.random.normal(k, shape, f32)

    L = DEPTH
    return {
        'x': jax.random.normal(ks[0], (BATCH, SEQ, D_MODEL), f32),
        'c': jax.random.normal(ks[1], (BATCH, D_MODEL), f32),
        'w_ada': dense(ks[2], (L, D_MODEL, 6 * D_MODEL), D_MODEL),
        'b_ada': bias(ks[3], (L, 6 * D_MODEL), 0.02),
        'norm1_g': gain(ks[4], (L, D_MODEL)),
        'w_in': dense(ks[5], (L, D_MODEL, IN_W), D_MODEL),
        'conv_w': dense(ks[6], (L, CONV_K, CONV_W), CONV_K),
        'q_norm_g': gain(ks[7], (L, HEAD_DIM)),
        'k_norm_g': gain(ks[8], (L, HEAD_DIM)),
        'w_conv_out': dense(ks[9], (L, CONV_W, D_MODEL), CONV_W),
        'w_attn_out': dense(ks[10], (L, ATT_W, D_MODEL), ATT_W),
        'w_o': dense(ks[11], (L, D_MODEL, D_MODEL), D_MODEL),
        'norm2_g': gain(ks[12], (L, D_MODEL)),
        'w_router': dense(ks[13], (L, D_MODEL, N_EXPERTS), D_MODEL),
        'b_router': bias(ks[14], (L, N_EXPERTS), 0.01),
        'w_gate_up': dense(ks[15], (L, N_EXPERTS, D_MODEL, 2 * D_FF), D_MODEL),
        'b_gate_up': bias(ks[16], (L, N_EXPERTS, 2 * D_FF), 0.02),
        'w_down': dense(ks[17], (L, N_EXPERTS, D_FF, D_MODEL), D_FF),
        'b_down': bias(ks[18], (L, N_EXPERTS, D_MODEL), 0.02),
    }

def reference(x, c, w_ada, b_ada, norm1_g, w_in, conv_w, q_norm_g, k_norm_g,
              w_conv_out, w_attn_out, w_o, norm2_g, w_router, b_router,
              w_gate_up, b_gate_up, w_down, b_down):
    for l in range(DEPTH):
        mod = jnp.einsum('bd,de->be', jax.nn.silu(c), w_ada[l]) + b_ada[l]
        sh1, sc1, g1, sh2, sc2, g2 = [m[:, None, :] for m in jnp.split(mod, 6, axis=-1)]
        h = rms_norm(x, norm1_g[l]) * (1 + sc1) + sh1
        x = x + g1 * hybrid_mixer(h, w_in[l], conv_w[l], q_norm_g[l], k_norm_g[l],
                                  w_conv_out[l], w_attn_out[l], w_o[l])
        h = rms_norm(x, norm2_g[l]) * (1 + sc2) + sh2
        x = x + g2 * routed_moe(h, w_router[l], b_router[l], w_gate_up[l], b_gate_up[l],
                                w_down[l], b_down[l])
    return x


_drawn_inputs = setup_inputs


def setup_inputs(seed=0):
    import zlib

    import numpy as np

    out = dict(_drawn_inputs(seed))
    spreads = {}
    factors = {'q_norm_g': 3.949, 'k_norm_g': 4.021, 'b_router': 3.2, 'b_gate_up': 8.0, 'b_down': 8.0}
    for name, (base, spread) in spreads.items():
        noise = np.random.default_rng([zlib.crc32(name.encode()), seed]).standard_normal(out[name].shape)
        drawn = base * np.exp(spread * noise) if base else spread * noise
        out[name] = __import__('jax').numpy.asarray(drawn.astype(out[name].dtype))
    for name, factor in factors.items():
        out[name] = (out[name] * factor).astype(out[name].dtype)
    return out
```

```python
from contextlib import ExitStack

import concourse.bass as bass
from concourse import mybir

F32 = mybir.dt.float32
BF16 = mybir.dt.bfloat16
I32 = mybir.dt.int32
U32 = mybir.dt.uint32
ALU = mybir.AluOpType
ACT = mybir.ActivationFunctionType
AX_X = mybir.AxisListType.X

P = 128
D = 1024
T = 256
NT = T // P
KC = D // P
CONV = 512
HEADS = 8
HD = 64
IDX_HEADS = 4
IDX_SCALE = (IDX_HEADS * 64) ** -0.5
CHUNK = 64
TOPK = 64
EXPERTS = 32
ROUTE = 4
FF = 1024
SLOTS = 64
LIMIT = 7.0
ALPHA = 1.702
EPS = 1e-6
NEG = -3.0e38
TAKEN = -3.3e38
UNSEEN = -1.0e30

BANK = 512
RING = 9
FRONT_RING = 6
SLOT = 4096
XIN, GB, GC, Q, K, V, QI, KI, WI, GA, GBR = 0, 512, 1024, 1536, 2048, 2560, 3072, 3328, 3392, 3396, 4420
IN_BLOCK = {"xin": (XIN, 512), "gb": (GB, 512), "gc": (GC, 512), "q": (Q, 512), "k": (K, 512), "v": (V, 512),
            "idx": (QI, GA - QI), "ga0": (GA, 512), "ga1": (GA + 512, 512), "gB0": (GBR, 512), "gB1": (GBR + 512, 512)}
ADA = [("ada", b) for b in range(12)]
STREAM = (ADA[0:4] + [("in", n) for n in ("idx", "q", "k", "v", "xin")] + ADA[4:6] + [("in", "gc"), ("in", "gb")]
          + ADA[6:8] + [("in", "ga0"), ("in", "ga1")] + ADA[8:10] + [("in", "gB0"), ("in", "gB1")] + ADA[10:12]
          + [("conv_out", 0), ("attn_out", 0), ("w_o", 0), ("w_o", 1)])
ITEM = {item: i for i, item in enumerate(STREAM)}
PE_ITEMS = [item for item in STREAM if item[0] != "ada"]
FRONT_PE = len(PE_ITEMS)
FRONT_USES = [len([i for i in range(len(STREAM)) if i % FRONT_RING == s]) for s in range(FRONT_RING)] \
    + [0] * (RING - FRONT_RING)

JOBS = (["qi", "kiwi", "q0", "q1", "k0", "k1", "v0", "v1", "xin0", "xin1", "gc0", "gc1", "mod4", "mod5", "gb0", "gb1",
         "mod6", "mod7", "ga0", "ga1", "ga2", "ga3", "mod8", "mod9", "gB0", "gB1", "gB2", "gB3", "mod10", "mod11"]
        + [f"pa{n}" for n in range(4)] + [f"pb{n}" for n in range(4)] + [f"wo{n}" for n in range(4)])
JOB = {name: i for i, name in enumerate(JOBS)}
UNITS = 2 * 4
FIRST_UNIT_JOB = JOB["xin0"]


def hybrid_block(nc, x, c, w_ada, b_ada, norm1_g, w_in, conv_w, q_norm_g, k_norm_g, w_conv_out, w_attn_out, w_o,
                 norm2_g, w_router, b_router, w_gate_up, b_gate_up, w_down, b_down, out):
    with ExitStack() as ctx:
        def sb(name, shape, dt=F32):
            return ctx.enter_context(nc.sbuf_tensor(name, shape, dt))

        def sem(name):
            return ctx.enter_context(nc.semaphore(name))

        ps = ctx.enter_context(nc.psum_tensor("ps", [P, 8, BANK], F32))

        ring = sb("ring", [P, RING, SLOT])
        xs = sb("xs", [P, NT, D])
        modacc = sb("modacc", [P, 2, D])
        featT = sb("featT", [P, 2048])
        work = sb("work", [P, 4096])
        g1_row = sb("g1_row", [P, D])
        a2_row = sb("a2_row", [P, D])
        sh2_row = sb("sh2_row", [P, D])
        g2_row = sb("g2_row", [P, D])
        prod = sb("prod", [P, BANK])
        iota = sb("iota", [P, T])
        ident = sb("ident", [P, P])
        ones = sb("ones", [P, P])
        before = sb("before", [P, P], BF16)
        ones_b = sb("ones_b", [P, P], BF16)
        zeros_b = sb("zeros_b", [1, P], BF16)
        pick = sb("pick", [96, EXPERTS])
        small = sb("small", [P, 32])
        wr = sb("wr", [P, KC, EXPERTS])
        br = sb("br", [1, EXPERTS])
        vec = sb("vec", [P, 64])
        rank = sb("rank", [P, NT, EXPERTS])
        gate = sb("gate", [P, NT, EXPERTS])
        counts = sb("counts", [1, EXPERTS], I32)

        ov = ring[:, FRONT_RING:RING, :].rearrange("p s n -> p (s n)")
        xn = ov[:, 0:2048].rearrange("p (i n) -> p i n", i=NT)
        sgA = ov[:, 0:2048].rearrange("p (d t) -> p d t", t=T)
        sgB = ov[:, 2048:4096].rearrange("p (d t) -> p d t", t=T)
        q_tok = ov[:, 4096:5120].rearrange("p (i n) -> p i n", i=NT)
        k_tok = ov[:, 5120:6144].rearrange("p (i n) -> p i n", i=NT)
        v_tok = ov[:, 6144:7168].rearrange("p (i n) -> p i n", i=NT)
        yA = ov[:, 4096:5120].rearrange("p (c t) -> p c t", t=T)
        qT = ov[:, 7168:8192].rearrange("p (c t) -> p c t", t=T)
        kT = ov[:, 8192:9216].rearrange("p (c t) -> p c t", t=T)
        qiT = ov[:, 9216:9728].rearrange("p (c t) -> p c t", t=T)
        kiT = ov[:, 9728:9984]
        gains = ov[:, 9984:10112].rearrange("p (a d) -> p a d", a=2)
        xinS = ov[:, 10112:11136].rearrange("p (c t) -> p c t", t=T)
        conv_u = ov[:, 11136:12168].rearrange("p (c t) -> p c t", t=T + 2)

        rows = prod[0:28, 0:P]
        ada_bias = prod[32:44, :]
        hT = featT[:, :].rearrange("p (c t) -> p c t", t=T)
        mT = hT
        h2T = featT[:, :].rearrange("p (i k t) -> p i k t", i=NT, k=KC)
        relu = work[:, 0:1024].rearrange("p (b h t) -> p b h t", b=2, h=2)
        yB = work[:, 0:1024].rearrange("p (c t) -> p c t", t=T)
        score = work[:, 1024:1536].rearrange("p (i s) -> p i s", i=NT)
        am = work[:, 1536:2048].rearrange("p (i s) -> p i s", i=NT)
        sq = work[:, 2048:2560]
        lg = work[:, 2048:3072].rearrange("p (b h s) -> p b h s", b=2, h=2)
        pT = work[:, 3072:4096].rearrange("p (b h s t) -> p b h s t", b=2, h=2, s=2)
        h2 = work[:, 0:2048].rearrange("p (i n) -> p i n", i=NT)
        bd = work[0:EXPERTS, 2048:3072]
        bias3 = work[0:96, 3072:4096].bitcast(BF16)
        bias_raw = modacc[0:96, :, :].rearrange("p i n -> p (i n)")
        part = [modacc[:, 0, :].bitcast(BF16).rearrange("p (i n) -> p i n", i=NT),
                modacc[:, 1, :].bitcast(BF16).rearrange("p (i n) -> p i n", i=NT),
                g1_row[:, :].bitcast(BF16).rearrange("p (i n) -> p i n", i=NT)]
        gT = prod[0:EXPERTS, 0:T]

        xg = featT[:, 0:512]
        xg_o = featT[:, 512:1024]
        glu = featT[:, 1024:1536]
        sig = featT[:, 1536:2048]
        lin = work[:, 0:512]
        act_v = work[:, 512:1024]
        actT = work[:, 1024:1536]
        y = work[:, 1536:2048]
        y_o = sh2_row[:, 0:512]
        sgT = sh2_row[:, 512:768]
        sgT_o = sh2_row[:, 768:1024]
        sg = a2_row[:, 0:256].rearrange("p (i j s) -> p i j s", i=NT, j=2)
        pick_e = a2_row[:, 256:288].bitcast(BF16)
        onehot = a2_row[:, 288:352].bitcast(BF16).rearrange("p (i s) -> p i s", i=NT)

        silu_c = vec[:, 0:8]
        sig_c = vec[:, 8:16]
        a1 = vec[:, 16:24]
        sh1 = vec[:, 24:32]
        wi = vec[:, 32:40].rearrange("p (i h) -> p i h", i=NT)
        ms = vec[:, 40:42]
        rstd = vec[:, 42:44]
        neg_max = vec[:, 44:48].rearrange("p (b h) -> p b h", b=2)
        row_sum = vec[:, 48:52].rearrange("p (b h) -> p b h", b=2)
        top8 = vec[:, 52:60]
        hs = sb("hs", [P, 32])
        rt = sb("rt", [P, 64])
        lr = sb("lr", [P, NT, EXPERTS])
        idx8 = sb("idx8", [P, NT, 8], U32)
        m_b = sb("m_b", [P, NT, EXPERTS], BF16)
        hit = prod[:, 0:256].rearrange("p (i k e) -> p i k e", i=NT, k=ROUTE)
        hit_g = prod[:, 0:256].rearrange("p (i k e) -> p i k e", i=NT, k=ROUTE)
        mask = prod[:, 256:320].rearrange("p (i e) -> p i e", i=NT)

        landed = [sem(f"landed{s}") for s in range(RING)]
        w_used = sem("w_used")
        ada_steps = sem("ada_steps")
        x_in = sem("x_in")
        rows_in = sem("rows_in")
        small_in = sem("small_in")
        gains_in = sem("gains_in")
        down_bias_in = sem("down_bias_in")
        gu_bias_in = sem("gu_bias_in")
        bias_steps = sem("bias_steps")
        consts = sem("consts")
        dve_step = sem("dve_step")
        act_step = sem("act_step")
        rows_T = sem("rows_T")
        rows_out = sem("rows_out")
        sig_c_done = sem("sig_c_done")
        silu_done = sem("silu_done")
        sumsq1 = sem("sumsq1")
        ms1_done = sem("ms1_done")
        std1_done = sem("std1_done")
        xn_ready = sem("xn_ready")
        xT_done = sem("xT_done")
        mod_summed = sem("mod_summed")
        mod1_ready = sem("mod1_ready")
        hT_dve = sem("hT_dve")
        hT_act = sem("hT_act")
        job_done = sem("job_done")
        bank_read = [sem(f"bank_read{b}") for b in range(2)]
        dots_done = sem("dots_done")
        relu_done = sem("relu_done")
        score_done = sem("score_done")
        mask_ready = sem("mask_ready")
        head_ms = sem("head_ms")
        head_std = sem("head_std")
        qk_normed = sem("qk_normed")
        qk_T = sem("qk_T")
        qkT_ready = sem("qkT_ready")
        logits_done = sem("logits_done")
        logits_read = sem("logits_read")
        max_ready = sem("max_ready")
        exp_done = sem("exp_done")
        probs_ready = sem("probs_ready")
        probs_T = sem("probs_T")
        pT_ready = sem("pT_ready")
        pv_done = sem("pv_done")
        yB_ready = sem("yB_ready")
        yA_ready = sem("yA_ready")
        merged = sem("merged")
        x1_ready = sem("x1_ready")
        sumsq2 = sem("sumsq2")
        ms2_done = sem("ms2_done")
        std2_done = sem("std2_done")
        h2_ready = sem("h2_ready")
        h2_T = sem("h2_T")
        h2T_dve = sem("h2T_dve")
        h2T_act = sem("h2T_act")
        part0 = sem("part0")
        rest0 = sem("rest0")
        part1 = sem("part1")
        parts_ready = sem("parts_ready")
        router_done = sem("router_done")
        top_ready = sem("top_ready")
        top_exp = sem("top_exp")
        mask_b_ready = sem("mask_b_ready")
        gates_ready = sem("gates_ready")
        rank_done = sem("rank_done")
        gate_T = sem("gate_T")
        gT_ready = sem("gT_ready")
        routed = sem("routed")

        onehot_ready = sem("onehot_ready")
        sg_ready = sem("sg_ready")
        pick_ready = sem("pick_ready")
        gathered = sem("gathered")
        xg_ready = sem("xg_ready")
        gu_done = sem("gu_done")
        glu_ready = sem("glu_ready")
        lin_ready = sem("lin_ready")
        prod_ready = sem("prod_ready")
        sig_ready = sem("sig_ready")
        act_ready = sem("act_ready")
        act_T = sem("act_T")
        actT_ready = sem("actT_ready")
        sgT_ready = sem("sgT_ready")
        down_done = sem("down_done")
        y_ready = sem("y_ready")
        main_sems = (onehot_ready, sg_ready, gathered, xg_ready, gu_done, glu_ready, lin_ready, prod_ready,
                     sig_ready, act_ready, act_T, actT_ready, sgT_ready, down_done, y_ready)
        more_sems = tuple(sem("more_" + n) for n in ("onehot_ready", "sg_ready", "gathered", "xg_ready", "gu_done",
                                                     "glu_ready", "lin_ready", "prod_ready", "sig_ready",
                                                     "act_ready", "act_T", "actT_ready", "sgT_ready", "down_done",
                                                     "y_ready"))
        acc_done = sem("acc_done")
        fin_ready = sem("fin_ready")
        out_done = sem("out_done")

        GLU, LIN, AUX, YB = 4, 5, 6, 7
        MORE_PASSES = range(1, T // SLOTS)

        def slot(item):
            return ring[:, ITEM[item] % FRONT_RING, :]

        def wait_landed(eng, item):
            i = ITEM[item]
            eng.wait_ge(landed[i % FRONT_RING], 16 * (i // FRONT_RING + 1))

        def turns(eng, body):
            body(0, 0)
            with eng.Fori(0, (EXPERTS - 2) // 3) as group:
                for j in range(3):
                    body(1 + j, group)
            body(EXPERTS - 1, 0)

        block = ctx.enter_context(nc.Block())

        @block.sync
        def _(sp):
            sp.dma_start(rows[0:8, :], c.rearrange("b (k p) -> (b k) p", p=P)).then_inc(rows_in, 16)
            sp.dma_start(rows[8:16, :], norm1_g.rearrange("b (k p) -> (b k) p", p=P)).then_inc(rows_in, 16)
            sp.dma_start(rows[16:28, :], conv_w.rearrange("b j (k p) -> (b j k) p", p=P)).then_inc(rows_in, 16)
            sp.dma_start(ada_bias, b_ada.rearrange("b (k n) -> (b k) n", n=BANK)).then_inc(rows_in, 16)
            sp.dma_start(xs[:], x[0].rearrange("(i p) n -> p i n", p=P)).then_inc(x_in, 16)
            for i, (kind, n) in enumerate(STREAM):
                if i >= FRONT_RING:
                    was = STREAM[i - FRONT_RING]
                    if was[0] == "ada":
                        sp.wait_ge(ada_steps, KC * (was[1] + 1))
                    else:
                        sp.wait_ge(w_used, PE_ITEMS.index(was) + 1)
                if kind == "ada":
                    src, m = w_ada[0, :, n * BANK:(n + 1) * BANK], BANK
                elif kind == "in":
                    at, m = IN_BLOCK[n]
                    src = w_in[0, :, at:at + m]
                elif kind == "conv_out":
                    src, m = w_conv_out[0], D
                elif kind == "attn_out":
                    src, m = w_attn_out[0], D
                else:
                    src, m = w_o[0, n * 512:(n + 1) * 512, :], D
                k = src.shape[0] // P
                sp.dma_start(ring[:, i % FRONT_RING, 0:k * m].rearrange("p (k m) -> p k m", m=m),
                             src.rearrange("(k p) m -> p k m", p=P)).then_inc(landed[i % FRONT_RING], 16)

            gu_src = w_gate_up.rearrange("l e (q a p) n -> (l e q) p a n", q=4, p=P)
            dn_src = w_down.rearrange("l e (q a p) n -> (l e q) p a n", q=2, p=P)

            def load_expert(first, group):
                for q in range(6):
                    n = 6 * first + q
                    s = n % RING
                    if first == 0:
                        was = STREAM[max(i for i in range(len(STREAM)) if i % FRONT_RING == s)]
                        if was[0] == "ada":
                            sp.wait_ge(ada_steps, KC * (was[1] + 1))
                        else:
                            sp.wait_ge(w_used, PE_ITEMS.index(was) + 1)
                    else:
                        sp.wait_ge(w_used, FRONT_PE + 18 * group + n - RING + 1)
                    e = first + 3 * group
                    if q < 4:
                        src = gu_src[e * 4 + q]
                        dst = ring[:, s, :].rearrange("p (a n) -> p a n", a=2)
                    else:
                        src = dn_src[e * 2 + q - 4]
                        dst = ring[:, s, :].rearrange("p (a n) -> p a n", a=4)
                    sp.dma_start(dst, src).then_inc(landed[s], 16)
                if first == 0:
                    sp.wait_ge(merged, 4)

            turns(sp, load_expert)
            for i in range(NT):
                sp.wait_ge(fin_ready, i + 1)
                sp.dma_start(out[0, i * P:(i + 1) * P, :], xs[:, i, :]).then_inc(out_done, 16)
            sp.wait_ge(out_done, 16 * NT)

        @block.gpsimd
        def _(pool):
            pool.memset(ident[:], 0.0).then_inc(consts, 1)
            pool.memset(ones[:], 1.0).then_inc(consts, 1)
            pool.memset(ones_b[:], 1.0).then_inc(consts, 1)
            pool.memset(pick[:], 0.0).then_inc(consts, 1)
            pool.memset(zeros_b[:], 0.0).then_inc(consts, 1)
            pool.iota(iota[:], [[1, T]], base=0, channel_multiplier=0,
                      allow_small_or_imprecise_dtypes=True).then_inc(consts, 1)
            pool.wait_ge(consts, 6)
            pool.affine_select(out=ident[:], in_=ident[:], compare_op=ALU.not_equal, fill=1.0, base=0,
                               pattern=[[-1, P]], channel_multiplier=1).then_inc(consts, 1)
            pool.affine_select(out=before[:], in_=ones_b[:], compare_op=ALU.is_gt, fill=0.0, base=0,
                               pattern=[[1, P]], channel_multiplier=-1).then_inc(consts, 1)
            for r in range(3):
                pool.affine_select(out=pick[:], in_=pick[:], compare_op=ALU.not_equal, fill=1.0, base=-32 * r,
                                   pattern=[[-1, EXPERTS]], channel_multiplier=1).then_inc(consts, 1)
                pool.wait_ge(consts, 9 + r)
            pool.wait_ge(mod_summed, 6)
            for r in range(3):
                pool.dma_start(bias_raw[32 * r:32 * r + 32, :], b_gate_up[0]).then_inc(gu_bias_in, 16)
            pool.wait_ge(gu_bias_in, 48)
            pool.wait_ge(pv_done, UNITS)
            n = 0
            for r in range(3):
                rs = slice(32 * r, 32 * r + 32)
                for step in range(r + 1):
                    if step:
                        pool.tensor_tensor(bias_raw[rs, :], bias_raw[rs, :], bias3[rs, :], ALU.subtract)\
                            .then_inc(bias_steps, 1)
                        n += 1
                        pool.wait_ge(bias_steps, n)
                    pool.tensor_copy(bias3[rs, :], bias_raw[rs, :]).then_inc(bias_steps, 1)
                    n += 1
                    pool.wait_ge(bias_steps, n)
            for i in range(NT):
                pool.wait_ge(part0, i + 1)
                pool.wait_ge(h2_T, i + 1)
                pool.tensor_tensor(h2[:, i, :], h2[:, i, :], part[0][:, i, :], ALU.subtract).then_inc(rest0, 1)
                pool.wait_ge(rest0, i + 1)
                pool.wait_ge(part1, i + 1)
                pool.wait_ge(x1_ready, 4)
                pool.tensor_tensor(part[2][:, i, :], h2[:, i, :], part[1][:, i, :], ALU.subtract)\
                    .then_inc(parts_ready, 1)

        @block.scalar
        def _(act):
            n_step = [0]

            def step(ins):
                n_step[0] += 1
                ins.then_inc(act_step, 1)
                act.wait_ge(act_step, n_step[0])

            act.wait_ge(rows_out, 1)
            act.activation(sig_c, small[:, 0:8], ACT.Sigmoid).then_inc(sig_c_done, 1)
            act.wait_ge(x_in, 16)
            for i in range(NT):
                act.activation(featT[:, 0:D], xs[:, i, :], ACT.Square, accum_out=ms[:, i:i + 1]).then_inc(sumsq1, 1)
                act.wait_ge(sumsq1, i + 1)
            act.wait_ge(ms1_done, 1)
            act.activation(rstd[:, :], ms[:, :], ACT.Sqrt).then_inc(std1_done, 1)

            act.wait_ge(xT_done, 1)
            act.wait_ge(mod1_ready, 1)
            for k in range(4, KC):
                act.activation(hT[:, k, :], ps[:, k // 2, (k % 2) * T:(k % 2 + 1) * T], ACT.Identity, bias=sh1[:, k:k + 1],
                               scale=a1[:, k:k + 1]).then_inc(hT_act, 1)

            act.dma_start(wr[:], w_router[0].rearrange("(k p) e -> p k e", p=P)).then_inc(small_in, 16)
            act.dma_start(br[:], b_router[0:1, :]).then_inc(small_in, 16)
            act.dma_start(a2_row[:], norm2_g[0:1, :].broadcast_to([P, D])).then_inc(small_in, 16)
            act.dma_start(gains[:, 0, :], q_norm_g[0:1, :].broadcast_to([P, HD])).then_inc(gains_in, 16)
            act.dma_start(gains[:, 1, :], k_norm_g[0:1, :].broadcast_to([P, HD])).then_inc(gains_in, 16)

            def job_copy(name, dst, func=ACT.Copy, scale=1.0):
                j = JOB[name]
                act.wait_ge(job_done, j + 1)
                act.activation(dst, ps[:, 4 + j % 2, :], func, scale=scale).then_inc(bank_read[j % 2], 1)

            def fold(ap):
                return ap.rearrange("p c t -> p (c t)")

            job_copy("qi", fold(qiT))
            j = JOB["kiwi"]
            act.wait_ge(job_done, j + 1)
            step(act.activation(kiT, ps[:, 5, 0:T], ACT.Copy))
            act.activation(vec[:, 32:40], ps[:, 5, T:T + 8], ACT.Copy, scale=IDX_SCALE).then_inc(bank_read[1], 1)
            for i in range(NT):
                w = P * (i + 1)
                act.wait_ge(dots_done, i + 1)
                if i:
                    act.wait_ge(score_done, i)
                for b in range(2):
                    act.activation(relu[:, b, :, 0:w], ps[:, 2 * i + b, :].rearrange("p (h s) -> p h s", h=2)[:, :, 0:w],
                                   ACT.Relu).then_inc(relu_done, 1)
            for i in range(NT):
                job_copy(f"q{i}", q_tok[:, i, :])
            for i in range(NT):
                job_copy(f"k{i}", k_tok[:, i, :])
            act.wait_ge(head_ms, 1)
            act.activation(hs[:], hs[:], ACT.Sqrt).then_inc(head_std, 1)
            for i in range(NT):
                job_copy(f"v{i}", v_tok[:, i, :])
            for n, dst in enumerate((qT, qT, kT, kT)):
                act.wait_ge(qk_T, n + 1)
                act.activation(dst[:, :, (n % 2) * P:(n % 2) * P + P], ps[:, n, :].rearrange("p (c t) -> p c t", c=4),
                               ACT.Copy).then_inc(qkT_ready, 1)

            def softmax_exp(u):
                i, w = u // 4, P * (u // 4 + 1)
                act.wait_ge(max_ready, u + 1)
                for h in range(2):
                    act.activation(lg[:, u % 2, h, 0:w], lg[:, u % 2, h, 0:w], ACT.Exp, bias=neg_max[:, u % 2, h:h + 1],
                                   accum_out=row_sum[:, u % 2, h:h + 1]).then_inc(exp_done, 1)

            def probs_T_copy(u):
                n = u // 4 + 1
                act.wait_ge(probs_T, u + 1)
                if u >= 2:
                    act.wait_ge(pv_done, u - 1)
                act.activation(pT[:, u % 2, :, 0:n, :],
                               ps[:, 6, :].rearrange("p (h s t) -> p h s t", h=2, s=2)[:, :, 0:n, :],
                               ACT.Copy).then_inc(pT_ready, 1)

            def pv_copy(u):
                i, hp = u // 4, u % 4
                act.wait_ge(pv_done, u + 1)
                act.activation(yB[:, hp, i * P:(i + 1) * P], ps[:, 7, (u % 2) * P:(u % 2) * P + P], ACT.Copy)\
                   .then_inc(yB_ready, 1)

            for name in JOBS[FIRST_UNIT_JOB:JOB["pa0"]]:
                j = JOB[name]
                n = int(name[-1])
                if name[:-1] == "xin":
                    job_copy(name, fold(xinS[:, 2 * n:2 * n + 2, :]))
                elif name[:-1] == "ga":
                    job_copy(name, fold(sgA[:, 2 * n:2 * n + 2, :]), ACT.Sigmoid)
                elif name[:-1] == "gB":
                    job_copy(name, fold(sgB[:, 2 * n:2 * n + 2, :]), ACT.Sigmoid)
                elif name in ("mod4", "mod5"):
                    job_copy(name, g1_row[:, (n - 4) * BANK:(n - 3) * BANK])
                elif name in ("mod6", "mod7"):
                    job_copy(name, sh2_row[:, (n - 6) * BANK:(n - 5) * BANK])
                elif name in ("mod10", "mod11"):
                    job_copy(name, g2_row[:, n * BANK:(n + 1) * BANK])
                k = j - FIRST_UNIT_JOB
                if k >= 2 and k % 2 == 0 and k // 2 - 1 < UNITS:
                    pv_copy(k // 2 - 1)
                if k % 2 == 1 and k // 2 < UNITS:
                    probs_T_copy(k // 2)
                if k % 2 == 0 and k // 2 < UNITS:
                    softmax_exp(k // 2)

            act.wait_ge(pv_done, UNITS)
            act.dma_start(bd, b_down[0]).then_inc(down_bias_in, 16)

            def square_sum(i):
                act.wait_ge(x1_ready, 2 * i + 2)
                act.activation(h2[:, i, :], xs[:, i, :], ACT.Square, accum_out=ms[:, i:i + 1]).then_inc(sumsq2, 1)

            def root(i):
                act.wait_ge(ms2_done, i + 1)
                act.activation(rstd[:, i:i + 1], ms[:, i:i + 1], ACT.Sqrt).then_inc(std2_done, 1)

            def h2T_copy(i):
                act.wait_ge(h2_T, i + 1)
                act.wait_ge(job_done, len(JOBS))
                act.activation(h2T[:, i, 4:8, :], ps[:, 2 * i + 1, :].rearrange("p (k t) -> p k t", k=4), ACT.Copy)\
                   .then_inc(h2T_act, 1)

            def split(i):
                act.wait_ge(h2_ready, i + 1)
                if i == 0:
                    act.wait_ge(bias_steps, 9)
                act.activation(part[0][:, i, :], h2[:, i, :], ACT.Copy).then_inc(part0, 1)
                act.wait_ge(rest0, i + 1)
                act.activation(part[1][:, i, :], h2[:, i, :], ACT.Copy).then_inc(part1, 1)

            square_sum(0)
            root(0)
            split(0)
            square_sum(1)
            h2T_copy(0)
            root(1)
            h2T_copy(1)
            split(1)
            for i in range(NT):
                act.wait_ge(top_ready, i + 1)
                act.activation(rt[:, 16 + 4 * i:20 + 4 * i], rt[:, 8 * i:8 * i + 4], ACT.Exp,
                               bias=rt[:, 24 + i:25 + i], accum_out=rt[:, 26 + i:27 + i]).then_inc(top_exp, 1)

            def evacuate_gather(sems, dst, v):
                act.wait_ge(sems[2], v)
                act.activation(dst, ps[:, AUX, :], ACT.Copy).then_inc(sems[3], 1)

            def gate_sigmoid(sems, v):
                act.wait_ge(sems[5], v)
                act.activation(sig, glu, ACT.Sigmoid, scale=ALPHA).then_inc(sems[8], 1)

            def evacuate_transposes(sems, dst, v):
                act.wait_ge(sems[10], v)
                act.activation(actT, ps[:, GLU, :], ACT.Copy).then_inc(sems[11], 1)
                act.activation(dst, ps[:, LIN, 0:T], ACT.Copy).then_inc(sems[12], 1)

            evacuate_gather(main_sems, xg, 1)
            more = act.alloc_register("act_more")
            act.reg_mov(more, 0)

            def expert(first, group):
                e = act.snap(first + 3 * group)
                count = act.value_load(counts[0:1, bass.ds(e, 1)])
                with act.If(count > SLOTS):
                    with act.Fori(1, T // SLOTS) as p:
                        with act.If(count > p * SLOTS):
                            v = act.snap(more) + 1
                            evacuate_gather(more_sems, xg_o, v)
                            gate_sigmoid(more_sems, v)
                            evacuate_transposes(more_sems, sgT_o, v)
                            act.reg_add(more, more, 1)
                gate_sigmoid(main_sems, e + 1)
                if first < EXPERTS - 1:
                    evacuate_gather(main_sems, xg, e + 2)
                evacuate_transposes(main_sems, sgT, e + 1)

            act.wait_ge(routed, 1)
            turns(act, expert)

        @block.vector
        def _(dve):
            n_step = [0]

            def step(ins):
                n_step[0] += 1
                ins.then_inc(dve_step, 1)
                dve.wait_ge(dve_step, n_step[0])

            def ada_pair(p):
                if p >= 2:
                    dve.wait_ge(mod_summed, p - 1)
                for b in (2 * p, 2 * p + 1):
                    wait_landed(dve, ("ada", b))
                    acc = modacc[:, p % 2, (b % 2) * BANK:(b % 2 + 1) * BANK]
                    for k in range(KC):
                        w = slot(("ada", b))[:, k * BANK:(k + 1) * BANK]
                        if k == 0:
                            ins = dve.tensor_scalar(acc, w, silu_c[:, 0:1], None, ALU.mult)
                        else:
                            ins = dve.scalar_tensor_tensor(out=acc, in0=w, scalar=silu_c[:, k:k + 1], in1=acc,
                                                           op0=ALU.mult, op1=ALU.add)
                        ins.then_inc(ada_steps, 1)
                        dve.wait_ge(ada_steps, KC * b + k + 1)

            dve.memset(conv_u[:, :, 0:2], 0.0)
            dve.wait_ge(rows_T, 1)
            dve.tensor_copy(small[:, 0:28], ps[:, 7, 0:28]).then_inc(rows_out, 1)
            dve.wait_ge(sig_c_done, 1)
            dve.wait_ge(rows_out, 1)
            dve.tensor_tensor(silu_c, small[:, 0:8], sig_c, ALU.mult).then_inc(silu_done, 1)
            dve.wait_ge(silu_done, 1)
            dve.wait_ge(sumsq1, 2)
            dve.tensor_scalar(ms[:, :], ms[:, :], 1.0 / D, EPS, ALU.mult, ALU.add).then_inc(ms1_done, 1)
            dve.wait_ge(std1_done, 1)
            step(dve.reciprocal(rstd[:, :], rstd[:, :]))
            for i in range(NT):
                dve.tensor_scalar(xn[:, i, :], xs[:, i, :], rstd[:, i:i + 1], None, ALU.mult).then_inc(xn_ready, 1)
            ada_pair(0)
            ada_pair(1)
            dve.wait_ge(mod_summed, 2)
            step(dve.tensor_copy(sh1, ps[:, 7, 32:40]))
            dve.scalar_tensor_tensor(out=a1, in0=ps[:, 7, 40:48], scalar=1.0, in1=small[:, 8:16], op0=ALU.add,
                                     op1=ALU.mult).then_inc(mod1_ready, 1)
            dve.wait_ge(mod1_ready, 1)
            dve.wait_ge(xT_done, 1)
            for k in range(4):
                dve.tensor_scalar(hT[:, k, :], ps[:, k // 2, (k % 2) * T:(k % 2 + 1) * T], a1[:, k:k + 1], sh1[:, k:k + 1], ALU.mult,
                                  ALU.add).then_inc(hT_dve, 1)

            for i in range(NT):
                w = P * (i + 1)
                dve.wait_ge(relu_done, 2 * i + 2)
                s = score[:, i, 0:w]
                step(dve.tensor_scalar(s, relu[:, 0, 0, 0:w], wi[:, i, 0:1], None, ALU.mult))
                for h in range(1, IDX_HEADS):
                    ins = dve.scalar_tensor_tensor(out=s, in0=relu[:, h % 2, h // 2, 0:w], scalar=wi[:, i, h:h + 1],
                                                   in1=s, op0=ALU.mult, op1=ALU.add)
                    if h < IDX_HEADS - 1:
                        step(ins)
                ins.then_inc(score_done, 1)
                dve.wait_ge(score_done, i + 1)
                step(dve.memset(score[0:CHUNK, i, w - CHUNK:w], NEG))
                for r in range(TOPK // 8):
                    step(dve.max(top8, s))
                    step(dve.match_replace(s, top8, s, TAKEN))
                dve.tensor_scalar(am[:, i, 0:w], s, (NEG + TAKEN) / 2, UNSEEN, ALU.is_gt, ALU.mult)\
                   .then_inc(mask_ready, 1)

            for n, (name, src) in enumerate((("q0", q_tok), ("q1", q_tok), ("k0", k_tok), ("k1", k_tok))):
                j = JOB[name]
                dve.wait_ge(bank_read[j % 2], j // 2 + 1)
                step(dve.tensor_tensor(sq, src[:, n % 2, :], src[:, n % 2, :], ALU.mult))
                step(dve.tensor_reduce(hs[:, 8 * n:8 * n + 8], sq.rearrange("p (h d) -> p h d", h=HEADS), AX_X, ALU.add))
            dve.tensor_scalar(hs[:], hs[:], 1.0 / HD, EPS, ALU.mult, ALU.add).then_inc(head_ms, 1)
            dve.wait_ge(head_std, 1)
            step(dve.reciprocal(hs[:], hs[:]))
            dve.wait_ge(gains_in, 32)
            for n, src in enumerate((q_tok, q_tok, k_tok, k_tok)):
                v = src[:, n % 2, :].rearrange("p (h d) -> p h d", h=HEADS)
                step(dve.tensor_tensor(v, v, hs[:, 8 * n:8 * n + 8].unsqueeze(2).broadcast_to([P, HEADS, HD]), ALU.mult))
                dve.tensor_tensor(v, v, gains[:, n // 2, :].unsqueeze(1).broadcast_to([P, HEADS, HD]), ALU.mult)\
                   .then_inc(qk_normed, 1)

            def softmax_max(u):
                i, w, b = u // 4, P * (u // 4 + 1), u % 2
                dve.wait_ge(logits_done, u + 1)
                if u >= 2:
                    dve.wait_ge(probs_T, u - 1)
                dve.scalar_tensor_tensor(out=lg[:, b, :, 0:w], in0=ps[:, 2 * b:2 * b + 2, 0:w], scalar=HD ** -0.5,
                                         in1=am[:, i, 0:w].unsqueeze(1).broadcast_to([P, 2, w]), op0=ALU.mult,
                                         op1=ALU.add).then_inc(logits_read, 1)
                dve.wait_ge(logits_read, u + 1)
                dve.tensor_reduce(neg_max[:, b, :], lg[:, b, :, 0:w], AX_X, ALU.max, negate=True)\
                   .then_inc(max_ready, 1)

            def softmax_scale(u):
                w, b = P * (u // 4 + 1), u % 2
                dve.wait_ge(exp_done, 2 * u + 2)
                step(dve.reciprocal(row_sum[:, b, :], row_sum[:, b, :]))
                dve.tensor_tensor(lg[:, b, :, 0:w], lg[:, b, :, 0:w],
                                  row_sum[:, b, :].unsqueeze(2).broadcast_to([P, 2, w]), ALU.mult)\
                   .then_inc(probs_ready, 1)

            def conv(n):
                j = JOB[f"gc{n}"]
                dve.wait_ge(job_done, j + 1)
                jx = JOB[f"xin{n}"]
                dve.wait_ge(bank_read[jx % 2], jx // 2 + 1)
                dve.tensor_tensor(conv_u[:, 2 * n:2 * n + 2, 2:T + 2],
                                  ps[:, 4 + j % 2, :].rearrange("p (c t) -> p c t", c=2),
                                  xinS[:, 2 * n:2 * n + 2, :], ALU.mult).then_inc(bank_read[j % 2], 1)
                dve.wait_ge(bank_read[j % 2], j // 2 + 1)
                if n == 0:
                    dve.wait_ge(qk_T, 4)
                for cc in (2 * n, 2 * n + 1):
                    step(dve.tensor_scalar(yA[:, cc, :], conv_u[:, cc, 0:T], small[:, 16 + cc:17 + cc], None, ALU.mult))
                    for tap in (1, 2):
                        step(dve.scalar_tensor_tensor(out=yA[:, cc, :], in0=conv_u[:, cc, tap:T + tap],
                                                      scalar=small[:, 16 + 4 * tap + cc:17 + 4 * tap + cc],
                                                      in1=yA[:, cc, :], op0=ALU.mult, op1=ALU.add))

            for name in JOBS[FIRST_UNIT_JOB:JOB["pa0"]]:
                j = JOB[name]
                n = int(name[-1])
                bank = ps[:, 4 + j % 2, :]
                if name == "gc0":
                    ada_pair(2)
                if name[:-1] == "gc":
                    conv(n)
                if name == "gc1":
                    ada_pair(3)
                if name[:-1] == "gb":
                    dve.wait_ge(job_done, j + 1)
                    dve.tensor_tensor(yA[:, 2 * n:2 * n + 2, :], bank.rearrange("p (c t) -> p c t", c=2),
                                      yA[:, 2 * n:2 * n + 2, :], ALU.mult).then_inc(bank_read[j % 2], 1)
                if name == "gb1":
                    ada_pair(4)
                if name in ("mod8", "mod9"):
                    a2 = a2_row[:, (n - 8) * BANK:(n - 7) * BANK]
                    dve.wait_ge(job_done, j + 1)
                    dve.wait_ge(small_in, 48)
                    dve.scalar_tensor_tensor(out=a2, in0=bank, scalar=1.0, in1=a2, op0=ALU.add, op1=ALU.mult)\
                       .then_inc(bank_read[j % 2], 1)
                if name == "mod9":
                    ada_pair(5)
                k = j - FIRST_UNIT_JOB
                if k % 2 == 0 and k // 2 < UNITS:
                    softmax_max(k // 2)
                    softmax_scale(k // 2)

            for n in range(4):
                j = JOB[f"pa{n}"]
                jg = JOB[f"ga{n}"]
                dve.wait_ge(job_done, j + 1)
                dve.wait_ge(bank_read[jg % 2], jg // 2 + 1)
                dve.tensor_tensor(mT[:, 2 * n:2 * n + 2, :].rearrange("p c t -> p (c t)"), ps[:, 4 + j % 2, :],
                                  sgA[:, 2 * n:2 * n + 2, :].rearrange("p c t -> p (c t)"), ALU.mult)\
                   .then_inc(bank_read[j % 2], 1)
            for n in range(4):
                j = JOB[f"pb{n}"]
                jg = JOB[f"gB{n}"]
                s = sgB[:, 2 * n:2 * n + 2, :].rearrange("p c t -> p (c t)")
                m = mT[:, 2 * n:2 * n + 2, :].rearrange("p c t -> p (c t)")
                dve.wait_ge(job_done, j + 1)
                dve.wait_ge(bank_read[jg % 2], jg // 2 + 1)
                dve.tensor_tensor(s, ps[:, 4 + j % 2, :], s, ALU.mult).then_inc(bank_read[j % 2], 1)
                dve.wait_ge(bank_read[j % 2], j // 2 + 1)
                dve.tensor_tensor(m, m, s, ALU.add).then_inc(merged, 1)
            dve.wait_ge(bank_read[1], JOB["mod5"] // 2 + 1)
            def residual(n):
                i, half = n // 2, n % 2
                j = JOB[f"wo{n}"]
                cols = slice(half * BANK, (half + 1) * BANK)
                dve.wait_ge(job_done, j + 1)
                if n:
                    dve.wait_ge(x1_ready, n)
                dve.tensor_tensor(prod[:], ps[:, 4 + j % 2, :], g1_row[:, cols], ALU.mult).then_inc(bank_read[j % 2], 1)
                dve.wait_ge(bank_read[j % 2], j // 2 + 1)
                dve.tensor_tensor(xs[:, i, cols], xs[:, i, cols], prod[:], ALU.add).then_inc(x1_ready, 1)

            def norm2_ms(i):
                dve.wait_ge(sumsq2, i + 1)
                dve.tensor_scalar(ms[:, i:i + 1], ms[:, i:i + 1], 1.0 / D, EPS, ALU.mult, ALU.add).then_inc(ms2_done, 1)

            def norm2_rows(i):
                dve.wait_ge(std2_done, i + 1)
                step(dve.reciprocal(rstd[:, i:i + 1], rstd[:, i:i + 1]))
                step(dve.scalar_tensor_tensor(out=h2[:, i, :], in0=xs[:, i, :], scalar=rstd[:, i:i + 1], in1=a2_row[:],
                                              op0=ALU.mult, op1=ALU.mult))
                dve.tensor_tensor(h2[:, i, :], h2[:, i, :], sh2_row[:], ALU.add).then_inc(h2_ready, 1)

            def h2T_copy(i):
                dve.wait_ge(h2_T, i + 1)
                dve.wait_ge(job_done, len(JOBS))
                dve.tensor_copy(h2T[:, i, 0:4, :], ps[:, 2 * i, :].rearrange("p (k t) -> p k t", k=4))\
                   .then_inc(h2T_dve, 1)

            idxf = rt[:, 28:36].rearrange("p (i k) -> p i k", i=NT)

            def route(i):
                dve.wait_ge(router_done, i + 1)
                step(dve.tensor_copy(lr[:, i, :], ps[:, AUX + i, 0:EXPERTS]))
                step(dve.max(rt[:, 8 * i:8 * i + 8], lr[:, i, :]))
                dve.tensor_scalar(rt[:, 24 + i:25 + i], rt[:, 8 * i:8 * i + 1], -1.0, None, ALU.mult)\
                   .then_inc(top_ready, 1)
                step(dve.max_index(idx8[:, i, :], rt[:, 8 * i:8 * i + 8], lr[:, i, :]))
                step(dve.tensor_copy(idxf[:, i, :], idx8[:, i, 0:ROUTE]))
                step(dve.tensor_tensor(hit[:, i], iota[:, 0:EXPERTS].unsqueeze(1).broadcast_to([P, ROUTE, EXPERTS]),
                                       idxf[:, i, :].unsqueeze(2).broadcast_to([P, ROUTE, EXPERTS]), ALU.is_equal))
                step(dve.tensor_reduce(mask[:, i, :], hit[:, i].rearrange("p k e -> p e k"), AX_X, ALU.add))
                dve.tensor_copy(m_b[:, i, :], mask[:, i, :]).then_inc(mask_b_ready, 1)

            dve.wait_ge(consts, 11)
            residual(0)
            residual(1)
            norm2_ms(0)
            norm2_rows(0)
            residual(2)
            residual(3)
            h2T_copy(0)
            norm2_ms(1)
            norm2_rows(1)
            route(0)
            h2T_copy(1)
            route(1)
            dve.wait_ge(rank_done, 1)
            step(dve.scalar_tensor_tensor(out=rank[:], in0=ps[:, GLU, 0:NT * EXPERTS].rearrange("p (i e) -> p i e", i=NT),
                                          scalar=1.0, in1=mask, op0=ALU.add, op1=ALU.mult))
            step(dve.tensor_scalar(rank[:], rank[:], -1.0, None, ALU.add))

            def build_onehot(sems, e, lo):
                for i in range(NT):
                    ins = dve.tensor_scalar(onehot[:, i, :], iota[:, lo], rank[:, i, bass.ds(e, 1)], None, ALU.is_equal)
                ins.then_inc(sems[0], 1)

            def build_scatter(sems, e, lo):
                for i in range(NT):
                    ins = dve.tensor_scalar(sg[:, i], iota[:, lo].unsqueeze(1).broadcast_to([P, 2, SLOTS]),
                                            rank[:, i, bass.ds(e, 1)], gate[:, i, bass.ds(e, 1)], ALU.is_equal, ALU.mult)
                ins.then_inc(sems[1], 1)

            def pick_expert(e):
                dve.tensor_copy(pick_e[0:96, :], pick[:, bass.ds(e, 1)].broadcast_to([96, SLOTS])).then_inc(pick_ready, 1)

            def swiglu(sems, v):
                dve.wait_ge(sems[4], v)
                dve.tensor_scalar(glu, ps[:, GLU, :], LIMIT, None, ALU.min).then_inc(sems[5], 1)
                dve.tensor_scalar(lin, ps[:, LIN, :], LIMIT, -LIMIT, ALU.min, ALU.max).then_inc(sems[6], 1)
                dve.wait_ge(sems[5], v)
                dve.wait_ge(sems[6], v)
                dve.scalar_tensor_tensor(out=lin, in0=lin, scalar=1.0, in1=glu, op0=ALU.add, op1=ALU.mult)\
                   .then_inc(sems[7], 1)
                dve.wait_ge(sems[7], v)
                dve.wait_ge(sems[8], v)
                dve.tensor_tensor(act_v, lin, sig, ALU.mult).then_inc(sems[9], 1)

            def evacuate_y(sems, bank, dst, v):
                dve.wait_ge(sems[13], v)
                dve.tensor_copy(dst, ps[:, bank, :]).then_inc(sems[14], 1)

            first_places = slice(0, SLOTS)
            build_onehot(main_sems, 0, first_places)
            step(dve.tensor_copy(counts[:], ps[0:1, GLU, NT * EXPERTS:(NT + 1) * EXPERTS]))
            pick_expert(0)
            dve.wait_ge(pick_ready, 1)
            dve.nop().then_inc(routed, 1)
            dve.wait_ge(top_exp, NT)
            step(dve.reciprocal(rt[:, 26:28], rt[:, 26:28]))
            for i in range(NT):
                step(dve.tensor_scalar(rt[:, 16 + 4 * i:20 + 4 * i], rt[:, 16 + 4 * i:20 + 4 * i], rt[:, 26 + i:27 + i],
                                       None, ALU.mult))
                step(dve.tensor_tensor(hit_g[:, i], hit[:, i],
                                       rt[:, 16 + 4 * i:20 + 4 * i].unsqueeze(2).broadcast_to([P, ROUTE, EXPERTS]),
                                       ALU.mult))
                dve.tensor_reduce(gate[:, i, :], hit_g[:, i].rearrange("p k e -> p e k"), AX_X, ALU.add)\
                   .then_inc(gates_ready, 1)
            dve.wait_ge(gates_ready, 2)
            more = dve.alloc_register("dve_more")
            dve.reg_mov(more, 0)

            def expert(first, group):
                e = dve.snap(first + 3 * group)
                count = dve.value_load(counts[0:1, bass.ds(e, 1)])

                def buffers_free():
                    dve.wait_ge(gathered, e + 1)
                    if first:
                        dve.wait_ge(act_T, e)

                with dve.If(count > SLOTS):
                    with dve.Fori(1, T // SLOTS) as p:
                        with dve.If(count > p * SLOTS):
                            v = dve.snap(more) + 1
                            lo = bass.ds(p * SLOTS, SLOTS)
                            buffers_free()
                            build_onehot(more_sems, e, lo)
                            build_scatter(more_sems, e, lo)
                            swiglu(more_sems, v)
                            evacuate_y(more_sems, AUX, y_o, v)
                            dve.reg_add(more, more, 1)
                buffers_free()
                if first < EXPERTS - 1:
                    build_onehot(main_sems, e + 1, first_places)
                build_scatter(main_sems, e, first_places)
                swiglu(main_sems, e + 1)
                if first < EXPERTS - 1:
                    pick_expert(e + 1)
                if not first:
                    dve.wait_ge(gate_T, 1)
                    dve.tensor_copy(gT, ps[0:EXPERTS, YB, 0:T]).then_inc(gT_ready, 1)
                evacuate_y(main_sems, YB, y, e + 1)

            turns(dve, expert)
            dve.wait_ge(acc_done, 1)
            for i in range(NT):
                for half in range(2):
                    cols = slice(half * BANK, (half + 1) * BANK)
                    step(dve.tensor_tensor(prod[:], ps[:, 2 * i + half, :], g2_row[:, cols], ALU.mult))
                    ins = dve.tensor_tensor(xs[:, i, cols], xs[:, i, cols], prod[:], ALU.add)
                    if half == 0:
                        step(ins)
                ins.then_inc(fin_ready, 1)
                dve.wait_ge(fin_ready, i + 1)

        @block.tensor
        def _(pe):
            def wait_bank(j):
                if j >= 2:
                    pe.wait_ge(bank_read[j % 2], j // 2)

            def feature_job(name, cols, item, src=hT, kc=KC, m=BANK):
                j = JOB[name]
                wait_bank(j)
                wait_landed(pe, item)
                w = slot(item)[:, 0:kc * m].rearrange("p (k m) -> p k m", m=m)
                for n, at in enumerate(cols):
                    for k in range(kc):
                        ins = pe.matmul(ps[:, 4 + j % 2, n * T:(n + 1) * T], w[:, k, at:at + P], src[:, k, :],
                                        start=(k == 0), stop=(k == kc - 1))
                return ins

            def finish(ins):
                ins.then_inc(job_done, 1)

            pe.wait_ge(consts, 7)
            pe.wait_ge(rows_in, 64)
            pe.transpose(ps[:, 7, 0:28], rows, ident[0:28, 0:28]).then_inc(rows_T, 1)
            pe.wait_ge(xn_ready, 2)
            for k in range(KC):
                for i in range(NT):
                    ins = pe.transpose(ps[:, k // 2, (k % 2) * T + i * P:(k % 2) * T + (i + 1) * P],
                                       xn[:, i, k * P:(k + 1) * P], ident[:])
            ins.then_inc(xT_done, 1)
            pe.wait_ge(rows_out, 1)
            for p in range(2):
                pe.wait_ge(ada_steps, 2 * KC * (p + 1))
                for k in range(KC):
                    o = ps[:, 7, 32 + 8 * p + k:33 + 8 * p + k]
                    b = 2 * p + k // 4
                    pe.matmul(o, modacc[:, p, k * P:(k + 1) * P], ones[:, 0:1], start=True, stop=False)
                    ins = pe.matmul(o, ada_bias[:, (k % 4) * P:(k % 4 + 1) * P], ident[32:44, 32 + b:33 + b],
                                    start=False, stop=True)
                ins.then_inc(mod_summed, 1)
            pe.wait_ge(hT_dve, 4)
            pe.wait_ge(hT_act, 4)

            used = [0]
            block_last = {"kiwi": ("in", "idx"), "q1": ("in", "q"), "k1": ("in", "k"), "v1": ("in", "v"),
                          "xin1": ("in", "xin"), "gc1": ("in", "gc"), "gb1": ("in", "gb"), "ga1": ("in", "ga0"),
                          "ga3": ("in", "ga1"), "gB1": ("in", "gB0"), "gB3": ("in", "gB1"), "pa3": ("conv_out", 0),
                          "pb3": ("attn_out", 0)}

            def release(name):
                if name in block_last:
                    assert PE_ITEMS[used[0]] == block_last[name]
                    used[0] += 1
                    pe.wait_ge(job_done, JOB[name] + 1)
                    pe.nop().then_inc(w_used, 1)

            def job(name):
                j = JOB[name]
                bank = ps[:, 4 + j % 2, :]
                n = int(name[-1]) if name[-1].isdigit() else 0
                if name == "qi":
                    finish(feature_job(name, (0, P), item=("in", "idx"), m=GA - QI))
                elif name == "kiwi":
                    wait_bank(j)
                    w = slot(("in", "idx"))[:, 0:KC * (GA - QI)].rearrange("p (k m) -> p k m", m=GA - QI)
                    for half in range(2):
                        for k in range(KC):
                            pe.matmul(bank[64 * half:64 * half + 64, 0:T], w[:, k, KI - QI:KI - QI + 64], hT[:, k, :],
                                      start=(k == 0), stop=(k == KC - 1), skip_group_check=True)
                    for i in range(NT):
                        for k in range(KC):
                            ins = pe.matmul(bank[:, T + 4 * i:T + 4 * i + 4], hT[:, k, i * P:(i + 1) * P],
                                            w[:, k, WI - QI:WI - QI + 4], start=(k == 0), stop=(k == KC - 1),
                                            skip_group_check=True)
                    finish(ins)
                elif name[0] in "qkv":
                    item = ("in", name[0])
                    wait_bank(j)
                    wait_landed(pe, item)
                    w = slot(item).rearrange("p (k m) -> p k m", m=BANK)
                    for k in range(KC):
                        ins = pe.matmul(bank, hT[:, k, n * P:(n + 1) * P], w[:, k, :], start=(k == 0), stop=(k == KC - 1))
                    finish(ins)
                elif name[:-1] in ("xin", "gc", "gb"):
                    finish(feature_job(name, (2 * n * P, (2 * n + 1) * P), item=("in", name[:-1])))
                elif name[:-1] in ("ga", "gB"):
                    m = n % 2
                    finish(feature_job(name, (2 * m * P, (2 * m + 1) * P), item=("in", f"{name[:-1]}{n // 2}")))
                elif name[:3] == "mod":
                    b = int(name[3:])
                    wait_bank(j)
                    pe.wait_ge(ada_steps, KC * (b + 1))
                    pe.matmul(bank, ones[:], modacc[:, (b // 2) % 2, (b % 2) * BANK:(b % 2 + 1) * BANK],
                              start=True, stop=False)
                    ins = pe.matmul(bank, ident[32:44, 32 + b:33 + b].broadcast_to([12, P]), ada_bias,
                                    start=False, stop=True)
                    finish(ins)
                    if b % 2:
                        pe.wait_ge(job_done, j + 1)
                        pe.nop().then_inc(mod_summed, 1)
                elif name[:2] in ("pa", "pb"):
                    if name == "pa0":
                        pe.wait_ge(bank_read[0], JOB["gb0"] // 2 + 1)
                        pe.wait_ge(bank_read[1], JOB["gb1"] // 2 + 1)
                    if name == "pb0":
                        pe.wait_ge(yB_ready, UNITS)
                    finish(feature_job(name, (2 * n * P, (2 * n + 1) * P), src=yA if name[1] == "a" else yB, kc=4,
                                       item=("conv_out", 0) if name[1] == "a" else ("attn_out", 0), m=D))
                else:
                    i, half = n // 2, n % 2
                    wait_bank(j)
                    if n == 0:
                        pe.wait_ge(merged, 4)
                        wait_landed(pe, ("w_o", 0))
                        wait_landed(pe, ("w_o", 1))
                    for k in range(KC):
                        w = slot(("w_o", k // 4)).rearrange("p (k m) -> p k m", m=D)
                        ins = pe.matmul(bank, mT[:, k, i * P:(i + 1) * P], w[:, k % 4, half * BANK:(half + 1) * BANK],
                                        start=(k == 0), stop=(k == KC - 1))
                    finish(ins)
                release(name)

            job("qi")
            job("kiwi")
            pe.wait_ge(bank_read[0], 1)
            pe.wait_ge(bank_read[1], 1)
            for i in range(NT):
                w = P * (i + 1)
                for h in range(IDX_HEADS):
                    half = slice(64 * (h % 2), 64 * (h % 2) + 64)
                    ins = pe.matmul(ps[:, 2 * i + h % 2, (h // 2) * T:(h // 2) * T + w], qiT[half, h // 2, i * P:(i + 1) * P],
                                    kiT[half, 0:w], start=True, stop=True, skip_group_check=True)
                ins.then_inc(dots_done, 1)
            for name in ("q0", "q1", "k0", "k1", "v0", "v1"):
                job(name)
            pe.wait_ge(relu_done, 4)
            for n, src in enumerate((q_tok, q_tok, k_tok, k_tok)):
                pe.wait_ge(qk_normed, n + 1)
                for hp in range(4):
                    ins = pe.transpose(ps[:, n, hp * P:(hp + 1) * P], src[:, n % 2, hp * P:(hp + 1) * P], ident[:])
                ins.then_inc(qk_T, 1)

            def logits(u):
                i, hp, w, b = u // 4, u % 4, P * (u // 4 + 1), u % 2
                if u == 0:
                    pe.wait_ge(qkT_ready, 4)
                    pe.wait_ge(mask_ready, 2)
                if u >= 2:
                    pe.wait_ge(logits_read, u - 1)
                for h in range(2):
                    half = slice(64 * h, 64 * h + 64)
                    ins = pe.matmul(ps[:, 2 * b + h, 0:w], qT[half, hp, i * P:(i + 1) * P], kT[half, hp, 0:w],
                                    start=True, stop=True)
                ins.then_inc(logits_done, 1)

            def probs_transpose(u):
                n = u // 4 + 1
                pe.wait_ge(probs_ready, u + 1)
                if u >= 1:
                    pe.wait_ge(pT_ready, u)
                for h in range(2):
                    for s in range(n):
                        ins = pe.transpose(ps[:, 6, (2 * h + s) * P:(2 * h + s + 1) * P],
                                           lg[:, u % 2, h, s * P:(s + 1) * P], ident[:])
                ins.then_inc(probs_T, 1)

            def values(u):
                n, hp = u // 4 + 1, u % 4
                pe.wait_ge(pT_ready, u + 1)
                if u >= 1:
                    pe.wait_ge(yB_ready, u)
                if u == 0:
                    pe.wait_ge(bank_read[1], JOB["v1"] // 2 + 1)
                for h in range(2):
                    for s in range(n):
                        head = 2 * hp + h
                        ins = pe.matmul(ps[64 * h:64 * h + 64, 7, (u % 2) * P:(u % 2) * P + P],
                                        v_tok[:, s, head * HD:(head + 1) * HD], pT[:, u % 2, h, s, :],
                                        start=(s == 0), stop=(s == n - 1), skip_group_check=True)
                ins.then_inc(pv_done, 1)

            for name in JOBS[FIRST_UNIT_JOB:JOB["wo3"]]:
                job(name)
                k = JOB[name] - FIRST_UNIT_JOB
                if k >= 2 and k % 2 == 0 and k // 2 - 1 < UNITS:
                    values(k // 2 - 1)
                if k % 2 == 1 and k // 2 < UNITS:
                    probs_transpose(k // 2)
                if k % 2 == 0 and k // 2 < UNITS:
                    logits(k // 2)

            def turn_h2(i):
                pe.wait_ge(h2_ready, i + 1)
                for k in range(KC):
                    ins = pe.transpose(ps[:, 2 * i + k // 4, (k % 4) * P:(k % 4 + 1) * P],
                                       h2[:, i, k * P:(k + 1) * P], ident[:])
                ins.then_inc(h2_T, 1)

            def router(i):
                pe.wait_ge(h2T_dve, i + 1)
                pe.wait_ge(h2T_act, i + 1)
                o = ps[:, AUX + i, 0:EXPERTS]
                for k in range(KC):
                    pe.matmul(o, h2T[:, i, k, :], wr[:, k, :], start=(k == 0), stop=False)
                pe.matmul(o, ones[0:1, :], br[:], start=False, stop=True).then_inc(router_done, 1)

            turn_h2(0)
            job("wo3")
            pe.wait_ge(job_done, len(JOBS))
            pe.nop().then_inc(w_used, 2)
            pe.wait_ge(small_in, 48)
            router(0)
            turn_h2(1)
            router(1)
            pe.wait_ge(consts, 11)
            for i in range(NT):
                for half in range(2):
                    pe.matmul(ps[:, 2 * i + half, :], zeros_b[:], ones_b[0:1, 0:1].broadcast_to([1, BANK]), start=True,
                              stop=False, skip_group_check=True)
            pe.wait_ge(mask_b_ready, 2)
            pe.matmul(ps[:, GLU, 0:32], before[:], m_b[:, 0, :], start=True, stop=True)
            pe.matmul(ps[:, GLU, 32:64], ones_b[:], m_b[:, 0, :], start=True, stop=False)
            pe.matmul(ps[:, GLU, 32:64], before[:], m_b[:, 1, :], start=False, stop=True)
            pe.matmul(ps[:, GLU, 64:96], ones_b[:], m_b[:, 0, :], start=True, stop=False)
            pe.matmul(ps[:, GLU, 64:96], ones_b[:], m_b[:, 1, :], start=False, stop=True).then_inc(rank_done, 1)

            def turn_gates():
                pe.wait_ge(gates_ready, 2)
                for i in range(NT):
                    ins = pe.transpose(ps[0:EXPERTS, YB, i * P:(i + 1) * P], gate[:, i, :], ident[:])
                ins.then_inc(gate_T, 1)

            def down_biases():
                pe.wait_ge(gT_ready, 1)
                pe.wait_ge(down_bias_in, 16)
                for i in range(NT):
                    for half in range(2):
                        pe.matmul(ps[:, 2 * i + half, :], gT[:, i * P:(i + 1) * P], bd[:, half * BANK:(half + 1) * BANK],
                                  start=False, stop=False, skip_group_check=True)

            def gather(sems, v):
                pe.wait_ge(sems[0], v)
                for k in range(KC):
                    n = 0
                    for h in part:
                        for i in range(NT):
                            ins = pe.matmul(ps[:, AUX, k * SLOTS:(k + 1) * SLOTS], h[:, i, k * P:(k + 1) * P],
                                            onehot[:, i, :], start=(n == 0), stop=(n == 5))
                            n += 1
                ins.then_inc(sems[2], 1)

            def wait_sixth(first, group, q):
                n = 6 * first + q
                pe.wait_ge(landed[n % RING], 16 * (FRONT_USES[n % RING] + n // RING + 1) + 32 * group)
                return ring[:, n % RING, :]

            def gate_up(sems, src, first, group, main):
                for j in range(2):
                    for bank, at in ((GLU, 0), (LIN, FF)):
                        pe.matmul(ps[64 * j:64 * j + 64, bank, :], pick_e[0:96, :],
                                  bias3[:, at + j * BANK:at + (j + 1) * BANK], start=True, stop=False,
                                  skip_group_check=True)
                for k in range(KC):
                    w = wait_sixth(first, group, k // 2) if k % 2 == 0 else w
                    for bank, at in ((GLU, 0), (LIN, FF)):
                        for j in range(2):
                            o = (k % 2) * 2 * FF + at + j * BANK
                            ins = pe.matmul(ps[64 * j:64 * j + 64, bank, :], src[:, k * SLOTS:(k + 1) * SLOTS],
                                            w[:, o:o + BANK], start=False, stop=(k == KC - 1), skip_group_check=True)
                    if main and k % 2 and k < KC - 1:
                        ins.then_inc(w_used, 1)
                ins.then_inc(sems[4], 1)

            def turn_act(sems, v):
                pe.wait_ge(sems[9], v)
                for k in range(4):
                    pe.transpose(ps[:, GLU, k * P:(k + 1) * P], act_v[:, k * P:(k + 1) * P], ident[:])
                pe.wait_ge(sems[1], v)
                for i in range(NT):
                    ins = pe.transpose(ps[:, LIN, i * P:(i + 1) * P], sg[:, i].rearrange("p j s -> p (j s)"), ident[:])
                ins.then_inc(sems[10], 1)

            def down(sems, bank, first, group, main, v):
                pe.wait_ge(sems[11], v)
                for half in range(2):
                    w = wait_sixth(first, group, 4 + half).rearrange("p (k m) -> p k m", m=D)
                    for k in range(4):
                        for j in range(2):
                            ins = pe.matmul(ps[64 * j:64 * j + 64, bank, :],
                                            actT[:, k * P + half * SLOTS:k * P + (half + 1) * SLOTS],
                                            w[:, k, j * BANK:(j + 1) * BANK], start=(half == 0 and k == 0),
                                            stop=(half == 1 and k == 3), skip_group_check=True)
                    if main and half == 0:
                        ins.then_inc(w_used, 1)
                ins.then_inc(sems[13], 1)

            def scatter(sems, src, rows_t, v, last=False):
                pe.wait_ge(sems[14], v)
                pe.wait_ge(sems[12], v)
                for i in range(NT):
                    for j in range(2):
                        ins = pe.matmul(ps[:, 2 * i + j, :], rows_t[64 * j:64 * j + 64, i * P:(i + 1) * P],
                                        src[64 * j:64 * j + 64, :], start=False, stop=last, skip_group_check=True)
                return ins

            pe.wait_ge(parts_ready, 2)
            gather(main_sems, 1)
            pe.wait_ge(routed, 1)
            pe.wait_ge(bias_steps, 9)
            more = pe.alloc_register("pe_more")
            pe.reg_mov(more, 0)

            def expert(first, group):
                e = pe.snap(first + 3 * group)
                count = pe.value_load(counts[0:1, bass.ds(e, 1)])

                def operands_ready():
                    pe.wait_ge(pick_ready, e + 1)
                    pe.wait_ge(xg_ready, e + 1)
                    if first:
                        pe.wait_ge(sgT_ready, e)

                with pe.If(count > SLOTS):
                    with pe.Fori(1, T // SLOTS) as p:
                        with pe.If(count > p * SLOTS):
                            v = pe.snap(more) + 1
                            operands_ready()
                            gather(more_sems, v)
                            pe.wait_ge(more_sems[3], v)
                            gate_up(more_sems, xg_o, first, group, False)
                            turn_act(more_sems, v)
                            down(more_sems, AUX, first, group, False, v)
                            scatter(more_sems, y_o, sgT_o, v)
                            pe.reg_add(more, more, 1)
                operands_ready()
                gate_up(main_sems, xg, first, group, True)
                if first < EXPERTS - 1:
                    gather(main_sems, e + 2)
                if first:
                    scatter(main_sems, y, sgT, e)
                else:
                    turn_gates()
                turn_act(main_sems, e + 1)
                pe.nop().then_inc(w_used, 1)
                if not first:
                    down_biases()
                down(main_sems, YB, first, group, True, e + 1)
                pe.wait_ge(down_done, e + 1)
                pe.nop().then_inc(w_used, 1)

            turns(pe, expert)
            scatter(main_sems, y, sgT, EXPERTS, last=True).then_inc(acc_done, 1)


_INS = ['x', 'c', 'w_ada', 'b_ada', 'norm1_g', 'w_in', 'conv_w', 'q_norm_g', 'k_norm_g', 'w_conv_out', 'w_attn_out',
        'w_o', 'norm2_g', 'w_router', 'b_router', 'w_gate_up', 'b_gate_up', 'w_down', 'b_down']


def kernel(**inputs):
    import numpy as _np
    import concourse.bacc as _bacc
    from concourse import mybir as _mybir
    from concourse.bass_utils import run_bass_kernel_spmd as _run

    nc = _bacc.Bacc("TRN2", target_bir_lowering=False, num_devices=1)
    arrays, args = {}, []
    for name in _INS:
        a = _np.ascontiguousarray(inputs[name])
        arrays[f"in_{name}"] = a
        args.append(nc.dram_tensor(f"in_{name}", a.shape, _mybir.dt.from_np(a.dtype), kind="ExternalInput").ap())
    args.append(nc.dram_tensor("out_0", (1, T, D), F32, kind="ExternalOutput").ap())
    hybrid_block(nc, *args)
    r = _run(nc, [arrays], core_ids=[0])
    return r.results[0]["out_0"]
```

```python
from contextlib import ExitStack

import concourse.bass as bass
from concourse import mybir

F32 = mybir.dt.float32
BF16 = mybir.dt.bfloat16
I32 = mybir.dt.int32
U32 = mybir.dt.uint32
ALU = mybir.AluOpType
ACT = mybir.ActivationFunctionType
AX_X = mybir.AxisListType.X

P = 128
D = 1024
T = 256
NT = T // P
KC = D // P
CONV = 512
HEADS = 8
HD = 64
IDX_HEADS = 4
IDX_SCALE = (IDX_HEADS * 64) ** -0.5
CHUNK = 64
TOPK = 64
EXPERTS = 32
ROUTE = 4
FF = 1024
SLOTS = 64
LIMIT = 7.0
ALPHA = 1.702
EPS = 1e-6
NEG = -3.0e38
TAKEN = -3.3e38
UNSEEN = -1.0e30

BANK = 512
RING = 9
FRONT_RING = 6
SLOT = 4096
XIN, GB, GC, Q, K, V, QI, KI, WI, GA, GBR = 0, 512, 1024, 1536, 2048, 2560, 3072, 3328, 3392, 3396, 4420
IN_BLOCK = {"xin": (XIN, 512), "gb": (GB, 512), "gc": (GC, 512), "q": (Q, 512), "k": (K, 512), "v": (V, 512),
            "idx": (QI, GA - QI), "ga0": (GA, 512), "ga1": (GA + 512, 512), "gB0": (GBR, 512), "gB1": (GBR + 512, 512)}
ADA = [("ada", b) for b in range(12)]
STREAM = (ADA[0:4] + [("in", n) for n in ("idx", "q", "k", "v", "xin")]
          + [ADA[4], ("in", "gc"), ADA[5], ("in", "gb"), ADA[6], ("in", "ga0"), ADA[7], ("in", "ga1"),
             ADA[8], ("in", "gB0"), ADA[9], ("in", "gB1"), ADA[10], ("conv_out", 0), ADA[11], ("attn_out", 0),
             ("w_o", 0), ("w_o", 1)])
EARLY_K = 6
ADA_HALF = ["xin0", "xin1", "gc0", "gc1", "gb0", "gb1", "ga0", "ga1", "ga2", "ga3", "gB0", "gB1", "gB2", "gB3"]
ITEM = {item: i for i, item in enumerate(STREAM)}
PE_ITEMS = [item for item in STREAM if item[0] != "ada"]
FRONT_PE = len(PE_ITEMS)
FRONT_USES = [len([i for i in range(len(STREAM)) if i % FRONT_RING == s]) for s in range(FRONT_RING)] \
    + [0] * (RING - FRONT_RING)

JOBS = (["qi", "kiwi", "q0", "q1", "k0", "k1", "v0", "v1", "xin0", "xin1", "gc0", "gc1", "gb0", "gb1", "mod4", "ga0",
         "mod5", "ga1", "ga2", "ga3", "mod6", "gB0", "mod7", "gB1", "gB2", "gB3", "mod8", "mod9"]
        + [f"pa{n}" for n in range(4)] + ["pb0", "mod10", "mod11", "pb1", "pb2", "pb3"] + [f"wo{n}" for n in range(4)])
JOB = {name: i for i, name in enumerate(JOBS)}
EXPERT_SLOT = len(STREAM) % FRONT_RING
UNITS = 2 * 4
FIRST_UNIT_JOB = JOB["xin0"]


def ada_steps_of(b):
    return EARLY_K * (b + 1) if b < 4 else EARLY_K * 4 + KC * (b - 3)


def hybrid_block(nc, x, c, w_ada, b_ada, norm1_g, w_in, conv_w, q_norm_g, k_norm_g, w_conv_out, w_attn_out, w_o,
                 norm2_g, w_router, b_router, w_gate_up, b_gate_up, w_down, b_down, out):
    with ExitStack() as ctx:
        def sb(name, shape, dt=F32):
            return ctx.enter_context(nc.sbuf_tensor(name, shape, dt))

        def sem(name):
            return ctx.enter_context(nc.semaphore(name))

        ps = ctx.enter_context(nc.psum_tensor("ps", [P, 8, BANK], F32))

        ring = sb("ring", [P, RING, SLOT])
        xs = sb("xs", [P, NT, D])
        modacc = sb("modacc", [P, 2, D])
        featT = sb("featT", [P, 2048])
        work = sb("work", [P, 4096])
        g1_row = sb("g1_row", [P, D])
        a2_row = sb("a2_row", [P, D])
        sh2_row = sb("sh2_row", [P, D])
        g2_row = sb("g2_row", [P, D])
        prod = sb("prod", [P, BANK])
        iota = sb("iota", [P, T])
        ident = sb("ident", [P, P])
        ones = sb("ones", [P, P])
        before = sb("before", [P, P], BF16)
        ones_b = sb("ones_b", [P, P], BF16)
        zeros_b = sb("zeros_b", [1, P], BF16)
        pick = sb("pick", [96, EXPERTS])
        small = sb("small", [P, 32])
        wr = sb("wr", [P, KC, EXPERTS])
        br = sb("br", [1, EXPERTS])
        vec = sb("vec", [P, 64])
        rank = sb("rank", [P, NT, EXPERTS])
        gate = sb("gate", [P, NT, EXPERTS])
        counts = sb("counts", [1, EXPERTS], I32)

        ov = ring[:, FRONT_RING:RING, :].rearrange("p s n -> p (s n)")
        xn = ov[:, 0:2048].rearrange("p (i n) -> p i n", i=NT)
        sgA = ov[:, 0:2048].rearrange("p (d t) -> p d t", t=T)
        sgB = ov[:, 2048:4096].rearrange("p (d t) -> p d t", t=T)
        q_tok = ov[:, 4096:5120].rearrange("p (i n) -> p i n", i=NT)
        k_tok = ov[:, 5120:6144].rearrange("p (i n) -> p i n", i=NT)
        v_tok = ov[:, 6144:7168].rearrange("p (i n) -> p i n", i=NT)
        yA = ov[:, 4096:5120].rearrange("p (c t) -> p c t", t=T)
        qT = ov[:, 7168:8192].rearrange("p (c t) -> p c t", t=T)
        kT = ov[:, 8192:9216].rearrange("p (c t) -> p c t", t=T)
        qiT = ov[:, 9216:9728].rearrange("p (c t) -> p c t", t=T)
        kiT = ov[:, 9728:9984]
        gains = ov[:, 9984:10112].rearrange("p (a d) -> p a d", a=2)
        xinS = ov[:, 10112:11136].rearrange("p (c t) -> p c t", t=T)
        conv_u = ov[:, 11136:12168].rearrange("p (c t) -> p c t", t=T + 2)

        rows = prod[0:28, 0:P]
        ada_bias = prod[32:44, :]
        hT = featT[:, :].rearrange("p (c t) -> p c t", t=T)
        mT = hT
        h2T = featT[:, :].rearrange("p (i k t) -> p i k t", i=NT, k=KC)
        relu = work[:, 0:1024].rearrange("p (b h t) -> p b h t", b=2, h=2)
        yB = work[:, 0:1024].rearrange("p (c t) -> p c t", t=T)
        score = work[:, 1024:1536].rearrange("p (i s) -> p i s", i=NT)
        am = work[:, 1536:2048].rearrange("p (i s) -> p i s", i=NT)
        sq = work[:, 2048:2560]
        lg = work[:, 2048:3072].rearrange("p (b h s) -> p b h s", b=2, h=2)
        pT = work[:, 3072:4096].rearrange("p (b h s t) -> p b h s t", b=2, h=2, s=2)
        h2 = work[:, 0:2048].rearrange("p (i n) -> p i n", i=NT)
        bd = work[0:EXPERTS, 2048:3072]
        bias3 = work[0:96, 3072:4096].bitcast(BF16)
        bias_raw = ov[0:96, 0:2048]
        bias_parts = g2_row[0:96, :].bitcast(BF16)
        ada_rows = work[0:1, 0:2048].rearrange("p (b n) -> p b n", b=4)
        part = [modacc[:, 0, :].bitcast(BF16).rearrange("p (i n) -> p i n", i=NT),
                modacc[:, 1, :].bitcast(BF16).rearrange("p (i n) -> p i n", i=NT),
                g1_row[:, :].bitcast(BF16).rearrange("p (i n) -> p i n", i=NT)]
        gT = prod[0:EXPERTS, 0:T]

        xg = featT[:, 0:512]
        xg_o = featT[:, 512:1024]
        glu = featT[:, 1024:1536]
        sig = featT[:, 1536:2048]
        lin = work[:, 0:512]
        act_v = work[:, 512:1024]
        actT = work[:, 1024:1536]
        y = work[:, 1536:2048]
        y_o = sh2_row[:, 0:512]
        sgT = sh2_row[:, 512:768]
        sgT_o = sh2_row[:, 768:1024]
        sg = a2_row[:, 0:256].rearrange("p (i j s) -> p i j s", i=NT, j=2)
        pick_e = a2_row[:, 256:288].bitcast(BF16)
        onehot = a2_row[:, 288:352].bitcast(BF16).rearrange("p (i s) -> p i s", i=NT)

        silu_c = vec[:, 0:8]
        sig_c = vec[:, 8:16]
        a1 = vec[:, 16:24]
        sh1 = vec[:, 24:32]
        wi = vec[:, 32:40].rearrange("p (i h) -> p i h", i=NT)
        ms = vec[:, 40:42]
        rstd = vec[:, 42:44]
        neg_max = vec[:, 44:48].rearrange("p (b h) -> p b h", b=2)
        row_sum = vec[:, 48:52].rearrange("p (b h) -> p b h", b=2)
        top8 = vec[:, 52:60]
        hs = sb("hs", [P, 32])
        rt = sb("rt", [P, 64])
        lr = sb("lr", [P, NT, EXPERTS])
        idx8 = sb("idx8", [P, NT, 8], U32)
        m_b = sb("m_b", [P, NT, EXPERTS], BF16)
        hit = prod[:, 0:256].rearrange("p (i k e) -> p i k e", i=NT, k=ROUTE)
        hit_g = prod[:, 0:256].rearrange("p (i k e) -> p i k e", i=NT, k=ROUTE)
        mask = prod[:, 256:320].rearrange("p (i e) -> p i e", i=NT)

        landed = [sem(f"landed{s}") for s in range(RING)]
        w_used = sem("w_used")
        ada_steps = sem("ada_steps")
        ada_row_done = sem("ada_row_done")
        ada_row_out = sem("ada_row_out")
        bias_moved = sem("bias_moved")
        x_in = sem("x_in")
        rows_in = sem("rows_in")
        small_in = sem("small_in")
        gains_in = sem("gains_in")
        down_bias_in = sem("down_bias_in")
        gu_bias_in = sem("gu_bias_in")
        bias_steps = sem("bias_steps")
        consts = sem("consts")
        dve_step = sem("dve_step")
        act_step = sem("act_step")
        rows_T = sem("rows_T")
        rows_out = sem("rows_out")
        sig_c_done = sem("sig_c_done")
        silu_done = sem("silu_done")
        sumsq1 = sem("sumsq1")
        ms1_done = sem("ms1_done")
        std1_done = sem("std1_done")
        rstd1_ready = sem("rstd1_ready")
        xn_ready = sem("xn_ready")
        xT_done = sem("xT_done")
        mod_summed = sem("mod_summed")
        mod1_ready = sem("mod1_ready")
        hT_dve = sem("hT_dve")
        hT_act = sem("hT_act")
        job_done = sem("job_done")
        bank_read = [sem(f"bank_read{b}") for b in range(2)]
        dots_done = sem("dots_done")
        relu_done = sem("relu_done")
        score_done = sem("score_done")
        mask_ready = sem("mask_ready")
        head_ms = sem("head_ms")
        head_std = sem("head_std")
        qk_normed = sem("qk_normed")
        qk_T = sem("qk_T")
        qkT_ready = sem("qkT_ready")
        logits_done = sem("logits_done")
        logits_read = sem("logits_read")
        max_ready = sem("max_ready")
        exp_done = sem("exp_done")
        probs_ready = sem("probs_ready")
        probs_T = sem("probs_T")
        pT_ready = sem("pT_ready")
        pv_done = sem("pv_done")
        yB_ready = sem("yB_ready")
        yA_ready = sem("yA_ready")
        merged = sem("merged")
        x1_ready = sem("x1_ready")
        sumsq2 = sem("sumsq2")
        ms2_done = sem("ms2_done")
        std2_done = sem("std2_done")
        h2_ready = sem("h2_ready")
        h2_T = sem("h2_T")
        h2T_dve = sem("h2T_dve")
        h2T_act = sem("h2T_act")
        part0 = sem("part0")
        rest0 = sem("rest0")
        part1 = sem("part1")
        parts_ready = sem("parts_ready")
        router_done = sem("router_done")
        top_ready = sem("top_ready")
        top_exp = sem("top_exp")
        mask_b_ready = sem("mask_b_ready")
        gates_ready = sem("gates_ready")
        rank_done = sem("rank_done")
        gate_T = sem("gate_T")
        gT_ready = sem("gT_ready")
        routed = sem("routed")

        onehot_ready = sem("onehot_ready")
        sg_ready = sem("sg_ready")
        pick_ready = sem("pick_ready")
        gathered = sem("gathered")
        xg_ready = sem("xg_ready")
        glu_ready = sem("glu_ready")
        lin_ready = sem("lin_ready")
        prod_ready = sem("prod_ready")
        sig_ready = sem("sig_ready")
        act_ready = sem("act_ready")
        act_T = sem("act_T")
        sg_T = sem("sg_T")
        actT_ready = sem("actT_ready")
        sgT_ready = sem("sgT_ready")
        y_ready = sem("y_ready")
        main_sems = {"onehot_ready": onehot_ready, "sg_ready": sg_ready, "gathered": gathered, "xg_ready": xg_ready,
                     "glu_ready": glu_ready, "lin_ready": lin_ready, "prod_ready": prod_ready, "sig_ready": sig_ready,
                     "act_ready": act_ready, "act_T": act_T, "actT_ready": actT_ready, "sgT_ready": sgT_ready,
                     "y_ready": y_ready, "sg_T": sg_T}
        more_sems = {name: sem("more_" + name) for name in main_sems}
        more_gu_done = sem("more_gu_done")
        more_down_done = sem("more_down_done")
        acc_done = sem("acc_done")
        fin_ready = sem("fin_ready")
        out_done = sem("out_done")

        GLU, LIN, AUX, YB = 4, 5, 6, 7
        MORE_PASSES = range(1, T // SLOTS)

        def slot(item):
            return ring[:, ITEM[item] % FRONT_RING, :]

        def wait_landed(eng, item):
            i = ITEM[item]
            eng.wait_ge(landed[i % FRONT_RING], 16 * (i // FRONT_RING + 1))

        def sixths_used(e, n):
            return e * 6 + (FRONT_PE + n)

        def turns(eng, body):
            body(0, 0)
            with eng.Fori(0, (EXPERTS - 2) // 3) as group:
                for j in range(3):
                    body(1 + j, group)
            body(EXPERTS - 1, 0)

        block = ctx.enter_context(nc.Block())

        @block.sync
        def _(sp):
            sp.dma_start(rows[0:8, :], c.rearrange("b (k p) -> (b k) p", p=P)).then_inc(rows_in, 16)
            sp.dma_start(rows[8:16, :], norm1_g.rearrange("b (k p) -> (b k) p", p=P)).then_inc(rows_in, 16)
            sp.dma_start(rows[16:28, :], conv_w.rearrange("b j (k p) -> (b j k) p", p=P)).then_inc(rows_in, 16)
            sp.dma_start(ada_bias, b_ada.rearrange("b (k n) -> (b k) n", n=BANK)).then_inc(rows_in, 16)
            sp.dma_start(xs[:], x[0].rearrange("(i p) n -> p i n", p=P)).then_inc(x_in, 16)
            for i, (kind, n) in enumerate(STREAM):
                if i >= FRONT_RING:
                    was = STREAM[i - FRONT_RING]
                    if was[0] == "ada":
                        sp.wait_ge(ada_steps, ada_steps_of(was[1]))
                        if was[1] < 4:
                            sp.wait_ge(ada_row_done, was[1] + 1)
                    else:
                        sp.wait_ge(w_used, PE_ITEMS.index(was) + 1)
                if kind == "ada":
                    src, m = w_ada[0, :, n * BANK:(n + 1) * BANK], BANK
                elif kind == "in":
                    at, m = IN_BLOCK[n]
                    src = w_in[0, :, at:at + m]
                elif kind == "conv_out":
                    src, m = w_conv_out[0], D
                elif kind == "attn_out":
                    src, m = w_attn_out[0], D
                else:
                    src, m = w_o[0, n * 512:(n + 1) * 512, :], D
                k = src.shape[0] // P
                sp.dma_start(ring[:, i % FRONT_RING, 0:k * m].rearrange("p (k m) -> p k m", m=m),
                             src.rearrange("(k p) m -> p k m", p=P)).then_inc(landed[i % FRONT_RING], 16)

            gu_src = w_gate_up.rearrange("l e (q a p) n -> (l e q) p a n", q=4, p=P)
            dn_src = w_down.rearrange("l e (q a p) n -> (l e q) p a n", q=2, p=P)

            def load_expert(first, group):
                for q in range(6):
                    n = 6 * first + q
                    s = (n + EXPERT_SLOT) % RING
                    if first == 0 and s >= FRONT_RING:
                        if s == FRONT_RING:
                            sp.wait_ge(merged, 4)
                    elif first == 0:
                        was = STREAM[max(i for i in range(len(STREAM)) if i % FRONT_RING == s)]
                        if was[0] == "ada":
                            sp.wait_ge(ada_steps, ada_steps_of(was[1]))
                        else:
                            sp.wait_ge(w_used, PE_ITEMS.index(was) + 1)
                    else:
                        sp.wait_ge(w_used, FRONT_PE + 18 * group + n - RING + 1)
                    e = first + 3 * group
                    if q < 4:
                        src = gu_src[e * 4 + q]
                        dst = ring[:, s, :].rearrange("p (a n) -> p a n", a=2)
                    else:
                        src = dn_src[e * 2 + q - 4]
                        dst = ring[:, s, :].rearrange("p (a n) -> p a n", a=4)
                    sp.dma_start(dst, src).then_inc(landed[s], 16)

            turns(sp, load_expert)
            for i in range(NT):
                sp.wait_ge(fin_ready, i + 1)
                sp.dma_start(out[0, i * P:(i + 1) * P, :], xs[:, i, :]).then_inc(out_done, 16)
            sp.wait_ge(out_done, 16 * NT)

        @block.gpsimd
        def _(pool):
            pool.memset(ident[:], 0.0).then_inc(consts, 1)
            pool.memset(ones[:], 1.0).then_inc(consts, 1)
            pool.memset(ones_b[:], 1.0).then_inc(consts, 1)
            pool.memset(pick[:], 0.0).then_inc(consts, 1)
            pool.memset(zeros_b[:], 0.0).then_inc(consts, 1)
            pool.iota(iota[:], [[1, T]], base=0, channel_multiplier=0,
                      allow_small_or_imprecise_dtypes=True).then_inc(consts, 1)
            pool.wait_ge(consts, 6)
            pool.affine_select(out=ident[:], in_=ident[:], compare_op=ALU.not_equal, fill=1.0, base=0,
                               pattern=[[-1, P]], channel_multiplier=1).then_inc(consts, 1)
            pool.affine_select(out=before[:], in_=ones_b[:], compare_op=ALU.is_gt, fill=0.0, base=0,
                               pattern=[[1, P]], channel_multiplier=-1).then_inc(consts, 1)
            for r in range(3):
                pool.affine_select(out=pick[:], in_=pick[:], compare_op=ALU.not_equal, fill=1.0, base=-32 * r,
                                   pattern=[[-1, EXPERTS]], channel_multiplier=1).then_inc(consts, 1)
                pool.wait_ge(consts, 9 + r)
            pool.wait_ge(xT_done, 1)
            for r in range(3):
                pool.dma_start(bias_raw[32 * r:32 * r + 32, :], b_gate_up[0]).then_inc(gu_bias_in, 16)
            pool.wait_ge(gu_bias_in, 48)
            n = 0
            for r in range(3):
                rs = slice(32 * r, 32 * r + 32)
                for step in range(r + 1):
                    if step:
                        pool.tensor_tensor(bias_raw[rs, :], bias_raw[rs, :], bias_parts[rs, :], ALU.subtract)\
                            .then_inc(bias_steps, 1)
                        n += 1
                        pool.wait_ge(bias_steps, n)
                    pool.tensor_copy(bias_parts[rs, :], bias_raw[rs, :]).then_inc(bias_steps, 1)
                    n += 1
                    pool.wait_ge(bias_steps, n)
            pool.wait_ge(pv_done, UNITS)
            pool.tensor_copy(bias3, bias_parts).then_inc(bias_moved, 1)
            for i in range(NT):
                pool.wait_ge(part0, i + 1)
                pool.wait_ge(h2_T, i + 1)
                pool.tensor_tensor(h2[:, i, :], h2[:, i, :], part[0][:, i, :], ALU.subtract).then_inc(rest0, 1)
                pool.wait_ge(rest0, i + 1)
                pool.wait_ge(part1, i + 1)
                pool.wait_ge(x1_ready, 4)
                pool.tensor_tensor(part[2][:, i, :], h2[:, i, :], part[1][:, i, :], ALU.subtract)\
                    .then_inc(parts_ready, 1)

        @block.scalar
        def _(act):
            n_step = [0]

            def step(ins):
                n_step[0] += 1
                ins.then_inc(act_step, 1)
                act.wait_ge(act_step, n_step[0])

            act.wait_ge(rows_out, 1)
            act.activation(sig_c, small[:, 0:8], ACT.Sigmoid).then_inc(sig_c_done, 1)
            act.wait_ge(x_in, 16)
            for i in range(NT):
                act.activation(featT[:, 0:D], xs[:, i, :], ACT.Square, accum_out=ms[:, i:i + 1]).then_inc(sumsq1, 1)
                act.wait_ge(sumsq1, i + 1)
            act.wait_ge(ms1_done, 1)
            act.activation(rstd[:, :], ms[:, :], ACT.Sqrt).then_inc(std1_done, 1)
            act.wait_ge(rstd1_ready, 1)
            for i in range(NT):
                act.activation(xn[:, i, :], xs[:, i, :], ACT.Copy, scale=rstd[:, i:i + 1]).then_inc(xn_ready, 1)
            for b in range(4):
                act.wait_ge(ada_row_done, b + 1)
                act.activation(ada_rows[:, b, :], ps[0:1, 4 + b % 2, :], ACT.Copy).then_inc(ada_row_out, 1)

            act.wait_ge(xT_done, 1)
            act.wait_ge(mod1_ready, 1)
            for k in range(4, KC):
                act.activation(hT[:, k, :], ps[:, k // 2, (k % 2) * T:(k % 2 + 1) * T], ACT.Identity, bias=sh1[:, k:k + 1],
                               scale=a1[:, k:k + 1]).then_inc(hT_act, 1)

            act.dma_start(wr[:], w_router[0].rearrange("(k p) e -> p k e", p=P)).then_inc(small_in, 16)
            act.dma_start(br[:], b_router[0:1, :]).then_inc(small_in, 16)
            act.dma_start(a2_row[:], norm2_g[0:1, :].broadcast_to([P, D])).then_inc(small_in, 16)
            act.dma_start(gains[:, 0, :], q_norm_g[0:1, :].broadcast_to([P, HD])).then_inc(gains_in, 16)
            act.dma_start(gains[:, 1, :], k_norm_g[0:1, :].broadcast_to([P, HD])).then_inc(gains_in, 16)

            def job_copy(name, dst, func=ACT.Copy, scale=1.0):
                j = JOB[name]
                act.wait_ge(job_done, j + 1)
                act.activation(dst, ps[:, 4 + j % 2, :], func, scale=scale).then_inc(bank_read[j % 2], 1)

            def fold(ap):
                return ap.rearrange("p c t -> p (c t)")

            job_copy("qi", fold(qiT))
            j = JOB["kiwi"]
            act.wait_ge(job_done, j + 1)
            step(act.activation(kiT, ps[:, 5, 0:T], ACT.Copy))
            act.activation(vec[:, 32:40], ps[:, 5, T:T + 8], ACT.Copy, scale=IDX_SCALE).then_inc(bank_read[1], 1)
            for i in range(NT):
                w = P * (i + 1)
                act.wait_ge(dots_done, i + 1)
                if i:
                    act.wait_ge(score_done, i)
                for b in range(2):
                    act.activation(relu[:, b, :, 0:w], ps[:, 2 * i + b, :].rearrange("p (h s) -> p h s", h=2)[:, :, 0:w],
                                   ACT.Relu).then_inc(relu_done, 1)
            for i in range(NT):
                job_copy(f"q{i}", q_tok[:, i, :])
            for i in range(NT):
                job_copy(f"k{i}", k_tok[:, i, :])
            act.wait_ge(head_ms, 1)
            act.activation(hs[:], hs[:], ACT.Sqrt).then_inc(head_std, 1)
            for i in range(NT):
                job_copy(f"v{i}", v_tok[:, i, :])
            for n, dst in enumerate((qT, qT, kT, kT)):
                act.wait_ge(qk_T, n + 1)
                act.activation(dst[:, :, (n % 2) * P:(n % 2) * P + P], ps[:, n, :].rearrange("p (c t) -> p c t", c=4),
                               ACT.Copy).then_inc(qkT_ready, 1)

            def softmax_exp(u):
                i, w = u // 4, P * (u // 4 + 1)
                act.wait_ge(max_ready, u + 1)
                for h in range(2):
                    act.activation(lg[:, u % 2, h, 0:w], lg[:, u % 2, h, 0:w], ACT.Exp, bias=neg_max[:, u % 2, h:h + 1],
                                   accum_out=row_sum[:, u % 2, h:h + 1]).then_inc(exp_done, 1)

            def probs_T_copy(u):
                n = u // 4 + 1
                act.wait_ge(probs_T, u + 1)
                if u >= 2:
                    act.wait_ge(pv_done, u - 1)
                act.activation(pT[:, u % 2, :, 0:n, :],
                               ps[:, 6, :].rearrange("p (h s t) -> p h s t", h=2, s=2)[:, :, 0:n, :],
                               ACT.Copy).then_inc(pT_ready, 1)

            def pv_copy(u):
                i, hp = u // 4, u % 4
                act.wait_ge(pv_done, u + 1)
                act.activation(yB[:, hp, i * P:(i + 1) * P], ps[:, 7, (u % 2) * P:(u % 2) * P + P], ACT.Copy)\
                   .then_inc(yB_ready, 1)

            for name in JOBS[FIRST_UNIT_JOB:JOB["wo0"]]:
                j = JOB[name]
                n = int(name[-1])
                if name == "ga0":
                    act.wait_ge(bias_steps, 9)
                if name == "mod10":
                    act.wait_ge(bias_moved, 1)
                if name[:-1] == "xin":
                    job_copy(name, fold(xinS[:, 2 * n:2 * n + 2, :]))
                elif name[:-1] == "ga":
                    job_copy(name, fold(sgA[:, 2 * n:2 * n + 2, :]), ACT.Sigmoid)
                elif name[:-1] == "gB":
                    job_copy(name, fold(sgB[:, 2 * n:2 * n + 2, :]), ACT.Sigmoid)
                elif name in ("mod4", "mod5"):
                    job_copy(name, g1_row[:, (n - 4) * BANK:(n - 3) * BANK])
                elif name in ("mod6", "mod7"):
                    job_copy(name, sh2_row[:, (n - 6) * BANK:(n - 5) * BANK])
                elif name in ("mod10", "mod11"):
                    job_copy(name, g2_row[:, n * BANK:(n + 1) * BANK])
                k = j - FIRST_UNIT_JOB
                if k >= 2 and k % 2 == 0 and k // 2 - 1 < UNITS:
                    pv_copy(k // 2 - 1)
                if k % 2 == 1 and k // 2 < UNITS:
                    probs_T_copy(k // 2)
                if k % 2 == 0 and k // 2 < UNITS:
                    softmax_exp(k // 2)

            act.wait_ge(pv_done, UNITS)
            act.dma_start(bd, b_down[0]).then_inc(down_bias_in, 16)

            def square_sum(i):
                act.wait_ge(x1_ready, 2 * i + 2)
                act.activation(h2[:, i, :], xs[:, i, :], ACT.Square, accum_out=ms[:, i:i + 1]).then_inc(sumsq2, 1)

            def root(i):
                act.wait_ge(ms2_done, i + 1)
                act.activation(rstd[:, i:i + 1], ms[:, i:i + 1], ACT.Sqrt).then_inc(std2_done, 1)

            def h2T_copy(i):
                act.wait_ge(h2_T, i + 1)
                act.wait_ge(job_done, len(JOBS))
                act.activation(h2T[:, i, 4:8, :], ps[:, 2 * i + 1, :].rearrange("p (k t) -> p k t", k=4), ACT.Copy)\
                   .then_inc(h2T_act, 1)

            def split(i):
                act.wait_ge(h2_ready, i + 1)
                act.activation(part[0][:, i, :], h2[:, i, :], ACT.Copy).then_inc(part0, 1)
                act.wait_ge(rest0, i + 1)
                act.activation(part[1][:, i, :], h2[:, i, :], ACT.Copy).then_inc(part1, 1)

            square_sum(0)
            root(0)
            split(0)
            square_sum(1)
            h2T_copy(0)
            root(1)
            h2T_copy(1)
            split(1)
            for i in range(NT):
                act.wait_ge(top_ready, i + 1)
                act.activation(rt[:, 16 + 4 * i:20 + 4 * i], rt[:, 8 * i:8 * i + 4], ACT.Exp,
                               bias=rt[:, 24 + i:25 + i], accum_out=rt[:, 26 + i:27 + i]).then_inc(top_exp, 1)

            def evacuate_gather(sems, dst, v):
                act.wait_ge(sems["gathered"], v)
                act.activation(dst, ps[:, AUX, :], ACT.Copy).then_inc(sems["xg_ready"], 1)

            def gate_sigmoid(sems, v):
                act.wait_ge(sems["glu_ready"], v)
                act.activation(sig, glu, ACT.Sigmoid, scale=ALPHA).then_inc(sems["sig_ready"], 1)

            def evacuate_transposes(sems, banks, dst, v):
                act.wait_ge(sems["act_T"], v)
                act.activation(actT, ps[:, banks[0], :], ACT.Copy).then_inc(sems["actT_ready"], 1)
                act.wait_ge(sems["sg_T"], v)
                act.activation(dst, ps[:, banks[1], 0:T], ACT.Copy).then_inc(sems["sgT_ready"], 1)

            evacuate_gather(main_sems, xg, 1)
            more = act.alloc_register("act_more")
            act.reg_mov(more, 0)

            def expert(first, group):
                e = act.snap(first + 3 * group)
                count = act.value_load(counts[0:1, bass.ds(e, 1)])
                with act.If(count > SLOTS):
                    with act.Fori(1, T // SLOTS) as p:
                        with act.If(count > p * SLOTS):
                            v = act.snap(more) + 1
                            evacuate_gather(more_sems, xg_o, v)
                            gate_sigmoid(more_sems, v)
                            evacuate_transposes(more_sems, (AUX, YB), sgT_o, v)
                            act.reg_add(more, more, 1)
                gate_sigmoid(main_sems, e + 1)
                if first < EXPERTS - 1:
                    evacuate_gather(main_sems, xg, e + 2)
                evacuate_transposes(main_sems, (GLU, LIN), sgT, e + 1)

            act.wait_ge(routed, 1)
            turns(act, expert)

        @block.vector
        def _(dve):
            n_step = [0]

            def step(ins):
                n_step[0] += 1
                ins.then_inc(dve_step, 1)
                dve.wait_ge(dve_step, n_step[0])

            def ada_block(b, lo, hi):
                if lo == 0:
                    if b >= 4 and b % 2 == 0:
                        dve.wait_ge(mod_summed, b - 2)
                    wait_landed(dve, ("ada", b))
                acc = modacc[:, (b // 2) % 2, (b % 2) * BANK:(b % 2 + 1) * BANK]
                for k in range(lo, hi):
                    w = slot(("ada", b))[:, k * BANK:(k + 1) * BANK]
                    if k == 0:
                        ins = dve.tensor_scalar(acc, w, silu_c[:, 0:1], None, ALU.mult)
                    else:
                        ins = dve.scalar_tensor_tensor(out=acc, in0=w, scalar=silu_c[:, k:k + 1], in1=acc,
                                                       op0=ALU.mult, op1=ALU.add)
                    ins.then_inc(ada_steps, 1)
                    dve.wait_ge(ada_steps, (ada_steps_of(b - 1) if b else 0) + k + 1)
                    if k == 0:
                        acc12 = acc[32:44, :]
                        step(dve.scalar_tensor_tensor(out=acc12, in0=ada_bias, scalar=ident[32:44, 32 + b:33 + b],
                                                      in1=acc12, op0=ALU.mult, op1=ALU.add))

            dve.memset(conv_u[:, :, 0:2], 0.0)
            dve.wait_ge(rows_T, 1)
            dve.tensor_copy(small[:, 0:28], ps[:, 7, 0:28]).then_inc(rows_out, 1)
            dve.wait_ge(sig_c_done, 1)
            dve.wait_ge(rows_out, 1)
            dve.tensor_tensor(silu_c, small[:, 0:8], sig_c, ALU.mult).then_inc(silu_done, 1)
            dve.wait_ge(silu_done, 1)
            dve.wait_ge(sumsq1, 2)
            dve.tensor_scalar(ms[:, :], ms[:, :], 1.0 / D, EPS, ALU.mult, ALU.add).then_inc(ms1_done, 1)
            dve.wait_ge(std1_done, 1)
            dve.reciprocal(rstd[:, :], rstd[:, :]).then_inc(rstd1_ready, 1)
            dve.wait_ge(consts, 7)
            for b in range(4):
                ada_block(b, 0, EARLY_K)
            dve.wait_ge(mod_summed, 4)
            step(dve.tensor_copy(sh1, ps[:, 7, 32:40]))
            dve.scalar_tensor_tensor(out=a1, in0=ps[:, 7, 40:48], scalar=1.0, in1=small[:, 8:16], op0=ALU.add,
                                     op1=ALU.mult).then_inc(mod1_ready, 1)
            dve.wait_ge(mod1_ready, 1)
            dve.wait_ge(xT_done, 1)
            for k in range(4):
                dve.tensor_scalar(hT[:, k, :], ps[:, k // 2, (k % 2) * T:(k % 2 + 1) * T], a1[:, k:k + 1], sh1[:, k:k + 1], ALU.mult,
                                  ALU.add).then_inc(hT_dve, 1)

            for i in range(NT):
                w = P * (i + 1)
                dve.wait_ge(relu_done, 2 * i + 2)
                s = score[:, i, 0:w]
                step(dve.tensor_scalar(s, relu[:, 0, 0, 0:w], wi[:, i, 0:1], None, ALU.mult))
                for h in range(1, IDX_HEADS):
                    ins = dve.scalar_tensor_tensor(out=s, in0=relu[:, h % 2, h // 2, 0:w], scalar=wi[:, i, h:h + 1],
                                                   in1=s, op0=ALU.mult, op1=ALU.add)
                    if h < IDX_HEADS - 1:
                        step(ins)
                ins.then_inc(score_done, 1)
                dve.wait_ge(score_done, i + 1)
                step(dve.memset(score[0:CHUNK, i, w - CHUNK:w], NEG))
                for r in range(TOPK // 8):
                    step(dve.max(top8, s))
                    step(dve.match_replace(s, top8, s, TAKEN))
                dve.tensor_scalar(am[:, i, 0:w], s, (NEG + TAKEN) / 2, UNSEEN, ALU.is_gt, ALU.mult)\
                   .then_inc(mask_ready, 1)

            for n, (name, src) in enumerate((("q0", q_tok), ("q1", q_tok), ("k0", k_tok), ("k1", k_tok))):
                j = JOB[name]
                dve.wait_ge(bank_read[j % 2], j // 2 + 1)
                step(dve.tensor_tensor(sq, src[:, n % 2, :], src[:, n % 2, :], ALU.mult))
                step(dve.tensor_reduce(hs[:, 8 * n:8 * n + 8], sq.rearrange("p (h d) -> p h d", h=HEADS), AX_X, ALU.add))
            dve.tensor_scalar(hs[:], hs[:], 1.0 / HD, EPS, ALU.mult, ALU.add).then_inc(head_ms, 1)
            dve.wait_ge(head_std, 1)
            step(dve.reciprocal(hs[:], hs[:]))
            dve.wait_ge(gains_in, 32)
            for n, src in enumerate((q_tok, q_tok, k_tok, k_tok)):
                v = src[:, n % 2, :].rearrange("p (h d) -> p h d", h=HEADS)
                step(dve.tensor_tensor(v, v, hs[:, 8 * n:8 * n + 8].unsqueeze(2).broadcast_to([P, HEADS, HD]), ALU.mult))
                dve.tensor_tensor(v, v, gains[:, n // 2, :].unsqueeze(1).broadcast_to([P, HEADS, HD]), ALU.mult)\
                   .then_inc(qk_normed, 1)

            def softmax_max(u):
                i, w, b = u // 4, P * (u // 4 + 1), u % 2
                dve.wait_ge(logits_done, u + 1)
                if u >= 2:
                    dve.wait_ge(probs_T, u - 1)
                dve.scalar_tensor_tensor(out=lg[:, b, :, 0:w], in0=ps[:, 2 * b:2 * b + 2, 0:w], scalar=HD ** -0.5,
                                         in1=am[:, i, 0:w].unsqueeze(1).broadcast_to([P, 2, w]), op0=ALU.mult,
                                         op1=ALU.add).then_inc(logits_read, 1)
                dve.wait_ge(logits_read, u + 1)
                dve.tensor_reduce(neg_max[:, b, :], lg[:, b, :, 0:w], AX_X, ALU.max, negate=True)\
                   .then_inc(max_ready, 1)

            def softmax_scale(u):
                w, b = P * (u // 4 + 1), u % 2
                dve.wait_ge(exp_done, 2 * u + 2)
                step(dve.reciprocal(row_sum[:, b, :], row_sum[:, b, :]))
                dve.tensor_tensor(lg[:, b, :, 0:w], lg[:, b, :, 0:w],
                                  row_sum[:, b, :].unsqueeze(2).broadcast_to([P, 2, w]), ALU.mult)\
                   .then_inc(probs_ready, 1)

            def conv(n):
                j = JOB[f"gc{n}"]
                dve.wait_ge(job_done, j + 1)
                jx = JOB[f"xin{n}"]
                dve.wait_ge(bank_read[jx % 2], jx // 2 + 1)
                dve.tensor_tensor(conv_u[:, 2 * n:2 * n + 2, 2:T + 2],
                                  ps[:, 4 + j % 2, :].rearrange("p (c t) -> p c t", c=2),
                                  xinS[:, 2 * n:2 * n + 2, :], ALU.mult).then_inc(bank_read[j % 2], 1)
                dve.wait_ge(bank_read[j % 2], j // 2 + 1)
                if n == 0:
                    dve.wait_ge(qk_T, 4)
                for cc in (2 * n, 2 * n + 1):
                    step(dve.tensor_scalar(yA[:, cc, :], conv_u[:, cc, 0:T], small[:, 16 + cc:17 + cc], None, ALU.mult))
                    for tap in (1, 2):
                        step(dve.scalar_tensor_tensor(out=yA[:, cc, :], in0=conv_u[:, cc, tap:T + tap],
                                                      scalar=small[:, 16 + 4 * tap + cc:17 + 4 * tap + cc],
                                                      in1=yA[:, cc, :], op0=ALU.mult, op1=ALU.add))

            for name in JOBS[FIRST_UNIT_JOB:JOB["pa0"]]:
                j = JOB[name]
                n = int(name[-1])
                bank = ps[:, 4 + j % 2, :]
                if name[:-1] == "gc":
                    conv(n)
                if name[:-1] == "gb":
                    dve.wait_ge(job_done, j + 1)
                    dve.tensor_tensor(yA[:, 2 * n:2 * n + 2, :], bank.rearrange("p (c t) -> p c t", c=2),
                                      yA[:, 2 * n:2 * n + 2, :], ALU.mult).then_inc(bank_read[j % 2], 1)
                if name in ("mod8", "mod9"):
                    a2 = a2_row[:, (n - 8) * BANK:(n - 7) * BANK]
                    dve.wait_ge(job_done, j + 1)
                    dve.wait_ge(small_in, 48)
                    dve.scalar_tensor_tensor(out=a2, in0=bank, scalar=1.0, in1=a2, op0=ALU.add, op1=ALU.mult)\
                       .then_inc(bank_read[j % 2], 1)
                k = j - FIRST_UNIT_JOB
                if k % 2 == 0 and k // 2 < UNITS:
                    softmax_max(k // 2)
                    softmax_scale(k // 2)
                if name in ADA_HALF:
                    b, half = divmod(ADA_HALF.index(name), 2)
                    ada_block(4 + b, 4 * half, 4 * half + 4)

            for n in range(4):
                j = JOB[f"pa{n}"]
                jg = JOB[f"ga{n}"]
                dve.wait_ge(job_done, j + 1)
                dve.wait_ge(bank_read[jg % 2], jg // 2 + 1)
                dve.tensor_tensor(mT[:, 2 * n:2 * n + 2, :].rearrange("p c t -> p (c t)"), ps[:, 4 + j % 2, :],
                                  sgA[:, 2 * n:2 * n + 2, :].rearrange("p c t -> p (c t)"), ALU.mult)\
                   .then_inc(bank_read[j % 2], 1)
                ada_block(11, 2 * n, 2 * n + 2)
            for n in range(4):
                j = JOB[f"pb{n}"]
                jg = JOB[f"gB{n}"]
                s = sgB[:, 2 * n:2 * n + 2, :].rearrange("p c t -> p (c t)")
                m = mT[:, 2 * n:2 * n + 2, :].rearrange("p c t -> p (c t)")
                dve.wait_ge(job_done, j + 1)
                dve.wait_ge(bank_read[jg % 2], jg // 2 + 1)
                dve.tensor_tensor(s, ps[:, 4 + j % 2, :], s, ALU.mult).then_inc(bank_read[j % 2], 1)
                dve.wait_ge(bank_read[j % 2], j // 2 + 1)
                dve.tensor_tensor(m, m, s, ALU.add).then_inc(merged, 1)
            dve.wait_ge(bank_read[1], JOB["mod5"] // 2 + 1)
            def residual(n):
                i, half = n // 2, n % 2
                j = JOB[f"wo{n}"]
                cols = slice(half * BANK, (half + 1) * BANK)
                dve.wait_ge(job_done, j + 1)
                if n:
                    dve.wait_ge(x1_ready, n)
                dve.tensor_tensor(prod[:], ps[:, 4 + j % 2, :], g1_row[:, cols], ALU.mult).then_inc(bank_read[j % 2], 1)
                dve.wait_ge(bank_read[j % 2], j // 2 + 1)
                dve.tensor_tensor(xs[:, i, cols], xs[:, i, cols], prod[:], ALU.add).then_inc(x1_ready, 1)

            def norm2_ms(i):
                dve.wait_ge(sumsq2, i + 1)
                dve.tensor_scalar(ms[:, i:i + 1], ms[:, i:i + 1], 1.0 / D, EPS, ALU.mult, ALU.add).then_inc(ms2_done, 1)

            def norm2_rows(i):
                dve.wait_ge(std2_done, i + 1)
                step(dve.reciprocal(rstd[:, i:i + 1], rstd[:, i:i + 1]))
                step(dve.scalar_tensor_tensor(out=h2[:, i, :], in0=xs[:, i, :], scalar=rstd[:, i:i + 1], in1=a2_row[:],
                                              op0=ALU.mult, op1=ALU.mult))
                dve.tensor_tensor(h2[:, i, :], h2[:, i, :], sh2_row[:], ALU.add).then_inc(h2_ready, 1)

            def h2T_copy(i):
                dve.wait_ge(h2_T, i + 1)
                dve.wait_ge(job_done, len(JOBS))
                dve.tensor_copy(h2T[:, i, 0:4, :], ps[:, 2 * i, :].rearrange("p (k t) -> p k t", k=4))\
                   .then_inc(h2T_dve, 1)

            idxf = rt[:, 28:36].rearrange("p (i k) -> p i k", i=NT)

            def route(i):
                dve.wait_ge(router_done, i + 1)
                step(dve.tensor_copy(lr[:, i, :], ps[:, AUX + i, 0:EXPERTS]))
                step(dve.max(rt[:, 8 * i:8 * i + 8], lr[:, i, :]))
                dve.tensor_scalar(rt[:, 24 + i:25 + i], rt[:, 8 * i:8 * i + 1], -1.0, None, ALU.mult)\
                   .then_inc(top_ready, 1)
                step(dve.max_index(idx8[:, i, :], rt[:, 8 * i:8 * i + 8], lr[:, i, :]))
                step(dve.tensor_copy(idxf[:, i, :], idx8[:, i, 0:ROUTE]))
                step(dve.tensor_tensor(hit[:, i], iota[:, 0:EXPERTS].unsqueeze(1).broadcast_to([P, ROUTE, EXPERTS]),
                                       idxf[:, i, :].unsqueeze(2).broadcast_to([P, ROUTE, EXPERTS]), ALU.is_equal))
                step(dve.tensor_reduce(mask[:, i, :], hit[:, i].rearrange("p k e -> p e k"), AX_X, ALU.add))
                dve.tensor_copy(m_b[:, i, :], mask[:, i, :]).then_inc(mask_b_ready, 1)

            dve.wait_ge(consts, 11)
            residual(0)
            residual(1)
            norm2_ms(0)
            norm2_rows(0)
            residual(2)
            residual(3)
            h2T_copy(0)
            norm2_ms(1)
            norm2_rows(1)
            route(0)
            h2T_copy(1)
            route(1)
            dve.wait_ge(rank_done, 1)
            step(dve.scalar_tensor_tensor(out=rank[:], in0=ps[:, GLU, 0:NT * EXPERTS].rearrange("p (i e) -> p i e", i=NT),
                                          scalar=1.0, in1=mask, op0=ALU.add, op1=ALU.mult))
            step(dve.tensor_scalar(rank[:], rank[:], -1.0, None, ALU.add))

            def build_onehot(sems, e, lo):
                for i in range(NT):
                    ins = dve.tensor_scalar(onehot[:, i, :], iota[:, lo], rank[:, i, bass.ds(e, 1)], None, ALU.is_equal)
                ins.then_inc(sems["onehot_ready"], 1)

            def build_scatter(sems, e, lo):
                for i in range(NT):
                    ins = dve.tensor_scalar(sg[:, i], iota[:, lo].unsqueeze(1).broadcast_to([P, 2, SLOTS]),
                                            rank[:, i, bass.ds(e, 1)], gate[:, i, bass.ds(e, 1)], ALU.is_equal, ALU.mult)
                ins.then_inc(sems["sg_ready"], 1)

            def pick_expert(e):
                dve.tensor_copy(pick_e[0:96, :], pick[:, bass.ds(e, 1)].broadcast_to([96, SLOTS])).then_inc(pick_ready, 1)

            def swiglu(sems, banks, v):
                dve.tensor_scalar(glu, ps[:, banks[0], :], LIMIT, None, ALU.min).then_inc(sems["glu_ready"], 1)
                dve.tensor_scalar(lin, ps[:, banks[1], :], LIMIT, -LIMIT, ALU.min, ALU.max).then_inc(sems["lin_ready"], 1)
                dve.wait_ge(sems["glu_ready"], v)
                dve.wait_ge(sems["lin_ready"], v)
                dve.scalar_tensor_tensor(out=lin, in0=lin, scalar=1.0, in1=glu, op0=ALU.add, op1=ALU.mult)\
                   .then_inc(sems["prod_ready"], 1)
                dve.wait_ge(sems["prod_ready"], v)
                dve.wait_ge(sems["sig_ready"], v)
                dve.tensor_tensor(act_v, lin, sig, ALU.mult).then_inc(sems["act_ready"], 1)

            def evacuate_y(sems, bank, dst):
                dve.tensor_copy(dst, ps[:, bank, :]).then_inc(sems["y_ready"], 1)

            first_places = slice(0, SLOTS)
            build_onehot(main_sems, 0, first_places)
            step(dve.tensor_copy(counts[:], ps[0:1, GLU, NT * EXPERTS:(NT + 1) * EXPERTS]))
            pick_expert(0)
            dve.wait_ge(pick_ready, 1)
            dve.nop().then_inc(routed, 1)
            dve.wait_ge(top_exp, NT)
            step(dve.reciprocal(rt[:, 26:28], rt[:, 26:28]))
            for i in range(NT):
                step(dve.tensor_scalar(rt[:, 16 + 4 * i:20 + 4 * i], rt[:, 16 + 4 * i:20 + 4 * i], rt[:, 26 + i:27 + i],
                                       None, ALU.mult))
                step(dve.tensor_tensor(hit_g[:, i], hit[:, i],
                                       rt[:, 16 + 4 * i:20 + 4 * i].unsqueeze(2).broadcast_to([P, ROUTE, EXPERTS]),
                                       ALU.mult))
                dve.tensor_reduce(gate[:, i, :], hit_g[:, i].rearrange("p k e -> p e k"), AX_X, ALU.add)\
                   .then_inc(gates_ready, 1)
            dve.wait_ge(gates_ready, 2)
            more = dve.alloc_register("dve_more")
            dve.reg_mov(more, 0)

            def expert(first, group):
                e = dve.snap(first + 3 * group)
                count = dve.value_load(counts[0:1, bass.ds(e, 1)])

                def buffers_free():
                    dve.wait_ge(gathered, e + 1)
                    if first:
                        dve.wait_ge(sg_T, e)

                with dve.If(count > SLOTS):
                    with dve.Fori(1, T // SLOTS) as p:
                        with dve.If(count > p * SLOTS):
                            v = dve.snap(more) + 1
                            lo = bass.ds(p * SLOTS, SLOTS)
                            buffers_free()
                            build_onehot(more_sems, e, lo)
                            build_scatter(more_sems, e, lo)
                            dve.wait_ge(more_gu_done, v)
                            swiglu(more_sems, (AUX, YB), v)
                            dve.wait_ge(more_down_done, v)
                            evacuate_y(more_sems, AUX, y_o)
                            dve.reg_add(more, more, 1)
                buffers_free()
                if first < EXPERTS - 1:
                    build_onehot(main_sems, e + 1, first_places)
                build_scatter(main_sems, e, first_places)
                dve.wait_ge(w_used, sixths_used(e, 4))
                swiglu(main_sems, (GLU, LIN), e + 1)
                if first < EXPERTS - 1:
                    pick_expert(e + 1)
                if not first:
                    dve.wait_ge(gate_T, 1)
                    dve.tensor_copy(gT, ps[0:EXPERTS, YB, 0:T]).then_inc(gT_ready, 1)
                dve.wait_ge(w_used, sixths_used(e, 6))
                evacuate_y(main_sems, YB, y)

            turns(dve, expert)
            dve.wait_ge(acc_done, 1)
            for i in range(NT):
                for half in range(2):
                    cols = slice(half * BANK, (half + 1) * BANK)
                    step(dve.tensor_tensor(prod[:], ps[:, 2 * i + half, :], g2_row[:, cols], ALU.mult))
                    ins = dve.tensor_tensor(xs[:, i, cols], xs[:, i, cols], prod[:], ALU.add)
                    if half == 0:
                        step(ins)
                ins.then_inc(fin_ready, 1)
                dve.wait_ge(fin_ready, i + 1)

        @block.tensor
        def _(pe):
            def wait_bank(j):
                if j >= 2:
                    pe.wait_ge(bank_read[j % 2], j // 2)

            def feature_job(name, cols, item, src=hT, kc=KC, m=BANK):
                j = JOB[name]
                wait_bank(j)
                wait_landed(pe, item)
                w = slot(item)[:, 0:kc * m].rearrange("p (k m) -> p k m", m=m)
                for n, at in enumerate(cols):
                    for k in range(kc):
                        ins = pe.matmul(ps[:, 4 + j % 2, n * T:(n + 1) * T], w[:, k, at:at + P], src[:, k, :],
                                        start=(k == 0), stop=(k == kc - 1))
                return ins

            def finish(ins):
                ins.then_inc(job_done, 1)

            pe.wait_ge(consts, 7)
            pe.wait_ge(rows_in, 64)
            pe.transpose(ps[:, 7, 0:28], rows, ident[0:28, 0:28]).then_inc(rows_T, 1)
            pe.wait_ge(xn_ready, 2)
            for k in range(KC):
                for i in range(NT):
                    ins = pe.transpose(ps[:, k // 2, (k % 2) * T + i * P:(k % 2) * T + (i + 1) * P],
                                       xn[:, i, k * P:(k + 1) * P], ident[:])
            ins.then_inc(xT_done, 1)
            pe.wait_ge(silu_done, 1)
            pe.wait_ge(rows_out, 1)

            def turn_row(b):
                pe.wait_ge(ada_row_out, b + 1)
                for k in range(4):
                    o = 32 + 4 * b + k
                    ins = pe.matmul(ps[:, 7, o:o + 1], ada_rows[:, b, k * P:(k + 1) * P], ones[0:1, 0:1], start=True,
                                    stop=True)
                ins.then_inc(mod_summed, 1)

            for b in range(4):
                wait_landed(pe, ("ada", b))
                for k in range(EARLY_K, KC):
                    pe.matmul(ps[0:1, 4 + b % 2, :], silu_c[:, k:k + 1], slot(("ada", b))[:, k * BANK:(k + 1) * BANK],
                              start=(k == EARLY_K), stop=False)
                if b:
                    turn_row(b - 1)
                pe.wait_ge(ada_steps, ada_steps_of(b))
                pe.matmul(ps[0:1, 4 + b % 2, :], ones[:, 0:1], modacc[:, b // 2, (b % 2) * BANK:(b % 2 + 1) * BANK],
                          start=False, stop=True).then_inc(ada_row_done, 1)
            turn_row(3)
            pe.wait_ge(hT_dve, 4)
            pe.wait_ge(hT_act, 4)

            used = [0]
            block_last = {"kiwi": ("in", "idx"), "q1": ("in", "q"), "k1": ("in", "k"), "v1": ("in", "v"),
                          "xin1": ("in", "xin"), "gc1": ("in", "gc"), "gb1": ("in", "gb"), "ga1": ("in", "ga0"),
                          "ga3": ("in", "ga1"), "gB1": ("in", "gB0"), "gB3": ("in", "gB1"), "pa3": ("conv_out", 0),
                          "pb3": ("attn_out", 0)}

            def release(name):
                if name in block_last:
                    assert PE_ITEMS[used[0]] == block_last[name]
                    used[0] += 1
                    pe.wait_ge(job_done, JOB[name] + 1)
                    pe.nop().then_inc(w_used, 1)

            def job(name):
                j = JOB[name]
                bank = ps[:, 4 + j % 2, :]
                n = int(name[-1]) if name[-1].isdigit() else 0
                if name == "qi":
                    finish(feature_job(name, (0, P), item=("in", "idx"), m=GA - QI))
                elif name == "kiwi":
                    wait_bank(j)
                    w = slot(("in", "idx"))[:, 0:KC * (GA - QI)].rearrange("p (k m) -> p k m", m=GA - QI)
                    for k in range(KC):
                        for half in range(2):
                            pe.matmul(bank[64 * half:64 * half + 64, 0:T], w[:, k, KI - QI:KI - QI + 64], hT[:, k, :],
                                      start=(k == 0), stop=(k == KC - 1), skip_group_check=True)
                    for i in range(NT):
                        for k in range(KC):
                            ins = pe.matmul(bank[:, T + 4 * i:T + 4 * i + 4], hT[:, k, i * P:(i + 1) * P],
                                            w[:, k, WI - QI:WI - QI + 4], start=(k == 0), stop=(k == KC - 1),
                                            skip_group_check=True)
                    finish(ins)
                elif name[0] in "qkv":
                    item = ("in", name[0])
                    wait_bank(j)
                    wait_landed(pe, item)
                    w = slot(item).rearrange("p (k m) -> p k m", m=BANK)
                    for k in range(KC):
                        ins = pe.matmul(bank, hT[:, k, n * P:(n + 1) * P], w[:, k, :], start=(k == 0), stop=(k == KC - 1))
                    finish(ins)
                elif name[:-1] in ("xin", "gc", "gb"):
                    finish(feature_job(name, (2 * n * P, (2 * n + 1) * P), item=("in", name[:-1])))
                elif name[:-1] in ("ga", "gB"):
                    m = n % 2
                    finish(feature_job(name, (2 * m * P, (2 * m + 1) * P), item=("in", f"{name[:-1]}{n // 2}")))
                elif name[:3] == "mod":
                    b = int(name[3:])
                    wait_bank(j)
                    pe.wait_ge(ada_steps, ada_steps_of(b))
                    finish(pe.matmul(bank, ones[:], modacc[:, (b // 2) % 2, (b % 2) * BANK:(b % 2 + 1) * BANK],
                                     start=True, stop=True))
                    if b % 2:
                        pe.wait_ge(job_done, j + 1)
                        pe.nop().then_inc(mod_summed, 2)
                elif name[:2] in ("pa", "pb"):
                    if name == "pa0":
                        pe.wait_ge(bank_read[0], JOB["gb0"] // 2 + 1)
                        pe.wait_ge(bank_read[1], JOB["gb1"] // 2 + 1)
                    if name == "pb0":
                        pe.wait_ge(yB_ready, UNITS)
                    finish(feature_job(name, (2 * n * P, (2 * n + 1) * P), src=yA if name[1] == "a" else yB, kc=4,
                                       item=("conv_out", 0) if name[1] == "a" else ("attn_out", 0), m=D))
                else:
                    i, half = n // 2, n % 2
                    wait_bank(j)
                    for k in range(KC):
                        if n == 0 and k % 2 == 0:
                            pe.wait_ge(merged, k // 2 + 1)
                        if n == 0 and k % 4 == 0:
                            wait_landed(pe, ("w_o", k // 4))
                        w = slot(("w_o", k // 4)).rearrange("p (k m) -> p k m", m=D)
                        ins = pe.matmul(bank, mT[:, k, i * P:(i + 1) * P], w[:, k % 4, half * BANK:(half + 1) * BANK],
                                        start=(k == 0), stop=(k == KC - 1))
                    finish(ins)
                release(name)

            job("qi")
            job("kiwi")
            pe.wait_ge(bank_read[0], 1)
            pe.wait_ge(bank_read[1], 1)
            for i in range(NT):
                w = P * (i + 1)
                for h in range(IDX_HEADS):
                    half = slice(64 * (h % 2), 64 * (h % 2) + 64)
                    ins = pe.matmul(ps[:, 2 * i + h % 2, (h // 2) * T:(h // 2) * T + w], qiT[half, h // 2, i * P:(i + 1) * P],
                                    kiT[half, 0:w], start=True, stop=True, skip_group_check=True)
                ins.then_inc(dots_done, 1)
            for name in ("q0", "q1", "k0", "k1", "v0", "v1"):
                job(name)
            pe.wait_ge(relu_done, 4)
            for n, src in enumerate((q_tok, q_tok, k_tok, k_tok)):
                pe.wait_ge(qk_normed, n + 1)
                for hp in range(4):
                    ins = pe.transpose(ps[:, n, hp * P:(hp + 1) * P], src[:, n % 2, hp * P:(hp + 1) * P], ident[:])
                ins.then_inc(qk_T, 1)

            def logits(u):
                i, hp, w, b = u // 4, u % 4, P * (u // 4 + 1), u % 2
                if u == 0:
                    pe.wait_ge(qkT_ready, 4)
                    pe.wait_ge(mask_ready, 2)
                if u >= 2:
                    pe.wait_ge(logits_read, u - 1)
                for h in range(2):
                    half = slice(64 * h, 64 * h + 64)
                    ins = pe.matmul(ps[:, 2 * b + h, 0:w], qT[half, hp, i * P:(i + 1) * P], kT[half, hp, 0:w],
                                    start=True, stop=True)
                ins.then_inc(logits_done, 1)

            def probs_transpose(u):
                n = u // 4 + 1
                pe.wait_ge(probs_ready, u + 1)
                if u >= 1:
                    pe.wait_ge(pT_ready, u)
                for h in range(2):
                    for s in range(n):
                        ins = pe.transpose(ps[:, 6, (2 * h + s) * P:(2 * h + s + 1) * P],
                                           lg[:, u % 2, h, s * P:(s + 1) * P], ident[:])
                ins.then_inc(probs_T, 1)

            def values(u):
                n, hp = u // 4 + 1, u % 4
                pe.wait_ge(pT_ready, u + 1)
                if u >= 1:
                    pe.wait_ge(yB_ready, u)
                if u == 0:
                    pe.wait_ge(bank_read[1], JOB["v1"] // 2 + 1)
                for h in range(2):
                    for s in range(n):
                        head = 2 * hp + h
                        ins = pe.matmul(ps[64 * h:64 * h + 64, 7, (u % 2) * P:(u % 2) * P + P],
                                        v_tok[:, s, head * HD:(head + 1) * HD], pT[:, u % 2, h, s, :],
                                        start=(s == 0), stop=(s == n - 1), skip_group_check=True)
                ins.then_inc(pv_done, 1)

            for name in JOBS[FIRST_UNIT_JOB:JOB["wo3"]]:
                job(name)
                k = JOB[name] - FIRST_UNIT_JOB
                if k >= 2 and k % 2 == 0 and k // 2 - 1 < UNITS:
                    values(k // 2 - 1)
                if k % 2 == 1 and k // 2 < UNITS:
                    probs_transpose(k // 2)
                if k % 2 == 0 and k // 2 < UNITS:
                    logits(k // 2)

            def turn_h2(i):
                pe.wait_ge(h2_ready, i + 1)
                for k in range(KC):
                    ins = pe.transpose(ps[:, 2 * i + k // 4, (k % 4) * P:(k % 4 + 1) * P],
                                       h2[:, i, k * P:(k + 1) * P], ident[:])
                ins.then_inc(h2_T, 1)

            def router(i):
                pe.wait_ge(h2T_dve, i + 1)
                pe.wait_ge(h2T_act, i + 1)
                o = ps[:, AUX + i, 0:EXPERTS]
                for k in range(KC):
                    pe.matmul(o, h2T[:, i, k, :], wr[:, k, :], start=(k == 0), stop=False)
                pe.matmul(o, ones[0:1, :], br[:], start=False, stop=True).then_inc(router_done, 1)

            turn_h2(0)
            job("wo3")
            pe.wait_ge(job_done, len(JOBS))
            pe.nop().then_inc(w_used, 2)
            pe.wait_ge(small_in, 48)
            router(0)
            turn_h2(1)
            router(1)
            pe.wait_ge(consts, 11)
            for i in range(NT):
                for half in range(2):
                    pe.matmul(ps[:, 2 * i + half, :], zeros_b[:], ones_b[0:1, 0:1].broadcast_to([1, BANK]), start=True,
                              stop=False, skip_group_check=True)
            pe.wait_ge(mask_b_ready, 2)
            pe.matmul(ps[:, GLU, 0:32], before[:], m_b[:, 0, :], start=True, stop=True)
            pe.matmul(ps[:, GLU, 32:64], ones_b[:], m_b[:, 0, :], start=True, stop=False)
            pe.matmul(ps[:, GLU, 32:64], before[:], m_b[:, 1, :], start=False, stop=True)
            pe.matmul(ps[:, GLU, 64:96], ones_b[:], m_b[:, 0, :], start=True, stop=False)
            pe.matmul(ps[:, GLU, 64:96], ones_b[:], m_b[:, 1, :], start=False, stop=True).then_inc(rank_done, 1)

            def turn_gates():
                pe.wait_ge(gates_ready, 2)
                for i in range(NT):
                    ins = pe.transpose(ps[0:EXPERTS, YB, i * P:(i + 1) * P], gate[:, i, :], ident[:])
                ins.then_inc(gate_T, 1)

            def down_biases():
                pe.wait_ge(gT_ready, 1)
                pe.wait_ge(down_bias_in, 16)
                for i in range(NT):
                    for half in range(2):
                        pe.matmul(ps[:, 2 * i + half, :], gT[:, i * P:(i + 1) * P], bd[:, half * BANK:(half + 1) * BANK],
                                  start=False, stop=False, skip_group_check=True)

            def gather(sems, v):
                pe.wait_ge(sems["onehot_ready"], v)
                for k in range(KC):
                    n = 0
                    for h in part:
                        for i in range(NT):
                            ins = pe.matmul(ps[:, AUX, k * SLOTS:(k + 1) * SLOTS], h[:, i, k * P:(k + 1) * P],
                                            onehot[:, i, :], start=(n == 0), stop=(n == 5))
                            n += 1
                ins.then_inc(sems["gathered"], 1)

            def wait_sixth(first, group, q):
                n = 6 * first + q
                s = (n + EXPERT_SLOT) % RING
                pe.wait_ge(landed[s], 16 * (FRONT_USES[s] + n // RING + 1) + 32 * group)
                return ring[:, s, :]

            main_pass = (main_sems, xg, (GLU, LIN))
            more_pass = (more_sems, xg_o, (AUX, YB))

            def gate_up(passes, first, group):
                for _, _, banks in passes:
                    for j in range(2):
                        for bank, at in zip(banks, (0, FF)):
                            pe.matmul(ps[64 * j:64 * j + 64, bank, :], pick_e[0:96, :],
                                      bias3[:, at + j * BANK:at + (j + 1) * BANK], start=True, stop=False,
                                      skip_group_check=True)
                for k in range(KC):
                    w = wait_sixth(first, group, k // 2) if k % 2 == 0 else w
                    for sems, src, banks in passes:
                        for bank, at in zip(banks, (0, FF)):
                            for j in range(2):
                                o = (k % 2) * 2 * FF + at + j * BANK
                                ins = pe.matmul(ps[64 * j:64 * j + 64, bank, :], src[:, k * SLOTS:(k + 1) * SLOTS],
                                                w[:, o:o + BANK], start=False, stop=(k == KC - 1),
                                                skip_group_check=True)
                        if sems is more_sems and k == KC - 1:
                            ins.then_inc(more_gu_done, 1)
                        if sems is main_sems and k % 2:
                            ins.then_inc(w_used, 1)

            def turn_act(sems, banks, v):
                pe.wait_ge(sems["act_ready"], v)
                for k in range(4):
                    ins = pe.transpose(ps[:, banks[0], k * P:(k + 1) * P], act_v[:, k * P:(k + 1) * P], ident[:])
                ins.then_inc(sems["act_T"], 1)
                pe.wait_ge(sems["sg_ready"], v)
                for i in range(NT):
                    ins = pe.transpose(ps[:, banks[1], i * P:(i + 1) * P], sg[:, i].rearrange("p j s -> p (j s)"), ident[:])
                ins.then_inc(sems["sg_T"], 1)

            def down(sems, bank, first, group, main, v):
                pe.wait_ge(sems["actT_ready"], v)
                for half in range(2):
                    w = wait_sixth(first, group, 4 + half).rearrange("p (k m) -> p k m", m=D)
                    for k in range(4):
                        for j in range(2):
                            ins = pe.matmul(ps[64 * j:64 * j + 64, bank, :],
                                            actT[:, k * P + half * SLOTS:k * P + (half + 1) * SLOTS],
                                            w[:, k, j * BANK:(j + 1) * BANK], start=(half == 0 and k == 0),
                                            stop=(half == 1 and k == 3), skip_group_check=True)
                    if main:
                        ins.then_inc(w_used, 1)
                if not main:
                    ins.then_inc(more_down_done, 1)

            def scatter(sems, src, rows_t, v, last=False):
                pe.wait_ge(sems["y_ready"], v)
                pe.wait_ge(sems["sgT_ready"], v)
                for i in range(NT):
                    for j in range(2):
                        ins = pe.matmul(ps[:, 2 * i + j, :], rows_t[64 * j:64 * j + 64, i * P:(i + 1) * P],
                                        src[64 * j:64 * j + 64, :], start=False, stop=last, skip_group_check=True)
                return ins

            pe.wait_ge(parts_ready, 2)
            gather(main_sems, 1)
            pe.wait_ge(routed, 1)
            pe.wait_ge(bias_moved, 1)
            more = pe.alloc_register("pe_more")
            pe.reg_mov(more, 0)

            def expert(first, group):
                e = pe.snap(first + 3 * group)
                count = pe.value_load(counts[0:1, bass.ds(e, 1)])

                def operands_ready():
                    pe.wait_ge(pick_ready, e + 1)
                    pe.wait_ge(xg_ready, e + 1)
                    if first:
                        pe.wait_ge(sgT_ready, e)

                def further_pass(passes):
                    v = pe.snap(more) + 1
                    gather(more_sems, v)
                    pe.wait_ge(more_sems["xg_ready"], v)
                    if first:
                        pe.wait_ge(y_ready, e)
                    gate_up(passes, first, group)
                    turn_act(more_sems, more_pass[2], v)
                    down(more_sems, AUX, first, group, False, v)
                    scatter(more_sems, y_o, sgT_o, v)
                    pe.reg_add(more, more, 1)

                operands_ready()
                with pe.If(count > SLOTS):
                    with pe.Fori(2, T // SLOTS) as p:
                        with pe.If(count > p * SLOTS):
                            further_pass([more_pass])
                    further_pass([more_pass, main_pass])
                with pe.Else():
                    gate_up([main_pass], first, group)
                if first < EXPERTS - 1:
                    gather(main_sems, e + 2)
                if first:
                    scatter(main_sems, y, sgT, e)
                else:
                    turn_gates()
                turn_act(main_sems, main_pass[2], e + 1)
                if not first:
                    down_biases()
                down(main_sems, YB, first, group, True, e + 1)

            turns(pe, expert)
            scatter(main_sems, y, sgT, EXPERTS, last=True).then_inc(acc_done, 1)


_INS = ['x', 'c', 'w_ada', 'b_ada', 'norm1_g', 'w_in', 'conv_w', 'q_norm_g', 'k_norm_g', 'w_conv_out', 'w_attn_out',
        'w_o', 'norm2_g', 'w_router', 'b_router', 'w_gate_up', 'b_gate_up', 'w_down', 'b_down']


def kernel(**inputs):
    import numpy as _np
    import concourse.bacc as _bacc
    from concourse import mybir as _mybir
    from concourse.bass_utils import run_bass_kernel_spmd as _run

    nc = _bacc.Bacc("TRN2", target_bir_lowering=False, num_devices=1)
    arrays, args = {}, []
    for name in _INS:
        a = _np.ascontiguousarray(inputs[name])
        arrays[f"in_{name}"] = a
        args.append(nc.dram_tensor(f"in_{name}", a.shape, _mybir.dt.from_np(a.dtype), kind="ExternalInput").ap())
    args.append(nc.dram_tensor("out_0", (1, T, D), F32, kind="ExternalOutput").ap())
    hybrid_block(nc, *args)
    r = _run(nc, [arrays], core_ids=[0])
    return r.results[0]["out_0"]
```

```python
from contextlib import ExitStack

import concourse.bass as bass
from concourse import mybir

F32 = mybir.dt.float32
BF16 = mybir.dt.bfloat16
I32 = mybir.dt.int32
U32 = mybir.dt.uint32
ALU = mybir.AluOpType
ACT = mybir.ActivationFunctionType
AX_X = mybir.AxisListType.X

P = 128
D = 1024
T = 256
NT = T // P
KC = D // P
CONV = 512
HEADS = 8
HD = 64
IDX_HEADS = 4
IDX_SCALE = (IDX_HEADS * 64) ** -0.5
CHUNK = 64
TOPK = 64
EXPERTS = 32
ROUTE = 4
FF = 1024
SLOTS = 64
LIMIT = 7.0
ALPHA = 1.702
EPS = 1e-6
NEG = -3.0e38
TAKEN = -3.3e38
UNSEEN = -1.0e30

BANK = 512
RING = 9
FRONT_RING = 6
SLOT = 4096
XIN, GB, GC, Q, K, V, QI, KI, WI, GA, GBR = 0, 512, 1024, 1536, 2048, 2560, 3072, 3328, 3392, 3396, 4420
IN_BLOCK = {"xin": (XIN, 512), "gb": (GB, 512), "gc": (GC, 512), "q": (Q, 512), "k": (K, 512), "v": (V, 512),
            "idx": (QI, GA - QI), "ga0": (GA, 512), "ga1": (GA + 512, 512), "gB0": (GBR, 512), "gB1": (GBR + 512, 512)}
ADA = [("ada", b) for b in range(12)]
STREAM = (ADA[0:4] + [("in", n) for n in ("idx", "q", "k", "v", "xin")]
          + [ADA[4], ("in", "gc"), ADA[5], ("in", "gb"), ADA[6], ("in", "ga0"), ADA[7], ("in", "ga1"),
             ADA[8], ("in", "gB0"), ADA[9], ("in", "gB1"), ADA[10], ("conv_out", 0), ADA[11], ("attn_out", 0),
             ("w_o", 0), ("w_o", 1)])
EARLY_K = 5
ADA_HALF = ["xin0", "xin1", "gc0", "gc1", "gb0", "gb1", "ga0", "ga1", "ga2", "ga3", "gB0", "gB1", "gB2", "gB3"]
ITEM = {item: i for i, item in enumerate(STREAM)}
FRONT_USES = [len([i for i in range(len(STREAM)) if i % FRONT_RING == s]) for s in range(FRONT_RING)] \
    + [0] * (RING - FRONT_RING)

JOBS = (["qi", "kiwi", "q0", "q1", "k0", "k1", "v0", "v1", "xin0", "xin1", "gc0", "gc1", "gb0", "gb1", "mod4", "ga0",
         "mod5", "ga1", "ga2", "ga3", "mod6", "gB0", "mod7", "gB1", "gB2", "gB3", "mod8", "mod9"]
        + [f"pa{n}" for n in range(4)] + [f"pb{n}" for n in range(4)] + [f"wo{n}" for n in range(4)] + ["mod10", "mod11"])
JOB = {name: i for i, name in enumerate(JOBS)}
LAST_JOB = {("in", "idx"): "kiwi", ("in", "q"): "q1", ("in", "k"): "k1", ("in", "v"): "v1", ("in", "xin"): "xin1",
            ("in", "gc"): "gc1", ("in", "gb"): "gb1", ("in", "ga0"): "ga1", ("in", "ga1"): "ga3", ("in", "gB0"): "gB1",
            ("in", "gB1"): "gB3", ("conv_out", 0): "pa3"}
LATE_BLOCKS = 3
EXPERT_SLOT = len(STREAM) % FRONT_RING
UNITS = 2 * 4
FIRST_UNIT_JOB = JOB["xin0"]


def ada_steps_of(b):
    return EARLY_K * (b + 1) if b < 4 else EARLY_K * 4 + KC * (b - 3)


def hybrid_block(nc, x, c, w_ada, b_ada, norm1_g, w_in, conv_w, q_norm_g, k_norm_g, w_conv_out, w_attn_out, w_o,
                 norm2_g, w_router, b_router, w_gate_up, b_gate_up, w_down, b_down, out):
    with ExitStack() as ctx:
        def sb(name, shape, dt=F32):
            return ctx.enter_context(nc.sbuf_tensor(name, shape, dt))

        def sem(name):
            return ctx.enter_context(nc.semaphore(name))

        ps = ctx.enter_context(nc.psum_tensor("ps", [P, 8, BANK], F32))

        ring = sb("ring", [P, RING, SLOT])
        xs = sb("xs", [P, NT, D])
        modacc = sb("modacc", [P, 2, D])
        featT = sb("featT", [P, 2048])
        work = sb("work", [P, 4096])
        g1_row = sb("g1_row", [P, D])
        a2_row = sb("a2_row", [P, D])
        sh2_row = sb("sh2_row", [P, D])
        g2_row = sb("g2_row", [P, D])
        prod = sb("prod", [P, BANK])
        iota = sb("iota", [P, T + 1])
        ident = sb("ident", [P, P])
        ones = sb("ones", [P, P])
        before = sb("before", [P, P], BF16)
        ones_b = sb("ones_b", [P, P], BF16)
        zeros_b = sb("zeros_b", [1, P], BF16)
        pick = sb("pick", [96, EXPERTS])
        small = sb("small", [P, 32])
        wr = sb("wr", [P, KC, EXPERTS])
        br = sb("br", [1, EXPERTS])
        vec = sb("vec", [P, 64])
        rank = sb("rank", [P, NT, EXPERTS])
        gate = sb("gate", [P, NT, EXPERTS])
        counts = sb("counts", [1, EXPERTS], I32)

        ov = ring[:, FRONT_RING:RING, :].rearrange("p s n -> p (s n)")
        xn = ov[:, 0:2048].rearrange("p (i n) -> p i n", i=NT)
        sgA = ov[:, 0:2048].rearrange("p (d t) -> p d t", t=T)
        sgB = ov[:, 2048:4096].rearrange("p (d t) -> p d t", t=T)
        q_tok = ov[:, 4096:5120].rearrange("p (i n) -> p i n", i=NT)
        k_tok = ov[:, 5120:6144].rearrange("p (i n) -> p i n", i=NT)
        v_tok = ov[:, 6144:7168].rearrange("p (i n) -> p i n", i=NT)
        yA = ov[:, 4096:5120].rearrange("p (c t) -> p c t", t=T)
        qT = ov[:, 7168:8192].rearrange("p (c t) -> p c t", t=T)
        kT = ov[:, 8192:9216].rearrange("p (c t) -> p c t", t=T)
        qiT = ov[:, 9216:9728].rearrange("p (c t) -> p c t", t=T)
        kiT = ov[:, 9728:9984]
        gains = ov[:, 9984:10112].rearrange("p (a d) -> p a d", a=2)
        xinS = ov[:, 10112:11136].rearrange("p (c t) -> p c t", t=T)
        conv_u = ov[:, 11136:12168].rearrange("p (c t) -> p c t", t=T + 2)

        rows = prod[0:28, 0:P]
        ada_bias = prod[32:44, :]
        hT = featT[:, :].rearrange("p (c t) -> p c t", t=T)
        mT = hT
        h2T = featT[:, :].rearrange("p (i k t) -> p i k t", i=NT, k=KC)
        relu = work[:, 0:1024].rearrange("p (b h t) -> p b h t", b=2, h=2)
        yB = work[:, 0:1024].rearrange("p (c t) -> p c t", t=T)
        score = work[:, 1024:1536].rearrange("p (i s) -> p i s", i=NT)
        am = work[:, 1536:2048].rearrange("p (i s) -> p i s", i=NT)
        sq = work[:, 2048:2560]
        wi_rows = work[64:64 + IDX_HEADS, 2048:2048 + T]
        lg = work[:, 2048:3072].rearrange("p (b h s) -> p b h s", b=2, h=2)
        pT = work[:, 3072:4096].rearrange("p (b h s t) -> p b h s t", b=2, h=2, s=2)
        h2 = work[:, 0:2048].rearrange("p (i n) -> p i n", i=NT)
        bd = work[0:EXPERTS, 2048:3072]
        bias3 = work[0:96, 3072:4096].bitcast(BF16)
        bias_raw = ov[0:96, 0:2048]
        bias_parts = g2_row[0:96, :].bitcast(BF16)
        ada_rows = work[0:1, 0:2048].rearrange("p (b n) -> p b n", b=4)
        part = [modacc[:, 0, :].bitcast(BF16).rearrange("p (i n) -> p i n", i=NT),
                modacc[:, 1, :].bitcast(BF16).rearrange("p (i n) -> p i n", i=NT),
                g1_row[:, :].bitcast(BF16).rearrange("p (i n) -> p i n", i=NT)]
        gT = prod[0:EXPERTS, 0:T]

        xg = featT[:, 0:512]
        xg_o = featT[:, 512:1024]
        glu = featT[:, 1024:1536]
        sig = featT[:, 1536:2048]
        lin = work[:, 0:512]
        act_v = work[:, 512:1024]
        actT = work[:, 1024:1536]
        y = work[:, 1536:2048]
        y_o = sh2_row[:, 0:512]
        g2_half = g2_row[:, 0:BANK]
        sgT = sh2_row[:, 512:768]
        sgT_o = sh2_row[:, 768:1024]
        sg = a2_row[:, 0:256].rearrange("p (i j s) -> p i j s", i=NT, j=2)
        pick_e = a2_row[:, 256:288].bitcast(BF16)
        actT_o = a2_row[:, 352:864]
        onehot = a2_row[:, 288:352].bitcast(BF16).rearrange("p (i s) -> p i s", i=NT)

        silu_c = vec[:, 0:8]
        sig_c = vec[:, 8:16]
        a1 = vec[:, 16:24]
        sh1 = vec[:, 24:32]
        wi = vec[:, 32:40].rearrange("p (i h) -> p i h", i=NT)
        ms = vec[:, 40:42]
        rstd = vec[:, 42:44]
        neg_max = vec[:, 44:48].rearrange("p (b h) -> p b h", b=2)
        row_sum = vec[:, 48:52].rearrange("p (b h) -> p b h", b=2)
        top8 = vec[:, 52:60]
        hs = sb("hs", [P, 32])
        rt = sb("rt", [P, 64])
        lr = sb("lr", [P, NT, EXPERTS])
        idx8 = sb("idx8", [P, NT, 8], U32)
        m_b = sb("m_b", [P, NT, EXPERTS], BF16)
        hit = prod[:, 0:256].rearrange("p (i k e) -> p i k e", i=NT, k=ROUTE)
        hit_g = prod[:, 0:256].rearrange("p (i k e) -> p i k e", i=NT, k=ROUTE)
        mask = prod[:, 256:320].rearrange("p (i e) -> p i e", i=NT)

        landed = [sem(f"landed{s}") for s in range(RING)]
        last_landed = sem("last_landed")
        w_used = sem("w_used")
        ada_steps = sem("ada_steps")
        ada_row_done = sem("ada_row_done")
        ada_row_out = sem("ada_row_out")
        bias_moved = sem("bias_moved")
        x_in = sem("x_in")
        rows_in = sem("rows_in")
        small_in = sem("small_in")
        gains_in = sem("gains_in")
        down_bias_in = sem("down_bias_in")
        down_bias_ready = sem("down_bias_ready")
        gu_bias_in = sem("gu_bias_in")
        bias_steps = sem("bias_steps")
        consts = sem("consts")
        dve_step = sem("dve_step")
        act_step = sem("act_step")
        rows_T = sem("rows_T")
        rows_out = sem("rows_out")
        sig_c_done = sem("sig_c_done")
        silu_done = sem("silu_done")
        sumsq1 = sem("sumsq1")
        ms1_done = sem("ms1_done")
        std1_done = sem("std1_done")
        rstd1_ready = sem("rstd1_ready")
        xn_ready = sem("xn_ready")
        xT_done = sem("xT_done")
        mod_summed = sem("mod_summed")
        mod1_ready = sem("mod1_ready")
        hT_dve = sem("hT_dve")
        hT_act = sem("hT_act")
        job_done = sem("job_done")
        bank_read = [sem(f"bank_read{b}") for b in range(2)]
        dots_done = sem("dots_done")
        wi_T = sem("wi_T")
        relu_done = sem("relu_done")
        score_done = sem("score_done")
        mask_ready = sem("mask_ready")
        head_ms = sem("head_ms")
        head_std = sem("head_std")
        qk_normed = sem("qk_normed")
        qk_T = sem("qk_T")
        qkT_ready = sem("qkT_ready")
        logits_done = sem("logits_done")
        logits_read = sem("logits_read")
        max_ready = sem("max_ready")
        exp_done = sem("exp_done")
        probs_ready = sem("probs_ready")
        probs_T = sem("probs_T")
        pT_ready = sem("pT_ready")
        pv_done = sem("pv_done")
        yB_ready = sem("yB_ready")
        merged = sem("merged")
        x1_ready = sem("x1_ready")
        sumsq2 = sem("sumsq2")
        ms2_done = sem("ms2_done")
        std2_done = sem("std2_done")
        h2_ready = sem("h2_ready")
        h2_T = sem("h2_T")
        h2T_dve = sem("h2T_dve")
        h2T_act = sem("h2T_act")
        part0 = sem("part0")
        rest0 = sem("rest0")
        part1 = sem("part1")
        parts_ready = sem("parts_ready")
        router_done = sem("router_done")
        top_ready = sem("top_ready")
        top_exp = sem("top_exp")
        mask_b_ready = sem("mask_b_ready")
        gates_ready = sem("gates_ready")
        rank_done = sem("rank_done")
        gate_T = sem("gate_T")
        gT_ready = sem("gT_ready")
        routed = sem("routed")

        onehot_ready = sem("onehot_ready")
        sg_ready = sem("sg_ready")
        pick_ready = sem("pick_ready")
        gathered = sem("gathered")
        xg_ready = sem("xg_ready")
        glu_ready = sem("glu_ready")
        lin_ready = sem("lin_ready")
        prod_ready = sem("prod_ready")
        sig_ready = sem("sig_ready")
        act_ready = sem("act_ready")
        act_T = sem("act_T")
        sg_T = sem("sg_T")
        actT_ready = sem("actT_ready")
        sgT_ready = sem("sgT_ready")
        y_ready = sem("y_ready")
        main_sems = {"onehot_ready": onehot_ready, "sg_ready": sg_ready, "gathered": gathered, "xg_ready": xg_ready,
                     "glu_ready": glu_ready, "lin_ready": lin_ready, "prod_ready": prod_ready, "sig_ready": sig_ready,
                     "act_ready": act_ready, "act_T": act_T, "actT_ready": actT_ready, "sgT_ready": sgT_ready,
                     "y_ready": y_ready, "sg_T": sg_T}
        more_sems = {name: sem("more_" + name) for name in main_sems}
        more_gu_done = sem("more_gu_done")
        more_down_done = sem("more_down_done")
        acc_done = sem("acc_done")
        out_dve = sem("out_dve")
        out_act = sem("out_act")
        out_done = sem("out_done")

        GLU, LIN, AUX, YB = 4, 5, 6, 7

        def slot(item):
            return ring[:, ITEM[item] % FRONT_RING, :]

        def wait_landed(eng, item):
            i = ITEM[item]
            eng.wait_ge(landed[i % FRONT_RING], 16 * (i // FRONT_RING + 1))

        def sixths_used(e, n):
            return e * 6 + (LATE_BLOCKS + n)

        def turns(eng, body):
            body(0, 0)
            with eng.Fori(0, (EXPERTS - 2) // 3) as group:
                for j in range(3):
                    body(1 + j, group)
            body(EXPERTS - 1, 0)

        block = ctx.enter_context(nc.Block())

        @block.sync
        def _(sp):
            sp.dma_start(rows[0:8, :], c.rearrange("b (k p) -> (b k) p", p=P)).then_inc(rows_in, 16)
            sp.dma_start(rows[8:16, :], norm1_g.rearrange("b (k p) -> (b k) p", p=P)).then_inc(rows_in, 16)
            sp.dma_start(rows[16:28, :], conv_w.rearrange("b j (k p) -> (b j k) p", p=P)).then_inc(rows_in, 16)
            sp.dma_start(ada_bias, b_ada.rearrange("b (k n) -> (b k) n", n=BANK)).then_inc(rows_in, 16)
            sp.dma_start(xs[:], x[0].rearrange("(i p) n -> p i n", p=P)).then_inc(x_in, 16)
            for i, (kind, n) in enumerate(STREAM):
                if i >= FRONT_RING:
                    was = STREAM[i - FRONT_RING]
                    if was[0] == "ada":
                        sp.wait_ge(ada_steps, ada_steps_of(was[1]))
                        if was[1] < 4:
                            sp.wait_ge(ada_row_done, was[1] + 1)
                    else:
                        sp.wait_ge(job_done, JOB[LAST_JOB[was]] + 1)
                if kind == "ada":
                    src, m = w_ada[0, :, n * BANK:(n + 1) * BANK], BANK
                elif kind == "in":
                    at, m = IN_BLOCK[n]
                    src = w_in[0, :, at:at + m]
                elif kind == "conv_out":
                    src, m = w_conv_out[0], D
                elif kind == "attn_out":
                    src, m = w_attn_out[0], D
                else:
                    src, m = w_o[0, n * 512:(n + 1) * 512, :], D
                k = src.shape[0] // P
                sp.dma_start(ring[:, i % FRONT_RING, 0:k * m].rearrange("p (k m) -> p k m", m=m),
                             src.rearrange("(k p) m -> p k m", p=P)).then_inc(landed[i % FRONT_RING], 16)

            gu_src = w_gate_up.rearrange("l e (q a p) n -> (l e q) p a n", q=4, p=P)
            dn_src = w_down.rearrange("l e (q a p) n -> (l e q) p a n", q=2, p=P)

            def load_expert(first, group):
                for q in range(6):
                    n = 6 * first + q
                    s = (n + EXPERT_SLOT) % RING
                    if first == 0 and s >= FRONT_RING:
                        if s == FRONT_RING:
                            sp.wait_ge(merged, 4)
                    elif first == 0:
                        was = STREAM[max(i for i in range(len(STREAM)) if i % FRONT_RING == s)]
                        if was[0] == "ada":
                            sp.wait_ge(ada_steps, ada_steps_of(was[1]))
                        else:
                            sp.wait_ge(job_done, JOB[LAST_JOB[was]] + 1)
                    else:
                        sp.wait_ge(w_used, LATE_BLOCKS + 18 * group + n - RING + 1)
                    e = first + 3 * group
                    if q < 4:
                        src = gu_src[e * 4 + q]
                        dst = ring[:, s, :].rearrange("p (a n) -> p a n", a=2)
                    else:
                        src = dn_src[e * 2 + q - 4]
                        dst = ring[:, s, :].rearrange("p (a n) -> p a n", a=4)
                    if first == EXPERTS - 1 and q == 5:
                        sp.dma_start(dst[:, 0:2, :], src[:, 0:2, :]).then_inc(landed[s], 16)
                        sp.dma_start(dst[:, 2:4, :], src[:, 2:4, :]).then_inc(last_landed, 16)
                    else:
                        sp.dma_start(dst, src).then_inc(landed[s], 16)

            turns(sp, load_expert)
            for i in range(NT):
                sp.wait_ge(out_dve, i + 1)
                sp.dma_start(out[0, i * P:(i + 1) * P, 0:BANK], xs[:, i, 0:BANK]).then_inc(out_done, 16)
            sp.wait_ge(out_done, 16 * 2 * NT)

        @block.gpsimd
        def _(pool):
            pool.memset(ident[:], 0.0).then_inc(consts, 1)
            pool.memset(ones[:], 1.0).then_inc(consts, 1)
            pool.memset(ones_b[:], 1.0).then_inc(consts, 1)
            pool.memset(pick[:], 0.0).then_inc(consts, 1)
            pool.memset(zeros_b[:], 0.0).then_inc(consts, 1)
            pool.iota(iota[:], [[1, T + 1]], base=0, channel_multiplier=0,
                      allow_small_or_imprecise_dtypes=True).then_inc(consts, 1)
            pool.wait_ge(consts, 6)
            pool.affine_select(out=ident[:], in_=ident[:], compare_op=ALU.not_equal, fill=1.0, base=0,
                               pattern=[[-1, P]], channel_multiplier=1).then_inc(consts, 1)
            pool.affine_select(out=before[:], in_=ones_b[:], compare_op=ALU.is_gt, fill=0.0, base=0,
                               pattern=[[1, P]], channel_multiplier=-1).then_inc(consts, 1)
            for r in range(3):
                pool.affine_select(out=pick[:], in_=pick[:], compare_op=ALU.not_equal, fill=1.0, base=-32 * r,
                                   pattern=[[-1, EXPERTS]], channel_multiplier=1).then_inc(consts, 1)
                pool.wait_ge(consts, 9 + r)
            pool.wait_ge(xT_done, 1)
            for r in range(3):
                pool.dma_start(bias_raw[32 * r:32 * r + 32, :], b_gate_up[0]).then_inc(gu_bias_in, 16)
            pool.wait_ge(gu_bias_in, 48)
            n = 0
            for r in range(3):
                rs = slice(32 * r, 32 * r + 32)
                for step in range(r + 1):
                    if step:
                        pool.tensor_tensor(bias_raw[rs, :], bias_raw[rs, :], bias_parts[rs, :], ALU.subtract)\
                            .then_inc(bias_steps, 1)
                        n += 1
                        pool.wait_ge(bias_steps, n)
                    pool.tensor_copy(bias_parts[rs, :], bias_raw[rs, :]).then_inc(bias_steps, 1)
                    n += 1
                    pool.wait_ge(bias_steps, n)
            pool.wait_ge(pv_done, UNITS)
            pool.tensor_copy(bias3, bias_parts).then_inc(bias_moved, 1)
            for i in range(NT):
                pool.wait_ge(part0, i + 1)
                pool.wait_ge(h2_T, 2 * i + 2)
                pool.tensor_tensor(h2[:, i, :], h2[:, i, :], part[0][:, i, :], ALU.subtract).then_inc(rest0, 1)
                pool.wait_ge(rest0, i + 1)
                pool.wait_ge(part1, i + 1)
                pool.wait_ge(x1_ready, 4)
                pool.tensor_tensor(part[2][:, i, :], h2[:, i, :], part[1][:, i, :], ALU.subtract)\
                    .then_inc(parts_ready, 1)
            pool.wait_ge(down_bias_in, 16)
            for name in ("mod10", "mod11"):
                pool.wait_ge(bank_read[JOB[name] % 2], JOB[name] // 2 + 1)
            pool.tensor_tensor(bd, bd, g2_row[0:EXPERTS, :], ALU.mult).then_inc(down_bias_ready, 1)

        @block.scalar
        def _(act):
            n_step = [0]

            def step(ins):
                n_step[0] += 1
                ins.then_inc(act_step, 1)
                act.wait_ge(act_step, n_step[0])

            act.wait_ge(rows_out, 1)
            act.activation(sig_c, small[:, 0:8], ACT.Sigmoid).then_inc(sig_c_done, 1)
            act.wait_ge(x_in, 16)
            for i in range(NT):
                act.activation(featT[:, 0:D], xs[:, i, :], ACT.Square, accum_out=ms[:, i:i + 1]).then_inc(sumsq1, 1)
                act.wait_ge(sumsq1, i + 1)
            act.wait_ge(ms1_done, 1)
            act.activation(rstd[:, :], ms[:, :], ACT.Sqrt).then_inc(std1_done, 1)
            act.wait_ge(rstd1_ready, 1)
            for i in range(NT):
                act.activation(xn[:, i, :], xs[:, i, :], ACT.Copy, scale=rstd[:, i:i + 1]).then_inc(xn_ready, 1)
            for b in range(4):
                act.wait_ge(ada_row_done, b + 1)
                act.activation(ada_rows[:, b, :], ps[0:1, 4 + b % 2, :], ACT.Copy).then_inc(ada_row_out, 1)

            act.wait_ge(xT_done, 1)
            act.wait_ge(mod1_ready, 1)
            for k in range(4, KC):
                act.activation(hT[:, k, :], ps[:, k // 2, (k % 2) * T:(k % 2 + 1) * T], ACT.Identity, bias=sh1[:, k:k + 1],
                               scale=a1[:, k:k + 1]).then_inc(hT_act, 1)

            act.dma_start(wr[:], w_router[0].rearrange("(k p) e -> p k e", p=P)).then_inc(small_in, 16)
            act.dma_start(br[:], b_router[0:1, :]).then_inc(small_in, 16)
            act.dma_start(a2_row[:], norm2_g[0:1, :].broadcast_to([P, D])).then_inc(small_in, 16)
            act.dma_start(gains[:, 0, :], q_norm_g[0:1, :].broadcast_to([P, HD])).then_inc(gains_in, 16)
            act.dma_start(gains[:, 1, :], k_norm_g[0:1, :].broadcast_to([P, HD])).then_inc(gains_in, 16)

            def job_copy(name, dst, func=ACT.Copy, scale=1.0):
                j = JOB[name]
                act.wait_ge(job_done, j + 1)
                act.activation(dst, ps[:, 4 + j % 2, :], func, scale=scale).then_inc(bank_read[j % 2], 1)

            def fold(ap):
                return ap.rearrange("p c t -> p (c t)")

            job_copy("qi", fold(qiT))
            j = JOB["kiwi"]
            act.wait_ge(job_done, j + 1)
            for half in range(2):
                step(act.activation(kiT[64 * half:64 * half + 64, :], ps[0:64, 5, 0:T], ACT.Copy))
            act.activation(wi_rows, ps[64:64 + IDX_HEADS, 5, 0:T], ACT.Copy, scale=IDX_SCALE).then_inc(bank_read[1], 1)
            job_copy("q0", q_tok[:, 0, :])
            for i in range(NT):
                w = P * (i + 1)
                act.wait_ge(dots_done, i + 1)
                if i:
                    act.wait_ge(score_done, i)
                for b in range(2):
                    act.activation(relu[:, b, :, 0:w], ps[:, 2 * i + b, :].rearrange("p (h s) -> p h s", h=2)[:, :, 0:w],
                                   ACT.Relu).then_inc(relu_done, 1)
            job_copy("q1", q_tok[:, 1, :])
            for i in range(NT):
                job_copy(f"k{i}", k_tok[:, i, :])
            act.wait_ge(head_ms, 1)
            act.activation(hs[:], hs[:], ACT.Sqrt).then_inc(head_std, 1)
            for i in range(NT):
                job_copy(f"v{i}", v_tok[:, i, :])
            for n, dst in enumerate((qT, qT, kT, kT)):
                act.wait_ge(qk_T, n + 1)
                act.activation(dst[:, :, (n % 2) * P:(n % 2) * P + P], ps[:, n, :].rearrange("p (c t) -> p c t", c=4),
                               ACT.Copy).then_inc(qkT_ready, 1)

            def softmax_exp(u):
                i, w = u // 4, P * (u // 4 + 1)
                act.wait_ge(max_ready, u + 1)
                for h in range(2):
                    act.activation(lg[:, u % 2, h, 0:w], lg[:, u % 2, h, 0:w], ACT.Exp, bias=neg_max[:, u % 2, h:h + 1],
                                   accum_out=row_sum[:, u % 2, h:h + 1]).then_inc(exp_done, 1)

            def probs_T_copy(u):
                n = u // 4 + 1
                act.wait_ge(probs_T, u + 1)
                if u >= 2:
                    act.wait_ge(pv_done, u - 1)
                act.activation(pT[:, u % 2, :, 0:n, :],
                               ps[:, 6, :].rearrange("p (h s t) -> p h s t", h=2, s=2)[:, :, 0:n, :],
                               ACT.Copy).then_inc(pT_ready, 1)

            def pv_copy(u):
                i, hp = u // 4, u % 4
                act.wait_ge(pv_done, u + 1)
                act.activation(yB[:, hp, i * P:(i + 1) * P], ps[:, 7, (u % 2) * P:(u % 2) * P + P], ACT.Copy)\
                   .then_inc(yB_ready, 1)

            for name in JOBS[FIRST_UNIT_JOB:JOB["wo0"]]:
                j = JOB[name]
                n = int(name[-1])
                if name == "ga0":
                    act.wait_ge(bias_steps, 9)
                if name[:-1] == "xin":
                    job_copy(name, fold(xinS[:, 2 * n:2 * n + 2, :]))
                elif name[:-1] == "ga":
                    job_copy(name, fold(sgA[:, 2 * n:2 * n + 2, :]), ACT.Sigmoid)
                elif name[:-1] == "gB":
                    job_copy(name, fold(sgB[:, 2 * n:2 * n + 2, :]), ACT.Sigmoid)
                elif name in ("mod4", "mod5"):
                    job_copy(name, g1_row[:, (n - 4) * BANK:(n - 3) * BANK])
                elif name in ("mod6", "mod7"):
                    job_copy(name, sh2_row[:, (n - 6) * BANK:(n - 5) * BANK])
                k = j - FIRST_UNIT_JOB
                if k >= 2 and k % 2 == 0 and k // 2 - 1 < UNITS:
                    pv_copy(k // 2 - 1)
                if k % 2 == 1 and k // 2 < UNITS:
                    probs_T_copy(k // 2)
                if k % 2 == 0 and k // 2 < UNITS:
                    softmax_exp(k // 2)

            act.wait_ge(pv_done, UNITS)
            act.dma_start(bd, b_down[0]).then_inc(down_bias_in, 16)

            def square_sum(i):
                act.wait_ge(x1_ready, 2 * i + 2)
                act.activation(h2[:, i, :], xs[:, i, :], ACT.Square, accum_out=ms[:, i:i + 1]).then_inc(sumsq2, 1)

            def root(i):
                act.wait_ge(ms2_done, i + 1)
                act.activation(rstd[:, i:i + 1], ms[:, i:i + 1], ACT.Sqrt).then_inc(std2_done, 1)

            def h2T_copy(i):
                act.wait_ge(h2_T, 2 * i + 2)
                act.wait_ge(job_done, JOB["wo3"] + 1)
                act.activation(h2T[:, i, 4:8, :], ps[:, 2 * i + 1, :].rearrange("p (k t) -> p k t", k=4), ACT.Copy)\
                   .then_inc(h2T_act, 1)

            def first_part(i):
                act.wait_ge(h2_ready, 2 * i + 2)
                act.activation(part[0][:, i, :], h2[:, i, :], ACT.Copy).then_inc(part0, 1)

            def second_part(i):
                act.wait_ge(rest0, i + 1)
                act.activation(part[1][:, i, :], h2[:, i, :], ACT.Copy).then_inc(part1, 1)

            square_sum(0)
            root(0)
            first_part(0)
            square_sum(1)
            h2T_copy(0)
            root(1)
            act.wait_ge(bias_moved, 1)
            job_copy("mod10", g2_row[:, 0:BANK])
            act.wait_ge(bank_read[JOB["mod10"] % 2], JOB["mod10"] // 2 + 1)
            act.wait_ge(job_done, JOB["mod11"] + 1)
            step(act.activation(g2_row[64:128, 0:BANK], ps[64:128, 4 + JOB["mod11"] % 2, :], ACT.Copy))
            job_copy("mod11", g2_row[:, BANK:D])
            second_part(0)
            first_part(1)
            h2T_copy(1)
            second_part(1)
            for i in range(NT):
                act.wait_ge(top_ready, i + 1)
                act.activation(rt[:, 16 + 4 * i:20 + 4 * i], rt[:, 8 * i:8 * i + 4], ACT.Exp,
                               bias=rt[:, 24 + i:25 + i], accum_out=rt[:, 26 + i:27 + i]).then_inc(top_exp, 1)

            def evacuate_gather(sems, dst, v):
                act.wait_ge(sems["gathered"], v)
                act.activation(dst, ps[:, AUX, :], ACT.Copy).then_inc(sems["xg_ready"], 1)

            def gate_sigmoid(sems, v):
                act.wait_ge(sems["glu_ready"], v)
                act.activation(sig, glu, ACT.Sigmoid, scale=ALPHA).then_inc(sems["sig_ready"], 1)

            def evacuate_transposes(sems, banks, act_dst, dst, v):
                act.wait_ge(sems["act_T"], v)
                act.activation(act_dst, ps[:, banks[0], :], ACT.Copy).then_inc(sems["actT_ready"], 1)
                act.wait_ge(sems["sg_T"], v)
                act.activation(dst, ps[:, banks[1], 0:T], ACT.Copy).then_inc(sems["sgT_ready"], 1)

            evacuate_gather(main_sems, xg, 1)
            more = act.alloc_register("act_more")
            act.reg_mov(more, 0)

            def expert(first, group):
                e = act.snap(first + 3 * group)
                count = act.value_load(counts[0:1, bass.ds(e, 1)])

                def further_pass(joint):
                    v = act.snap(more) + 1
                    evacuate_gather(more_sems, xg_o, v)
                    gate_sigmoid(more_sems, v)
                    if joint:
                        gate_sigmoid(main_sems, e + 1)
                    evacuate_transposes(more_sems, (AUX, YB), actT_o, sgT_o, v)
                    act.reg_add(more, more, 1)

                def next_gather():
                    if first < EXPERTS - 1:
                        evacuate_gather(main_sems, xg, e + 2)

                with act.If(count > SLOTS):
                    with act.Fori(2, T // SLOTS) as p:
                        with act.If(count > p * SLOTS):
                            further_pass(False)
                    further_pass(True)
                    evacuate_transposes(main_sems, (GLU, LIN), actT, sgT, e + 1)
                    next_gather()
                with act.Else():
                    gate_sigmoid(main_sems, e + 1)
                    next_gather()
                    evacuate_transposes(main_sems, (GLU, LIN), actT, sgT, e + 1)

            act.wait_ge(routed, 1)
            turns(act, expert)
            for i in range(NT):
                act.wait_ge(acc_done, 2 * i + 2)
                act.activation(xs[:, i, BANK:D], ps[:, 2 * i + 1, :], ACT.Copy).then_inc(out_act, 1)
                act.wait_ge(out_act, i + 1)
                act.dma_start(out[0, i * P:(i + 1) * P, BANK:D], xs[:, i, BANK:D]).then_inc(out_done, 16)

        @block.vector
        def _(dve):
            n_step = [0]

            def step(ins):
                n_step[0] += 1
                ins.then_inc(dve_step, 1)
                dve.wait_ge(dve_step, n_step[0])

            def ada_block(b, lo, hi):
                if lo == 0:
                    if b in (4, 6):
                        dve.wait_ge(mod_summed, b - 2)
                    elif b in (8, 10):
                        dve.wait_ge(job_done, JOB[f"mod{b - 3}"] + 1)
                    wait_landed(dve, ("ada", b))
                acc = modacc[:, (b // 2) % 2, (b % 2) * BANK:(b % 2 + 1) * BANK]
                for k in range(lo, hi):
                    w = slot(("ada", b))[:, k * BANK:(k + 1) * BANK]
                    if k == 0:
                        ins = dve.tensor_scalar(acc, w, silu_c[:, 0:1], None, ALU.mult)
                    else:
                        ins = dve.scalar_tensor_tensor(out=acc, in0=w, scalar=silu_c[:, k:k + 1], in1=acc,
                                                       op0=ALU.mult, op1=ALU.add)
                    ins.then_inc(ada_steps, 1)
                    dve.wait_ge(ada_steps, (ada_steps_of(b - 1) if b else 0) + k + 1)
                    if k == 0:
                        acc12 = acc[32:44, :]
                        step(dve.scalar_tensor_tensor(out=acc12, in0=ada_bias, scalar=ident[32:44, 32 + b:33 + b],
                                                      in1=acc12, op0=ALU.mult, op1=ALU.add))

            dve.memset(conv_u[:, :, 0:2], 0.0)
            dve.wait_ge(rows_T, 1)
            dve.tensor_copy(small[:, 0:28], ps[:, 7, 0:28]).then_inc(rows_out, 1)
            dve.wait_ge(sig_c_done, 1)
            dve.wait_ge(rows_out, 1)
            dve.tensor_tensor(silu_c, small[:, 0:8], sig_c, ALU.mult).then_inc(silu_done, 1)
            dve.wait_ge(silu_done, 1)
            dve.wait_ge(sumsq1, 2)
            dve.tensor_scalar(ms[:, :], ms[:, :], 1.0 / D, EPS, ALU.mult, ALU.add).then_inc(ms1_done, 1)
            dve.wait_ge(std1_done, 1)
            dve.reciprocal(rstd[:, :], rstd[:, :]).then_inc(rstd1_ready, 1)
            dve.wait_ge(consts, 7)
            for b in range(4):
                ada_block(b, 0, EARLY_K)
            dve.wait_ge(mod_summed, 4)
            step(dve.tensor_copy(sh1, ps[:, 7, 32:40]))
            dve.scalar_tensor_tensor(out=a1, in0=ps[:, 7, 40:48], scalar=1.0, in1=small[:, 8:16], op0=ALU.add,
                                     op1=ALU.mult).then_inc(mod1_ready, 1)
            dve.wait_ge(mod1_ready, 1)
            dve.wait_ge(xT_done, 1)
            for k in range(4):
                dve.tensor_scalar(hT[:, k, :], ps[:, k // 2, (k % 2) * T:(k % 2 + 1) * T], a1[:, k:k + 1], sh1[:, k:k + 1], ALU.mult,
                                  ALU.add).then_inc(hT_dve, 1)

            dve.wait_ge(wi_T, 1)
            step(dve.tensor_copy(vec[:, 32:40], ps[:, 6, 0:NT * IDX_HEADS]))
            for i in range(NT):
                w = P * (i + 1)
                dve.wait_ge(relu_done, 2 * i + 2)
                s = score[:, i, 0:w]
                step(dve.tensor_scalar(s, relu[:, 0, 0, 0:w], wi[:, i, 0:1], None, ALU.mult))
                for h in range(1, IDX_HEADS):
                    ins = dve.scalar_tensor_tensor(out=s, in0=relu[:, h % 2, h // 2, 0:w], scalar=wi[:, i, h:h + 1],
                                                   in1=s, op0=ALU.mult, op1=ALU.add)
                    if h < IDX_HEADS - 1:
                        step(ins)
                ins.then_inc(score_done, 1)
                dve.wait_ge(score_done, i + 1)
                step(dve.memset(score[0:CHUNK, i, w - CHUNK:w], NEG))
                for r in range(TOPK // 8):
                    step(dve.max(top8, s))
                    step(dve.match_replace(s, top8, s, TAKEN))
                dve.tensor_scalar(am[:, i, 0:w], s, (NEG + TAKEN) / 2, UNSEEN, ALU.is_gt, ALU.mult)\
                   .then_inc(mask_ready, 1)

            for n, (name, src) in enumerate((("q0", q_tok), ("q1", q_tok), ("k0", k_tok), ("k1", k_tok))):
                j = JOB[name]
                dve.wait_ge(bank_read[j % 2], j // 2 + 1)
                step(dve.tensor_tensor(sq, src[:, n % 2, :], src[:, n % 2, :], ALU.mult))
                step(dve.tensor_reduce(hs[:, 8 * n:8 * n + 8], sq.rearrange("p (h d) -> p h d", h=HEADS), AX_X, ALU.add))
            dve.tensor_scalar(hs[:], hs[:], 1.0 / HD, EPS, ALU.mult, ALU.add).then_inc(head_ms, 1)
            dve.wait_ge(head_std, 1)
            step(dve.reciprocal(hs[:], hs[:]))
            dve.wait_ge(gains_in, 32)
            for n, src in enumerate((q_tok, q_tok, k_tok, k_tok)):
                v = src[:, n % 2, :].rearrange("p (h d) -> p h d", h=HEADS)
                step(dve.tensor_tensor(v, v, hs[:, 8 * n:8 * n + 8].unsqueeze(2).broadcast_to([P, HEADS, HD]), ALU.mult))
                dve.tensor_tensor(v, v, gains[:, n // 2, :].unsqueeze(1).broadcast_to([P, HEADS, HD]), ALU.mult)\
                   .then_inc(qk_normed, 1)

            def softmax_max(u):
                i, w, b = u // 4, P * (u // 4 + 1), u % 2
                dve.wait_ge(logits_done, u + 1)
                if u >= 2:
                    dve.wait_ge(probs_T, u - 1)
                dve.scalar_tensor_tensor(out=lg[:, b, :, 0:w], in0=ps[:, 2 * b:2 * b + 2, 0:w], scalar=HD ** -0.5,
                                         in1=am[:, i, 0:w].unsqueeze(1).broadcast_to([P, 2, w]), op0=ALU.mult,
                                         op1=ALU.add).then_inc(logits_read, 1)
                dve.wait_ge(logits_read, u + 1)
                dve.tensor_reduce(neg_max[:, b, :], lg[:, b, :, 0:w], AX_X, ALU.max, negate=True)\
                   .then_inc(max_ready, 1)

            def softmax_scale(u):
                w, b = P * (u // 4 + 1), u % 2
                dve.wait_ge(exp_done, 2 * u + 2)
                step(dve.reciprocal(row_sum[:, b, :], row_sum[:, b, :]))
                dve.tensor_tensor(lg[:, b, :, 0:w], lg[:, b, :, 0:w],
                                  row_sum[:, b, :].unsqueeze(2).broadcast_to([P, 2, w]), ALU.mult)\
                   .then_inc(probs_ready, 1)

            def conv(n):
                j = JOB[f"gc{n}"]
                dve.wait_ge(job_done, j + 1)
                jx = JOB[f"xin{n}"]
                dve.wait_ge(bank_read[jx % 2], jx // 2 + 1)
                dve.tensor_tensor(conv_u[:, 2 * n:2 * n + 2, 2:T + 2],
                                  ps[:, 4 + j % 2, :].rearrange("p (c t) -> p c t", c=2),
                                  xinS[:, 2 * n:2 * n + 2, :], ALU.mult).then_inc(bank_read[j % 2], 1)
                dve.wait_ge(bank_read[j % 2], j // 2 + 1)
                if n == 0:
                    dve.wait_ge(qk_T, 4)
                for cc in (2 * n, 2 * n + 1):
                    step(dve.tensor_scalar(yA[:, cc, :], conv_u[:, cc, 0:T], small[:, 16 + cc:17 + cc], None, ALU.mult))
                    for tap in (1, 2):
                        step(dve.scalar_tensor_tensor(out=yA[:, cc, :], in0=conv_u[:, cc, tap:T + tap],
                                                      scalar=small[:, 16 + 4 * tap + cc:17 + 4 * tap + cc],
                                                      in1=yA[:, cc, :], op0=ALU.mult, op1=ALU.add))

            for name in JOBS[FIRST_UNIT_JOB:JOB["pa0"]]:
                j = JOB[name]
                n = int(name[-1])
                bank = ps[:, 4 + j % 2, :]
                if name[:-1] == "gc":
                    conv(n)
                if name[:-1] == "gb":
                    dve.wait_ge(job_done, j + 1)
                    dve.tensor_tensor(yA[:, 2 * n:2 * n + 2, :], bank.rearrange("p (c t) -> p c t", c=2),
                                      yA[:, 2 * n:2 * n + 2, :], ALU.mult).then_inc(bank_read[j % 2], 1)
                if name in ("mod8", "mod9"):
                    a2 = a2_row[:, (n - 8) * BANK:(n - 7) * BANK]
                    dve.wait_ge(job_done, j + 1)
                    dve.wait_ge(small_in, 48)
                    dve.scalar_tensor_tensor(out=a2, in0=bank, scalar=1.0, in1=a2, op0=ALU.add, op1=ALU.mult)\
                       .then_inc(bank_read[j % 2], 1)
                k = j - FIRST_UNIT_JOB
                if k % 2 == 0 and k // 2 < UNITS:
                    softmax_max(k // 2)
                    softmax_scale(k // 2)
                if name in ADA_HALF:
                    b, half = divmod(ADA_HALF.index(name), 2)
                    ada_block(4 + b, 4 * half, 4 * half + 4)

            for n in range(4):
                j = JOB[f"pa{n}"]
                jg = JOB[f"ga{n}"]
                dve.wait_ge(job_done, j + 1)
                dve.wait_ge(bank_read[jg % 2], jg // 2 + 1)
                dve.tensor_tensor(mT[:, 2 * n:2 * n + 2, :].rearrange("p c t -> p (c t)"), ps[:, 4 + j % 2, :],
                                  sgA[:, 2 * n:2 * n + 2, :].rearrange("p c t -> p (c t)"), ALU.mult)\
                   .then_inc(bank_read[j % 2], 1)
                ada_block(11, 2 * n, 2 * n + 2)
            for n in range(4):
                j = JOB[f"pb{n}"]
                jg = JOB[f"gB{n}"]
                s = sgB[:, 2 * n:2 * n + 2, :].rearrange("p c t -> p (c t)")
                m = mT[:, 2 * n:2 * n + 2, :].rearrange("p c t -> p (c t)")
                dve.wait_ge(job_done, j + 1)
                dve.wait_ge(bank_read[jg % 2], jg // 2 + 1)
                dve.tensor_tensor(s, ps[:, 4 + j % 2, :], s, ALU.mult).then_inc(bank_read[j % 2], 1)
                dve.wait_ge(bank_read[j % 2], j // 2 + 1)
                dve.tensor_tensor(m, m, s, ALU.add).then_inc(merged, 1)
            dve.wait_ge(bank_read[1], JOB["mod5"] // 2 + 1)
            def residual(n):
                i, half = n // 2, n % 2
                j = JOB[f"wo{n}"]
                cols = slice(half * BANK, (half + 1) * BANK)
                dve.wait_ge(job_done, j + 1)
                if n:
                    dve.wait_ge(x1_ready, n)
                dve.tensor_tensor(prod[:], ps[:, 4 + j % 2, :], g1_row[:, cols], ALU.mult).then_inc(bank_read[j % 2], 1)
                dve.wait_ge(bank_read[j % 2], j // 2 + 1)
                dve.tensor_tensor(xs[:, i, cols], xs[:, i, cols], prod[:], ALU.add).then_inc(x1_ready, 1)

            def norm2_ms(i):
                dve.wait_ge(sumsq2, i + 1)
                dve.tensor_scalar(ms[:, i:i + 1], ms[:, i:i + 1], 1.0 / D, EPS, ALU.mult, ALU.add).then_inc(ms2_done, 1)

            def norm2_rows(i):
                dve.wait_ge(std2_done, i + 1)
                step(dve.reciprocal(rstd[:, i:i + 1], rstd[:, i:i + 1]))
                for half in range(2):
                    cols = slice(half * BANK, (half + 1) * BANK)
                    step(dve.scalar_tensor_tensor(out=h2[:, i, cols], in0=xs[:, i, cols], scalar=rstd[:, i:i + 1],
                                                  in1=a2_row[:, cols], op0=ALU.mult, op1=ALU.mult))
                    dve.tensor_tensor(h2[:, i, cols], h2[:, i, cols], sh2_row[:, cols], ALU.add).then_inc(h2_ready, 1)

            def h2T_copy(i):
                dve.wait_ge(h2_T, 2 * i + 1)
                dve.wait_ge(job_done, JOB["wo3"] + 1)
                dve.tensor_copy(h2T[:, i, 0:4, :], ps[:, 2 * i, :].rearrange("p (k t) -> p k t", k=4))\
                   .then_inc(h2T_dve, 1)

            idxf = rt[:, 28:36].rearrange("p (i k) -> p i k", i=NT)

            def route(i):
                dve.wait_ge(router_done, i + 1)
                step(dve.tensor_copy(lr[:, i, :], ps[:, AUX + i, 0:EXPERTS]))
                step(dve.max(rt[:, 8 * i:8 * i + 8], lr[:, i, :]))
                dve.tensor_scalar(rt[:, 24 + i:25 + i], rt[:, 8 * i:8 * i + 1], -1.0, None, ALU.mult)\
                   .then_inc(top_ready, 1)
                step(dve.max_index(idx8[:, i, :], rt[:, 8 * i:8 * i + 8], lr[:, i, :]))
                step(dve.tensor_copy(idxf[:, i, :], idx8[:, i, 0:ROUTE]))
                step(dve.tensor_tensor(hit[:, i], iota[:, 0:EXPERTS].unsqueeze(1).broadcast_to([P, ROUTE, EXPERTS]),
                                       idxf[:, i, :].unsqueeze(2).broadcast_to([P, ROUTE, EXPERTS]), ALU.is_equal))
                step(dve.tensor_reduce(mask[:, i, :], hit[:, i].rearrange("p k e -> p e k"), AX_X, ALU.add))
                dve.tensor_copy(m_b[:, i, :], mask[:, i, :]).then_inc(mask_b_ready, 1)

            dve.wait_ge(consts, 11)
            residual(0)
            residual(1)
            norm2_ms(0)
            norm2_rows(0)
            residual(2)
            residual(3)
            h2T_copy(0)
            norm2_ms(1)
            norm2_rows(1)
            route(0)
            h2T_copy(1)
            route(1)
            dve.wait_ge(rank_done, 1)
            step(dve.scalar_tensor_tensor(out=rank[:], in0=ps[:, GLU, 0:NT * EXPERTS].rearrange("p (i e) -> p i e", i=NT),
                                          scalar=1.0, in1=mask, op0=ALU.add, op1=ALU.mult))

            def build_onehot(sems, e, lo):
                for i in range(NT):
                    ins = dve.tensor_scalar(onehot[:, i, :], iota[:, lo], rank[:, i, bass.ds(e, 1)], None, ALU.is_equal)
                ins.then_inc(sems["onehot_ready"], 1)

            def build_scatter(sems, e, lo):
                for i in range(NT):
                    ins = dve.tensor_scalar(sg[:, i], iota[:, lo].unsqueeze(1).broadcast_to([P, 2, SLOTS]),
                                            rank[:, i, bass.ds(e, 1)], gate[:, i, bass.ds(e, 1)], ALU.is_equal, ALU.mult)
                ins.then_inc(sems["sg_ready"], 1)

            def pick_expert(e):
                dve.tensor_copy(pick_e[0:96, :], pick[:, bass.ds(e, 1)].broadcast_to([96, SLOTS])).then_inc(pick_ready, 1)

            def swiglu_factors(sems, banks, v):
                dve.tensor_scalar(glu, ps[:, banks[0], :], LIMIT, None, ALU.min).then_inc(sems["glu_ready"], 1)
                dve.tensor_scalar(lin, ps[:, banks[1], :], LIMIT, -LIMIT, ALU.min, ALU.max).then_inc(sems["lin_ready"], 1)
                dve.wait_ge(sems["glu_ready"], v)
                dve.wait_ge(sems["lin_ready"], v)
                dve.scalar_tensor_tensor(out=lin, in0=lin, scalar=1.0, in1=glu, op0=ALU.add, op1=ALU.mult)\
                   .then_inc(sems["prod_ready"], 1)

            def swiglu_product(sems, v):
                dve.wait_ge(sems["prod_ready"], v)
                dve.wait_ge(sems["sig_ready"], v)
                dve.tensor_tensor(act_v, lin, sig, ALU.mult).then_inc(sems["act_ready"], 1)

            def evacuate_y(sems, bank, dst):
                dve.tensor_tensor(dst, ps[:, bank, :], g2_half, ALU.mult).then_inc(sems["y_ready"], 1)

            first_places = slice(1, SLOTS + 1)
            build_onehot(main_sems, 0, first_places)
            step(dve.tensor_copy(counts[:], ps[0:1, GLU, NT * EXPERTS:(NT + 1) * EXPERTS]))
            pick_expert(0)
            dve.wait_ge(pick_ready, 1)
            dve.nop().then_inc(routed, 1)
            dve.wait_ge(top_exp, NT)
            step(dve.reciprocal(rt[:, 26:28], rt[:, 26:28]))
            for i in range(NT):
                step(dve.tensor_scalar(rt[:, 16 + 4 * i:20 + 4 * i], rt[:, 16 + 4 * i:20 + 4 * i], rt[:, 26 + i:27 + i],
                                       None, ALU.mult))
                step(dve.tensor_tensor(hit_g[:, i], hit[:, i],
                                       rt[:, 16 + 4 * i:20 + 4 * i].unsqueeze(2).broadcast_to([P, ROUTE, EXPERTS]),
                                       ALU.mult))
                dve.tensor_reduce(gate[:, i, :], hit_g[:, i].rearrange("p k e -> p e k"), AX_X, ALU.add)\
                   .then_inc(gates_ready, 1)
            dve.wait_ge(gates_ready, 2)
            more = dve.alloc_register("dve_more")
            dve.reg_mov(more, 0)

            def expert(first, group):
                e = dve.snap(first + 3 * group)
                count = dve.value_load(counts[0:1, bass.ds(e, 1)])

                def buffers_free():
                    dve.wait_ge(gathered, e + 1)
                    if first:
                        dve.wait_ge(sg_T, e)

                def next_onehot():
                    if first < EXPERTS - 1:
                        build_onehot(main_sems, e + 1, first_places)

                def tables_and_swiglu(lo, v):
                    buffers_free()
                    build_onehot(more_sems, e, lo)
                    build_scatter(more_sems, e, lo)
                    dve.wait_ge(more_gu_done, v)
                    swiglu_factors(more_sems, (AUX, YB), v)
                    swiglu_product(more_sems, v)

                with dve.If(count > SLOTS):
                    with dve.Fori(2, T // SLOTS) as p:
                        with dve.If(count > p * SLOTS):
                            v = dve.snap(more) + 1
                            tables_and_swiglu(bass.ds(p * SLOTS + 1, SLOTS), v)
                            dve.wait_ge(more_down_done, v)
                            evacuate_y(more_sems, AUX, y_o)
                            dve.reg_add(more, more, 1)
                    v = dve.snap(more) + 1
                    tables_and_swiglu(slice(SLOTS + 1, 2 * SLOTS + 1), v)
                    dve.wait_ge(more_sems["act_ready"], v)
                    dve.wait_ge(w_used, sixths_used(e, 4))
                    swiglu_factors(main_sems, (GLU, LIN), e + 1)
                    dve.wait_ge(more_sems["act_T"], v)
                    swiglu_product(main_sems, e + 1)
                    dve.wait_ge(more_sems["sg_T"], v)
                    build_scatter(main_sems, e, first_places)
                    next_onehot()
                    dve.reg_add(more, more, 1)
                with dve.Else():
                    buffers_free()
                    next_onehot()
                    build_scatter(main_sems, e, first_places)
                    dve.wait_ge(w_used, sixths_used(e, 4))
                    swiglu_factors(main_sems, (GLU, LIN), e + 1)
                    swiglu_product(main_sems, e + 1)
                if first < EXPERTS - 1:
                    pick_expert(e + 1)
                if not first:
                    dve.wait_ge(gate_T, 1)
                    dve.tensor_copy(gT, ps[0:EXPERTS, YB, 0:T]).then_inc(gT_ready, 1)
                with dve.If(count > SLOTS):
                    v = dve.snap(more)
                    dve.wait_ge(more_down_done, v)
                    evacuate_y(more_sems, AUX, y_o)
                dve.wait_ge(w_used, sixths_used(e, 6))
                evacuate_y(main_sems, YB, y)

            turns(dve, expert)
            for i in range(NT):
                dve.wait_ge(acc_done, 2 * i + 1)
                dve.tensor_copy(xs[:, i, 0:BANK], ps[:, 2 * i, :]).then_inc(out_dve, 1)

        @block.tensor
        def _(pe):
            def wait_bank(j):
                if j >= 2:
                    pe.wait_ge(bank_read[j % 2], j // 2)

            def feature_job(name, cols, item, src=hT, kc=KC, m=BANK):
                j = JOB[name]
                wait_bank(j)
                wait_landed(pe, item)
                w = slot(item)[:, 0:kc * m].rearrange("p (k m) -> p k m", m=m)
                for n, at in enumerate(cols):
                    for k in range(kc):
                        ins = pe.matmul(ps[:, 4 + j % 2, n * T:(n + 1) * T], w[:, k, at:at + P], src[:, k, :],
                                        start=(k == 0), stop=(k == kc - 1))
                return ins

            def finish(ins):
                ins.then_inc(job_done, 1)

            def keep_clock(bank, n):
                for _ in range(n):
                    pe.matmul(ps[:, bank, :], ones_b[:], ones_b[:, 0:1].broadcast_to([P, BANK]), start=True, stop=True,
                              skip_group_check=True)

            pe.wait_ge(consts, 7)
            pe.wait_ge(rows_in, 64)
            pe.transpose(ps[:, 7, 0:28], rows, ident[0:28, 0:28]).then_inc(rows_T, 1)
            pe.wait_ge(xn_ready, 2)
            for k in range(KC):
                for i in range(NT):
                    ins = pe.transpose(ps[:, k // 2, (k % 2) * T + i * P:(k % 2) * T + (i + 1) * P],
                                       xn[:, i, k * P:(k + 1) * P], ident[:])
            ins.then_inc(xT_done, 1)
            pe.wait_ge(silu_done, 1)
            pe.wait_ge(rows_out, 1)

            def turn_row(b):
                pe.wait_ge(ada_row_out, b + 1)
                for k in range(4):
                    o = 32 + 4 * b + k
                    ins = pe.matmul(ps[:, 7, o:o + 1], ada_rows[:, b, k * P:(k + 1) * P], ones[0:1, 0:1], start=True,
                                    stop=True)
                ins.then_inc(mod_summed, 1)

            for b in range(4):
                wait_landed(pe, ("ada", b))
                for k in range(EARLY_K, KC):
                    pe.matmul(ps[0:1, 4 + b % 2, :], silu_c[:, k:k + 1], slot(("ada", b))[:, k * BANK:(k + 1) * BANK],
                              start=(k == EARLY_K), stop=False)
                if b:
                    turn_row(b - 1)
                if b >= 2:
                    keep_clock(6, 5)
                pe.wait_ge(ada_steps, ada_steps_of(b))
                pe.matmul(ps[0:1, 4 + b % 2, :], ones[:, 0:1], modacc[:, b // 2, (b % 2) * BANK:(b % 2 + 1) * BANK],
                          start=False, stop=True).then_inc(ada_row_done, 1)
            keep_clock(6, 4)
            turn_row(3)
            keep_clock(6, 12)
            pe.wait_ge(hT_dve, 4)
            pe.wait_ge(hT_act, 4)

            def job(name):
                j = JOB[name]
                bank = ps[:, 4 + j % 2, :]
                n = int(name[-1]) if name[-1].isdigit() else 0
                if name == "qi":
                    finish(feature_job(name, (0, P), item=("in", "idx"), m=GA - QI))
                elif name == "kiwi":
                    wait_bank(j)
                    w = slot(("in", "idx"))[:, 0:KC * (GA - QI)].rearrange("p (k m) -> p k m", m=GA - QI)
                    for k in range(KC):
                        ins = pe.matmul(bank[0:64 + IDX_HEADS, 0:T], w[:, k, KI - QI:WI - QI + IDX_HEADS], hT[:, k, :],
                                        start=(k == 0), stop=(k == KC - 1))
                    finish(ins)
                elif name[0] in "qkv":
                    item = ("in", name[0])
                    wait_bank(j)
                    wait_landed(pe, item)
                    w = slot(item).rearrange("p (k m) -> p k m", m=BANK)
                    for k in range(KC):
                        ins = pe.matmul(bank, hT[:, k, n * P:(n + 1) * P], w[:, k, :], start=(k == 0), stop=(k == KC - 1))
                    finish(ins)
                elif name[:-1] in ("xin", "gc", "gb"):
                    finish(feature_job(name, (2 * n * P, (2 * n + 1) * P), item=("in", name[:-1])))
                elif name[:-1] in ("ga", "gB"):
                    m = n % 2
                    finish(feature_job(name, (2 * m * P, (2 * m + 1) * P), item=("in", f"{name[:-1]}{n // 2}")))
                elif name[:3] == "mod":
                    b = int(name[3:])
                    wait_bank(j)
                    pe.wait_ge(ada_steps, ada_steps_of(b))
                    finish(pe.matmul(bank, ones[:], modacc[:, (b // 2) % 2, (b % 2) * BANK:(b % 2 + 1) * BANK],
                                     start=True, stop=True))
                elif name[:2] in ("pa", "pb"):
                    if name == "pa0":
                        pe.wait_ge(bank_read[0], JOB["gb0"] // 2 + 1)
                        pe.wait_ge(bank_read[1], JOB["gb1"] // 2 + 1)
                    if name == "pb0":
                        pe.wait_ge(yB_ready, UNITS)
                    finish(feature_job(name, (2 * n * P, (2 * n + 1) * P), src=yA if name[1] == "a" else yB, kc=4,
                                       item=("conv_out", 0) if name[1] == "a" else ("attn_out", 0), m=D))
                else:
                    i, half = n // 2, n % 2
                    wait_bank(j)
                    for k in range(KC):
                        if n == 0 and k % 2 == 0:
                            pe.wait_ge(merged, k // 2 + 1)
                        if n == 0 and k % 4 == 0:
                            wait_landed(pe, ("w_o", k // 4))
                        w = slot(("w_o", k // 4)).rearrange("p (k m) -> p k m", m=D)
                        ins = pe.matmul(bank, mT[:, k, i * P:(i + 1) * P], w[:, k % 4, half * BANK:(half + 1) * BANK],
                                        start=(k == 0), stop=(k == KC - 1))
                        if n == 0 and k == 0:
                            ins.then_inc(w_used, 1)
                    finish(ins)

            job("qi")
            job("kiwi")
            job("q0")
            pe.wait_ge(bank_read[0], 1)
            pe.wait_ge(bank_read[1], 1)
            for i in range(NT):
                w = P * (i + 1)
                for h in range(IDX_HEADS):
                    half = slice(64 * (h % 2), 64 * (h % 2) + 64)
                    ins = pe.matmul(ps[:, 2 * i + h % 2, (h // 2) * T:(h // 2) * T + w], qiT[half, h // 2, i * P:(i + 1) * P],
                                    kiT[half, 0:w], start=True, stop=True, skip_group_check=True)
                ins.then_inc(dots_done, 1)
            for i in range(NT):
                ins = pe.transpose(ps[:, 6, IDX_HEADS * i:IDX_HEADS * (i + 1)], wi_rows[:, i * P:(i + 1) * P],
                                   ident[64:64 + IDX_HEADS, 64:64 + IDX_HEADS])
            ins.then_inc(wi_T, 1)
            for name in ("q1", "k0", "k1", "v0", "v1"):
                job(name)
            pe.wait_ge(relu_done, 4)
            for n, src in enumerate((q_tok, q_tok, k_tok, k_tok)):
                pe.wait_ge(qk_normed, n + 1)
                for hp in range(4):
                    ins = pe.transpose(ps[:, n, hp * P:(hp + 1) * P], src[:, n % 2, hp * P:(hp + 1) * P], ident[:])
                ins.then_inc(qk_T, 1)

            def logits(u):
                i, hp, w, b = u // 4, u % 4, P * (u // 4 + 1), u % 2
                if u == 0:
                    pe.wait_ge(qkT_ready, 4)
                    pe.wait_ge(mask_ready, 2)
                if u >= 2:
                    pe.wait_ge(logits_read, u - 1)
                for h in range(2):
                    half = slice(64 * h, 64 * h + 64)
                    ins = pe.matmul(ps[:, 2 * b + h, 0:w], qT[half, hp, i * P:(i + 1) * P], kT[half, hp, 0:w],
                                    start=True, stop=True)
                ins.then_inc(logits_done, 1)

            def probs_transpose(u):
                n = u // 4 + 1
                pe.wait_ge(probs_ready, u + 1)
                if u >= 1:
                    pe.wait_ge(pT_ready, u)
                for h in range(2):
                    for s in range(n):
                        ins = pe.transpose(ps[:, 6, (2 * h + s) * P:(2 * h + s + 1) * P],
                                           lg[:, u % 2, h, s * P:(s + 1) * P], ident[:])
                ins.then_inc(probs_T, 1)

            def values(u):
                n, hp = u // 4 + 1, u % 4
                pe.wait_ge(pT_ready, u + 1)
                if u >= 1:
                    pe.wait_ge(yB_ready, u)
                if u == 0:
                    pe.wait_ge(bank_read[1], JOB["v1"] // 2 + 1)
                for s in range(n):
                    for h in range(2):
                        head = 2 * hp + h
                        ins = pe.matmul(ps[64 * h:64 * h + 64, 7, (u % 2) * P:(u % 2) * P + P],
                                        v_tok[:, s, head * HD:(head + 1) * HD], pT[:, u % 2, h, s, :],
                                        start=(s == 0), stop=(s == n - 1), skip_group_check=True)
                ins.then_inc(pv_done, 1)

            for name in JOBS[FIRST_UNIT_JOB:JOB["wo3"]]:
                job(name)
                k = JOB[name] - FIRST_UNIT_JOB
                if k >= 2 and k % 2 == 0 and k // 2 - 1 < UNITS:
                    values(k // 2 - 1)
                if k % 2 == 1 and k // 2 < UNITS:
                    probs_transpose(k // 2)
                if k % 2 == 0 and k // 2 < UNITS:
                    logits(k // 2)

            def turn_h2(i):
                for half in range(2):
                    pe.wait_ge(h2_ready, 2 * i + half + 1)
                    for k in range(4):
                        ins = pe.transpose(ps[:, 2 * i + half, k * P:(k + 1) * P],
                                           h2[:, i, half * BANK + k * P:half * BANK + (k + 1) * P], ident[:])
                    ins.then_inc(h2_T, 1)

            def router(i):
                o = ps[:, AUX + i, 0:EXPERTS]
                pe.wait_ge(h2T_dve, i + 1)
                for k in range(KC):
                    if k == 4:
                        pe.wait_ge(h2T_act, i + 1)
                    pe.matmul(o, h2T[:, i, k, :], wr[:, k, :], start=(k == 0), stop=False)
                pe.matmul(o, ones[0:1, :], br[:], start=False, stop=True).then_inc(router_done, 1)

            turn_h2(0)
            job("wo3")
            pe.transpose(ps[:, YB, 0:P], ident[:], ident[:]).then_inc(w_used, 2)
            pe.wait_ge(small_in, 48)
            job("mod10")
            job("mod11")
            keep_clock(YB, 4)
            router(0)
            turn_h2(1)
            keep_clock(YB, 3)
            router(1)
            pe.wait_ge(bank_read[0], len(JOBS) // 2)
            pe.wait_ge(bank_read[1], len(JOBS) // 2)
            pe.wait_ge(consts, 11)
            for i in range(NT):
                for half in range(2):
                    pe.matmul(ps[:, 2 * i + half, :], zeros_b[:], ones_b[0:1, 0:1].broadcast_to([1, BANK]), start=True,
                              stop=False, skip_group_check=True)
            keep_clock(LIN, 4)
            pe.wait_ge(mask_b_ready, 2)
            pe.matmul(ps[:, GLU, 0:32], before[:], m_b[:, 0, :], start=True, stop=True)
            pe.matmul(ps[:, GLU, 32:64], ones_b[:], m_b[:, 0, :], start=True, stop=False)
            pe.matmul(ps[:, GLU, 32:64], before[:], m_b[:, 1, :], start=False, stop=True)
            pe.matmul(ps[:, GLU, 64:96], ones_b[:], m_b[:, 0, :], start=True, stop=False)
            pe.matmul(ps[:, GLU, 64:96], ones_b[:], m_b[:, 1, :], start=False, stop=True).then_inc(rank_done, 1)
            keep_clock(LIN, 4)

            def turn_gates():
                pe.wait_ge(gates_ready, 2)
                for i in range(NT):
                    ins = pe.transpose(ps[0:EXPERTS, YB, i * P:(i + 1) * P], gate[:, i, :], ident[:])
                ins.then_inc(gate_T, 1)

            def down_biases():
                pe.wait_ge(gT_ready, 1)
                pe.wait_ge(down_bias_ready, 1)
                for i in range(NT):
                    for half in range(2):
                        pe.matmul(ps[:, 2 * i + half, :], gT[:, i * P:(i + 1) * P], bd[:, half * BANK:(half + 1) * BANK],
                                  start=False, stop=False, skip_group_check=True)

            def gather(sems, v):
                pe.wait_ge(sems["onehot_ready"], v)
                for k in range(KC):
                    n = 0
                    for h in part:
                        for i in range(NT):
                            ins = pe.matmul(ps[:, AUX, k * SLOTS:(k + 1) * SLOTS], h[:, i, k * P:(k + 1) * P],
                                            onehot[:, i, :], start=(n == 0), stop=(n == 5))
                            n += 1
                ins.then_inc(sems["gathered"], 1)

            def wait_sixth(first, group, q):
                n = 6 * first + q
                s = (n + EXPERT_SLOT) % RING
                pe.wait_ge(landed[s], 16 * (FRONT_USES[s] + n // RING + 1) + 32 * group)
                return ring[:, s, :]

            main_pass = (main_sems, xg, actT, (GLU, LIN), YB)
            more_pass = (more_sems, xg_o, actT_o, (AUX, YB), AUX)

            def gate_up(passes, first, group):
                for _, _, _, banks, _ in passes:
                    for j in range(2):
                        for bank, at in zip(banks, (0, FF)):
                            pe.matmul(ps[64 * j:64 * j + 64, bank, :], pick_e[0:96, :],
                                      bias3[:, at + j * BANK:at + (j + 1) * BANK], start=True, stop=False,
                                      skip_group_check=True)
                for k in range(KC):
                    w = wait_sixth(first, group, k // 2) if k % 2 == 0 else w
                    for sems, src, _, banks, _ in passes:
                        for bank, at in zip(banks, (0, FF)):
                            for j in range(2):
                                o = (k % 2) * 2 * FF + at + j * BANK
                                ins = pe.matmul(ps[64 * j:64 * j + 64, bank, :], src[:, k * SLOTS:(k + 1) * SLOTS],
                                                w[:, o:o + BANK], start=False, stop=(k == KC - 1),
                                                skip_group_check=True)
                        if sems is more_sems and k == KC - 1:
                            ins.then_inc(more_gu_done, 1)
                        if sems is main_sems and k % 2:
                            ins.then_inc(w_used, 1)

            def turn_act(sems, banks, v):
                pe.wait_ge(sems["act_ready"], v)
                for k in range(4):
                    ins = pe.transpose(ps[:, banks[0], k * P:(k + 1) * P], act_v[:, k * P:(k + 1) * P], ident[:])
                ins.then_inc(sems["act_T"], 1)
                pe.wait_ge(sems["sg_ready"], v)
                for i in range(NT):
                    ins = pe.transpose(ps[:, banks[1], i * P:(i + 1) * P], sg[:, i].rearrange("p j s -> p (j s)"), ident[:])
                ins.then_inc(sems["sg_T"], 1)

            def down(passes, first, group):
                for half in range(2):
                    w = wait_sixth(first, group, 4 + half).rearrange("p (k m) -> p k m", m=D)
                    for sems, _, src, _, bank in passes:
                        for k in range(4):
                            if first == EXPERTS - 1 and half == 1 and k == 2:
                                pe.wait_ge(last_landed, 16)
                            for j in range(2):
                                ins = pe.matmul(ps[64 * j:64 * j + 64, bank, :],
                                                src[:, k * P + half * SLOTS:k * P + (half + 1) * SLOTS],
                                                w[:, k, j * BANK:(j + 1) * BANK], start=(half == 0 and k == 0),
                                                stop=(half == 1 and k == 3), skip_group_check=True)
                        if sems is main_sems:
                            ins.then_inc(w_used, 1)
                        elif half:
                            ins.then_inc(more_down_done, 1)

            def add_residual():
                for i in range(NT):
                    for half in range(2):
                        pe.matmul(ps[:, 2 * i + half, :], ident[:], xs[:, i, half * BANK:(half + 1) * BANK], start=False,
                                  stop=False, skip_group_check=True)

            def scatter(sems, src, rows_t, v, last=False):
                pe.wait_ge(sems["y_ready"], v)
                pe.wait_ge(sems["sgT_ready"], v)
                for i in range(NT):
                    for j in range(2):
                        ins = pe.matmul(ps[:, 2 * i + j, :], rows_t[64 * j:64 * j + 64, i * P:(i + 1) * P],
                                        src[64 * j:64 * j + 64, :], start=False, stop=last, skip_group_check=True)
                        if last:
                            ins.then_inc(acc_done, 1)

            pe.wait_ge(parts_ready, 2)
            gather(main_sems, 1)
            pe.wait_ge(routed, 1)
            pe.wait_ge(bias_moved, 1)
            more = pe.alloc_register("pe_more")
            pe.reg_mov(more, 0)

            def expert(first, group):
                e = pe.snap(first + 3 * group)
                count = pe.value_load(counts[0:1, bass.ds(e, 1)])

                def operands_ready():
                    pe.wait_ge(pick_ready, e + 1)
                    pe.wait_ge(xg_ready, e + 1)
                    if first:
                        pe.wait_ge(sgT_ready, e)

                def gather_further():
                    v = pe.snap(more) + 1
                    gather(more_sems, v)
                    pe.wait_ge(more_sems["xg_ready"], v)
                    if first:
                        pe.wait_ge(y_ready, e)
                    return v

                def gather_next():
                    if first < EXPERTS - 1:
                        gather(main_sems, e + 2)

                if first == EXPERTS - 1:
                    add_residual()
                operands_ready()
                with pe.If(count > SLOTS):
                    with pe.Fori(2, T // SLOTS) as p:
                        with pe.If(count > p * SLOTS):
                            v = gather_further()
                            gate_up([more_pass], first, group)
                            turn_act(more_sems, more_pass[3], v)
                            pe.wait_ge(more_sems["actT_ready"], v)
                            down([more_pass], first, group)
                            scatter(more_sems, y_o, sgT_o, v)
                            pe.reg_add(more, more, 1)
                    v = gather_further()
                    gate_up([more_pass, main_pass], first, group)
                    if first:
                        scatter(main_sems, y, sgT, e)
                    turn_act(more_sems, more_pass[3], v)
                    turn_act(main_sems, main_pass[3], e + 1)
                    pe.wait_ge(more_sems["actT_ready"], v)
                    pe.wait_ge(more_sems["sgT_ready"], v)
                    if not first:
                        turn_gates()
                        down_biases()
                    pe.wait_ge(actT_ready, e + 1)
                    down([more_pass, main_pass], first, group)
                    pe.wait_ge(more_sems["y_ready"], v)
                    gather_next()
                    scatter(more_sems, y_o, sgT_o, v)
                    pe.reg_add(more, more, 1)
                with pe.Else():
                    gate_up([main_pass], first, group)
                    gather_next()
                    if first:
                        scatter(main_sems, y, sgT, e)
                    else:
                        turn_gates()
                    turn_act(main_sems, main_pass[3], e + 1)
                    if not first:
                        down_biases()
                    pe.wait_ge(actT_ready, e + 1)
                    down([main_pass], first, group)

            turns(pe, expert)
            scatter(main_sems, y, sgT, EXPERTS, last=True)


_INS = ['x', 'c', 'w_ada', 'b_ada', 'norm1_g', 'w_in', 'conv_w', 'q_norm_g', 'k_norm_g', 'w_conv_out', 'w_attn_out',
        'w_o', 'norm2_g', 'w_router', 'b_router', 'w_gate_up', 'b_gate_up', 'w_down', 'b_down']


def kernel(**inputs):
    import numpy as _np
    import concourse.bacc as _bacc
    from concourse import mybir as _mybir
    from concourse.bass_utils import run_bass_kernel_spmd as _run

    nc = _bacc.Bacc("TRN2", target_bir_lowering=False, num_devices=1)
    arrays, args = {}, []
    for name in _INS:
        a = _np.ascontiguousarray(inputs[name])
        arrays[f"in_{name}"] = a
        args.append(nc.dram_tensor(f"in_{name}", a.shape, _mybir.dt.from_np(a.dtype), kind="ExternalInput").ap())
    args.append(nc.dram_tensor("out_0", (1, T, D), F32, kind="ExternalOutput").ap())
    hybrid_block(nc, *args)
    r = _run(nc, [arrays], core_ids=[0])
    return r.results[0]["out_0"]
```
